# Optimizing a Trainium2 kernel written in Bass

```python
import jax, jax.numpy as jnp
from jax import lax
import numpy as np

D_MODEL = 2048
BATCH = 1
SEQ = 256
DEPTH = 1

N_META = 16
D_MIX = D_MODEL
GLA_HEADS = 4
GLA_DK = 128
GLA_DV = 256
GLA_DK_TOT = GLA_HEADS * GLA_DK
GLA_DV_TOT = GLA_HEADS * GLA_DV
GLA_RANK = 16
GLA_TAU = 16.0
GLA_CHUNK = 64
FOX_HEADS = 8
FOX_HD = 128
FOX_W = FOX_HEADS * FOX_HD
FOX_BLOCK = 128
PAD_FRONT = FOX_BLOCK - N_META
N_GROUPS = 4
EXPERTS_PER_GROUP = 8
TOP_K = 2
D_EXPERT = 512
EPS = 1e-6
SPLIT_SIZES = (FOX_W, FOX_W, FOX_W, FOX_HEADS, GLA_DK_TOT, GLA_DK_TOT, GLA_DV_TOT, GLA_DV_TOT, GLA_RANK)
D_IN_PROJ = 3 * FOX_W + FOX_HEADS + 2 * GLA_DK_TOT + 2 * GLA_DV_TOT + GLA_RANK

kernel_name = "hymba_gla_fox_hiermoe_block"

def _rmsnorm(x, g):
    xf = x.astype(jnp.float32)
    y = xf * lax.rsqrt(jnp.mean(xf * xf, axis=-1, keepdims=True) + EPS)
    return (y * g.astype(jnp.float32)).astype(x.dtype)

def _pad_front(a):
    return jnp.pad(a, [(0, 0), (PAD_FRONT, 0)] + [(0, 0)] * (a.ndim - 2))

def _split_cols(proj):
    out = []
    start = 0
    for s in SPLIT_SIZES:
        out.append(proj[..., start:start + s])
        start += s
    return out

def gla_mixer(q, k, v, r, z, w_gate2, b_gate, norm_g):
    f32 = jnp.float32
    B, L, _ = q.shape
    T = L + PAD_FRONT
    C = GLA_CHUNK
    N = T // C
    log_a = jax.nn.log_sigmoid((z @ w_gate2).astype(f32) + b_gate.astype(f32)) / GLA_TAU

    def heads(a, d):
        return _pad_front(a.astype(f32).reshape(B, L, GLA_HEADS, d))

    def chunks(a):
        return a.reshape(B, N, C, GLA_HEADS, a.shape[-1])

    qc = chunks(heads(q, GLA_DK) * GLA_DK ** -0.5)
    kc = chunks(heads(k, GLA_DK))
    vc = chunks(heads(v, GLA_DV))
    gc = chunks(heads(log_a, GLA_DK))
    b = jnp.cumsum(gc, axis=2)
    b_ref = b[:, :, C // 2:C // 2 + 1]
    b_last = b[:, :, C - 1:]
    causal = jnp.tril(jnp.ones((C, C), dtype=bool))
    A = jnp.einsum('bnihd,bnjhd->bnhij', qc * jnp.exp(b - b_ref), kc * jnp.exp(b_ref - b))
    A = jnp.where(causal, A, 0.0)
    o_intra = jnp.einsum('bnhij,bnjhv->bnihv', A, vc)
    U = jnp.einsum('bnjhd,bnjhv->bnhdv', kc * jnp.exp(b_last - b), vc)
    decay = jnp.exp(b_last[:, :, 0])

    def step(S, inp):
        dec, u = inp
        return dec[..., None] * S + u, S

    S0 = jnp.zeros((B, GLA_HEADS, GLA_DK, GLA_DV), f32)
    _, S_prev = lax.scan(step, S0, (jnp.moveaxis(decay, 1, 0), jnp.moveaxis(U, 1, 0)))
    S_prev = jnp.moveaxis(S_prev, 0, 1)
    o_inter = jnp.einsum('bnihd,bnhdv->bnihv', qc * jnp.exp(b), S_prev)
    o = (o_intra + o_inter).reshape(B, T, GLA_HEADS, GLA_DV)[:, PAD_FRONT:]
    o = _rmsnorm(o, norm_g) * jax.nn.silu(r.astype(f32).reshape(B, L, GLA_HEADS, GLA_DV))
    return o.reshape(B, L, GLA_DV_TOT)

def fox_mixer(q, k, v, f_logit, b_f, norm_g):
    f32 = jnp.float32
    B, L, _ = q.shape
    T = L + PAD_FRONT

    def heads(a):
        return _pad_front(a.astype(f32).reshape(B, L, FOX_HEADS, FOX_HD))

    qh = heads(q) * FOX_HD ** -0.5
    kh = heads(k)
    vh = heads(v)
    log_f = _pad_front(jax.nn.log_sigmoid(f_logit.astype(f32) + b_f.astype(f32)))
    c = jnp.cumsum(log_f, axis=1).transpose(0, 2, 1)
    neg = jnp.finfo(f32).min
    outs = []
    for i in range(T // FOX_BLOCK):
        q0, q1 = i * FOX_BLOCK, (i + 1) * FOX_BLOCK
        s = jnp.einsum('bqhd,bkhd->bhqk', qh[:, q0:q1], kh[:, :q1])
        s = s + c[:, :, q0:q1, None] - c[:, :, None, :q1]
        qpos = jnp.arange(q0, q1)[:, None]
        kpos = jnp.arange(q1)[None, :]
        mask = (kpos <= qpos) & (kpos >= PAD_FRONT)
        p = jax.nn.softmax(jnp.where(mask, s, neg), axis=-1)
        outs.append(jnp.einsum('bhqk,bkhd->bqhd', p, vh[:, :q1]))
    o = jnp.concatenate(outs, axis=1)[:, PAD_FRONT:]
    o = _rmsnorm(o, norm_g)
    return o.reshape(B, L, FOX_W)

def hier_moe(u, w_rg, b_rg, w_re, b_re, w_g, w_u, w_d):
    f32 = jnp.float32
    B, L, D = u.shape
    xt = u.reshape(B * L, D)
    p_group = jax.nn.softmax((xt @ w_rg).astype(f32) + b_rg.astype(f32), axis=-1)
    g_idx = jnp.argmax(p_group, axis=-1)
    p_g = jnp.max(p_group, axis=-1)
    e_logits = jnp.einsum('nd,gde->nge', xt, w_re).astype(f32) + b_re.astype(f32)
    e_logits = jnp.take_along_axis(e_logits, g_idx[:, None, None], axis=1)[:, 0]
    p_e = jax.nn.softmax(e_logits, axis=-1)
    top_v, top_i = lax.top_k(p_e, TOP_K)
    top_v = top_v / jnp.sum(top_v, axis=-1, keepdims=True)
    w_sel = jnp.sum(jax.nn.one_hot(top_i, EXPERTS_PER_GROUP, dtype=f32) * top_v[..., None], axis=1)
    combine = (jax.nn.one_hot(g_idx, N_GROUPS, dtype=f32) * p_g[:, None])[:, :, None] * w_sel[:, None, :]
    y = jnp.zeros((B * L, D), f32)
    for g in range(N_GROUPS):
        hg = jax.nn.silu(jnp.einsum('nd,edf->nef', xt, w_g[g])) * jnp.einsum('nd,edf->nef', xt, w_u[g])
        y = y + jnp.einsum('nef,efd->nd', hg * combine[:, g, :, None].astype(hg.dtype), w_d[g])
    return y.astype(u.dtype).reshape(B, L, D)

def setup_inputs(seed: int = 0) -> dict:
    key = jax.random.key(seed)
    ks = jax.random.split(key, 20)
    nrm = jax.random.normal
    D = D_MODEL
    return {
        "x": nrm(ks[0], (BATCH, SEQ, D), jnp.float32),
        "meta_tokens": nrm(ks[1], (N_META, D), jnp.float32),
        "norm1_g": 1.0 + 0.02 * nrm(ks[2], (DEPTH, D), jnp.float32),
        "w_in": nrm(ks[3], (DEPTH, D, D_IN_PROJ), jnp.float32) * D ** -0.5,
        "b_fox_f": 3.0 + 0.1 * nrm(ks[4], (DEPTH, FOX_HEADS), jnp.float32),
        "gla_w_gate2": nrm(ks[5], (DEPTH, GLA_RANK, GLA_DK_TOT), jnp.float32) * GLA_RANK ** -0.5,
        "gla_b_gate": 0.1 * nrm(ks[6], (DEPTH, GLA_DK_TOT), jnp.float32),
        "gla_norm_g": 1.0 + 0.02 * nrm(ks[7], (DEPTH, GLA_DV), jnp.float32),
        "fox_norm_g": 1.0 + 0.02 * nrm(ks[8], (DEPTH, FOX_HD), jnp.float32),
        "w_out": nrm(ks[9], (DEPTH, D_MIX, D), jnp.float32) * D_MIX ** -0.5,
        "norm2_g": 1.0 + 0.02 * nrm(ks[10], (DEPTH, D), jnp.float32),
        "w_router_group": nrm(ks[11], (DEPTH, D, N_GROUPS), jnp.float32) * D ** -0.5,
        "b_router_group": 0.01 * nrm(ks[12], (DEPTH, N_GROUPS), jnp.float32),
        "w_router_expert": nrm(ks[13], (DEPTH, N_GROUPS, D, EXPERTS_PER_GROUP), jnp.float32) * D ** -0.5,
        "b_router_expert": 0.01 * nrm(ks[14], (DEPTH, N_GROUPS, EXPERTS_PER_GROUP), jnp.float32),
        "w_exp_gate": nrm(ks[15], (DEPTH, N_GROUPS, EXPERTS_PER_GROUP, D, D_EXPERT), jnp.float32) * D ** -0.5,
        "w_exp_up": nrm(ks[16], (DEPTH, N_GROUPS, EXPERTS_PER_GROUP, D, D_EXPERT), jnp.float32) * D ** -0.5,
        "w_exp_down": nrm(ks[17], (DEPTH, N_GROUPS, EXPERTS_PER_GROUP, D_EXPERT, D), jnp.float32) * D_EXPERT ** -0.5,
        "norm_f_g": 1.0 + 0.02 * nrm(ks[18], (D,), jnp.float32),
    }

def reference(x, meta_tokens, norm1_g, w_in, b_fox_f, gla_w_gate2, gla_b_gate, gla_norm_g, fox_norm_g,
              w_out, norm2_g, w_router_group, b_router_group, w_router_expert, b_router_expert,
              w_exp_gate, w_exp_up, w_exp_down, norm_f_g):
    B = x.shape[0]
    meta = jnp.broadcast_to(meta_tokens[None].astype(x.dtype), (B, N_META, D_MODEL))
    h = jnp.concatenate([meta, x], axis=1)
    for l in range(DEPTH):
        u = _rmsnorm(h, norm1_g[l])
        proj = u @ w_in[l]
        fq, fk, fv, ff, gq, gk, gv, gr, gz = _split_cols(proj)
        o_gla = gla_mixer(gq, gk, gv, gr, gz, gla_w_gate2[l], gla_b_gate[l], gla_norm_g[l])
        o_fox = fox_mixer(fq, fk, fv, ff, b_fox_f[l], fox_norm_g[l])
        mix = jnp.concatenate([o_gla, o_fox], axis=-1).astype(h.dtype)
        h = h + mix @ w_out[l]
        u2 = _rmsnorm(h, norm2_g[l])
        h = h + hier_moe(u2, w_router_group[l], b_router_group[l], w_router_expert[l], b_router_expert[l],
                         w_exp_gate[l], w_exp_up[l], w_exp_down[l])
    out = _rmsnorm(h, norm_f_g)[:, N_META:]
    return out


_drawn_inputs = setup_inputs


def setup_inputs(seed=0):
    import zlib

    import numpy as np

    out = dict(_drawn_inputs(seed))
    spreads = {}
    factors = {'gla_norm_g': 3.63,
     'b_router_group': 19.363,
     'b_router_expert': 8.0,
     'norm_f_g': 8.093,
     'fox_norm_g': 4.615,
     'norm2_g': 3.414}
    for name, (base, spread) in spreads.items():
        noise = np.random.default_rng([zlib.crc32(name.encode()), seed]).standard_normal(out[name].shape)
        drawn = base * np.exp(spread * noise) if base else spread * noise
        out[name] = __import__('jax').numpy.asarray(drawn.astype(out[name].dtype))
    for name, factor in factors.items():
        out[name] = (out[name] * factor).astype(out[name].dtype)
    return out
```

```python
from contextlib import ExitStack

import concourse.bass as bass
from concourse import mybir

F32 = mybir.dt.float32
F32R = mybir.dt.float32r
U32 = mybir.dt.uint32
ALU = mybir.AluOpType
ACT = mybir.ActivationFunctionType
AX = mybir.AxisListType.X

P = 128
EPS = 1e-6
GLA_TAU = 16.0
CHUNK = 64
SLOTS = 64
RAW = 6
SPLIT = 2
UNIT = 2048
BIG = 4096.0
LOWEST = -3.4028234663852886e38


def hybrid_layer(nc, x, meta_tokens, norm1_g, w_in, b_fox_f, gla_w_gate2, gla_b_gate, gla_norm_g,
                 fox_norm_g, w_out, norm2_g, w_router_group, b_router_group, w_router_expert,
                 b_router_expert, w_exp_gate, w_exp_up, w_exp_down, norm_f_g, out):
    _, SEQ, D = x.shape
    META = meta_tokens.shape[0]
    L = META + SEQ
    KD = D // P
    TT = SEQ // P
    GH = gla_w_gate2.shape[2] // P
    DV = gla_norm_g.shape[1]
    VH = DV // P
    FH = b_fox_f.shape[1]
    HD = fox_norm_g.shape[1]
    G, E8 = w_router_expert.shape[1], w_router_expert.shape[3]
    E = G * E8
    FE = w_exp_gate.shape[4]
    RANK = gla_w_gate2.shape[1]
    NCH = SEQ // CHUNK
    QSCALE = float(P) ** -0.5

    FOX_COLS = 3 * FH * HD
    GLA_COL0 = FOX_COLS + FH
    GLA_BLOCKS = GH + GH + GH * VH + GH * VH
    Z_COL = GLA_COL0 + GLA_BLOCKS * P
    NB = GLA_BLOCKS + FOX_COLS // P
    GQ, GK, GV, GR = 0, GH, 2 * GH, 2 * GH + GH * VH
    FQ = GLA_BLOCKS
    FK, FV = FQ + FH, FQ + 2 * FH
    Z_AT = 32

    U_IN = 1
    U_OUT = U_IN + NB
    NOUT = (D // 512) * (D // 512)
    U_EXP = U_OUT + NOUT
    PER = 12
    assert GLA_BLOCKS % RAW == 0 and NB % RAW == 0 and PER % RAW == 0 and PER % SPLIT == 0
    assert KD * P == UNIT and FE == 512 and D == 2048 and RAW % SPLIT == 0

    win = w_in[0].rearrange("(p k) n -> p k n", k=KD)
    wout = w_out[0]
    wg = w_exp_gate[0].rearrange("g e d f -> (g e) d f")
    wu = w_exp_up[0].rearrange("g e d f -> (g e) d f")
    wd = w_exp_down[0].rearrange("g e f d -> (g e) f d")

    with ExitStack() as ctx:
        def sem(name):
            return ctx.enter_context(nc.semaphore(name))

        class Area:

            def __init__(self, at):
                self.at = at

            def __call__(self, name, shape, dt=F32):
                size = 4
                for n in shape[1:]:
                    size *= n
                t = nc.alloc_sbuf_tensor_at(name, shape, dt, offset=self.at)
                self.at += (size + 31) // 32 * 32
                assert self.at <= SBUF_END, name
                return t

        SBUF_END = nc.sbuf_top
        keep = Area((nc.sbuf_base + 31) // 32 * 32)
        raw = [keep(f"raw{i}", [P, UNIT]) for i in range(RAW)]
        hi = [keep(f"hi{i}", [P, UNIT], F32R) for i in range(SPLIT)]
        lo = [keep(f"lo{i}", [P, UNIT], F32R) for i in range(SPLIT)]
        resid = keep("resid", [P, TT, D])
        ident = keep("ident", [P, P])
        above = keep("above", [P, P])
        chunkm = keep("chunkm", [P, P])
        ones = keep("ones", [P, L])
        count = keep("count", [P, CHUNK + 1])
        rowno = keep("rowno", [P, 1])
        g1 = keep("g1", [P, KD])
        wr = keep("wr", [P, KD, G + E])
        br = keep("br", [P, G + E])
        gbias = keep("gbias", [P, GH])
        ggain = keep("ggain", [P, VH])
        fgain = keep("fgain", [P, 1])
        wgate2 = keep("wgate2", [RANK, GH * P])
        fbias = keep("fbias", [FH, 1])
        stat = keep("stat", [P, 8])
        stat2 = keep("stat2", [P, 8])

        proj_area = Area(keep.at)
        proj = proj_area("proj", [P, NB, L])
        temp = Area(proj_area.at)
        gt = [temp(f"gt{i}", [P, GH, L]) for i in range(4)]
        dec = temp("dec", [P, GH, NCH])
        ss = temp("ss", [P, 2 * (GH + FH)])
        rms = temp("rms", [P, 2 * (GH + FH)])
        rs = temp("rs", [P, FH, 8])
        mtmp_area = Area(proj_area.at)
        mtmp = [mtmp_area(f"mtmp{i}", [P, SEQ]) for i in range(2)]
        xn_area = Area(keep.at)
        xn = xn_area("xn", [P, TT, D])
        mn = xn_area("mn", [META, D])
        xjunk = xn_area("xjunk", [P, D])
        u_area = Area(temp.at)
        uh = u_area("uh", [P, KD, L], F32R)
        ul = u_area("ul", [P, KD, L], F32R)
        head = Area(temp.at)
        sel = head("sel", [FH, FH, P])
        ct = head("ct", [FH, 4, L])
        cq = head("cq", [P, TT, FH])
        a2 = [head(f"a2_{i}", [P, TT, P]) for i in range(2)]
        kln = head("kln", [P, 1 + TT, P])
        vn = head("vn", [P, 1 + TT, DV])
        st = head("st", [P, NCH, DV])
        qs = [head(f"qs{i}", [P, SEQ]) for i in range(2)]
        pr = head("pr", [P, TT, L])
        pt = head("pt", [P, 3, P])
        ptm = head("ptm", [META, TT, P])
        vf = [head(f"vf{i}", [P, 1 + TT, HD]) for i in range(2)]
        junk = head("junk", [P, DV])
        zt = head("zt", [RANK, L])
        lowest = head("lowest", [P, P])
        reset = head("reset", [P, L])
        mix_area = Area(temp.at)
        mixh = mix_area("mixh", [P, KD, SEQ], F32R)
        mixl = mix_area("mixl", [P, KD, SEQ], F32R)

        ex = Area(keep.at)
        g2b = ex("g2b", [P, D])
        u2 = ex("u2", [P, TT, D])
        key = ex("key", [P, TT, E + 1])
        rowid = ex("rowid", [P, TT, E + 1])
        pick = ex("pick", [P, TT, SLOTS], F32R)
        idn = ex("idn", [SLOTS, 1], U32)
        idx = ex("idx", [SLOTS, 1], U32)
        nil = ex("nil", [SLOTS, 1], U32)
        empty = ex("empty", [P, 1])
        cw = ex("cw", [P, TT, 2])
        rounds = ex("rounds", [P, 4])
        limit = ex("limit", [P, 4])
        nrounds = ex("nrounds", [P, 1], U32)
        rt = {}
        for name, n in (("lg", G + E), ("gp", 8), ("gm", 8), ("gi", 8), ("ge", 8), ("oh", G), ("sel8", 8),
                        ("pe", 8), ("top", 8), ("ti", 8), ("eid", 2), ("m0", E), ("m1", E), ("mm", E), ("t32", E)):
            rt[name] = ex("rt_" + name, [P, TT, n])
        gix = ex("gix", [P, TT, 8], U32)
        tix = ex("tix", [P, TT, 8], U32)
        esum = ex("esum", [P, 32])
        u2_area = Area(ex.at)
        u2h = u2_area("u2h", [P, TT, D], F32R)
        u2l = u2_area("u2l", [P, TT, D], F32R)
        ex2 = Area(u2_area.at)
        yrow = ex2("yrow", [SLOTS, D])
        ylo = ex2("ylo", [SLOTS, D])
        xs = ex2("xs", [P, KD, 2 * SLOTS], F32R)
        hs = ex2("hs", [P, FE // P, 2 * SLOTS], F32R)
        glo = ex2("glo", [SLOTS, FE])
        gsum = ex2("gsum", [SLOTS, FE])
        ulo = ex2("ulo", [SLOTS, FE])
        usum = ex2("usum", [SLOTS, FE])
        u2t = Area(u2_area.at)("u2t", [P, KD, SEQ])
        fin = Area(ex.at)
        yk = fin("yk", [P, TT, 2, D])
        gfb = Area(keep.at)("gfb", [P, D])

        scratch = nc.dram_tensor("expert_rows", [2 * SEQ, D], F32)
        bank = [ctx.enter_context(nc.psum_tensor(f"bank{i}", [P, 512], F32)) for i in range(8)]
        masks_ready = sem("masks_ready")
        heads_consts = sem("heads_consts")
        params_in = sem("params_in")
        routers_in = sem("routers_in")
        x_in = sem("x_in")
        raw_zero = sem("raw_zero")
        narrow_in = sem("narrow_in")
        raw_in = [sem(f"raw_in{i}") for i in range(RAW)]
        hi_ready = sem("hi_ready")
        lo_ready = sem("lo_ready")
        units_used = sem("units_used")
        proj_out = sem("proj_out")
        act_step = sem("act_step")
        dve_step = sem("dve_step")
        sums_ready = sem("sums_ready")
        root_in = sem("root_in")
        root_out = sem("root_out")
        xn_ready = sem("xn_ready")
        xt_ready = sem("xt_ready")
        uh_ready = sem("uh_ready")
        ul_ready = sem("ul_ready")
        z_ready = sem("z_ready")
        gates_mm = sem("gates_mm")
        gate_d = sem("gate_d")
        gate_a = sem("gate_a")
        fgate_d = sem("fgate_d")
        fgate_a = sem("fgate_a")
        fgate_t = sem("fgate_t")
        cq_ready = sem("cq_ready")
        gla_ops = sem("gla_ops")
        scores_g = sem("scores_g")
        kv_t = sem("kv_t")
        a_ready = sem("a_ready")
        k_ready = sem("k_ready")
        v_ready = sem("v_ready")
        upd_g = sem("upd_g")
        st_ready = sem("st_ready")
        o_g = sem("o_g")
        o_gout = sem("o_gout")
        q_ready = sem("q_ready")
        scores_f = sem("scores_f")
        bias_f = sem("bias_f")
        p_ready = sem("p_ready")
        vf_t = sem("vf_t")
        vf_ready = sem("vf_ready")
        p_t = sem("p_t")
        pt_a = sem("pt_a")
        pt_d = sem("pt_d")
        o_f = sem("o_f")
        o_fout = sem("o_fout")
        sq_f = sem("sq_f")
        silu_ready = sem("silu_ready")
        on_d = sem("on_d")
        mix_t = sem("mix_t")
        mix_f = sem("mix_f")
        mixh_ready = sem("mixh_ready")
        mixl_ready = sem("mixl_ready")
        resid_ready = sem("resid_ready")
        u2_ready = sem("u2_ready")
        u2h_ready = sem("u2h_ready")
        u2l_ready = sem("u2l_ready")
        u2_t = sem("u2_t")
        u2t_a = sem("u2t_a")
        logits = sem("logits")
        route_d = sem("route_d")
        route_a = sem("route_a")
        ranks = sem("ranks")
        routed = sem("routed")
        pick_ready = sem("pick_ready")
        xs_mm = sem("xs_mm")
        xs_ready = sem("xs_ready")
        glo_ready = sem("glo_ready")
        gsum_ready = sem("gsum_ready")
        silu_e = sem("silu_e")
        ulo_ready = sem("ulo_ready")
        usum_ready = sem("usum_ready")
        h_ready = sem("h_ready")
        h_t = sem("h_t")
        hsh_ready = sem("hsh_ready")
        hsl_ready = sem("hsl_ready")
        idn_ready = sem("idn_ready")
        idx_ready = sem("idx_ready")
        ylo_ready = sem("ylo_ready")
        y_ready = sem("y_ready")
        scattered = sem("scattered")
        scatters = sem("scatters")
        yk_in = sem("yk_in")
        out_ready = sem("out_ready")
        stat_zero = sem("stat_zero")
        summed = sem("summed")
        idn_mm = sem("idn_mm")
        stand_in = sem("stand_in")
        key_moved = sem("key_moved")
        stored = sem("stored")

        def slot(c):
            return c % RAW

        def turn(c, m):
            return m + c // RAW

        def nth(c, m):
            return RAW * m + c

        def hi_unit(act, c, m=0):
            act.wait_ge(raw_in[slot(c)], 16 * (turn(c, m) + 1))
            if c == 0:
                act.wait_ge(narrow_in, 16)
            if c >= SPLIT:
                act.wait_ge(units_used, nth(c - SPLIT + 1, m))
            act.copy(hi[c % SPLIT][:, :], raw[slot(c)][:, :]).then_inc(hi_ready, 1)

        def lo_unit(dve, c, m=0):
            dve.wait_ge(hi_ready, nth(c + 1, m))
            if c >= SPLIT:
                dve.wait_ge(units_used, nth(c - SPLIT + 1, m))
            dve.tensor_tensor(lo[c % SPLIT][:, :], raw[slot(c)][:, :], hi[c % SPLIT][:, :].bitcast(F32),
                              ALU.subtract).then_inc(lo_ready, 1)

        def load_unit(sp, source, c, m=0):
            if c >= RAW:
                sp.wait_ge(lo_ready, nth(c - RAW + 1, m))
            n = source.shape[-1]
            sp.dma_start(raw[slot(c)][:, :].rearrange("p (k n) -> p k n", n=n),
                         source).then_inc(raw_in[slot(c)], 16)

        STRAIGHT = U_IN + RAW
        LOOPS = (NB - RAW) // RAW

        def part(w, k, n):
            return w[:, k * n:(k + 1) * n]

        def chunked(t):
            return t.rearrange("p h (c i) -> p h c i", i=CHUNK)

        upd = [bank[5][:, 0:DV], bank[4][:, 0:DV], bank[7][:, 0:DV], bank[4][:, DV:2 * DV]]

        block = ctx.enter_context(nc.Block())

        @block.sync
        def _(sp):
            sp.dma_start(resid[:, :, :], x[0].rearrange("(t p) d -> p t d", p=P)).then_inc(x_in, 16)
            sp.dma_start(mn[:, :], meta_tokens).then_inc(x_in, 16)
            sp.dma_start(g1[:, :], norm1_g[0].rearrange("(p k) -> p k", k=KD)).then_inc(x_in, 16)
            sp.wait_ge(raw_zero, 1)
            narrow = raw[0][:, :].rearrange("p (k n) -> p k n", n=P)
            sp.dma_start(narrow[:, :, 0:FH], win[:, :, FOX_COLS:FOX_COLS + FH]).then_inc(raw_in[0], 16)
            sp.dma_start(narrow[:, :, Z_AT:Z_AT + RANK],
                         win[:, :, Z_COL:Z_COL + RANK]).then_inc(narrow_in, 16)
            for c in range(U_IN, STRAIGHT):
                load_unit(sp, win[:, :, GLA_COL0 + (c - U_IN) * P:GLA_COL0 + (c - U_IN + 1) * P], c)
            with sp.Fori(0, (GLA_BLOCKS - RAW) // RAW) as i:
                for j in range(RAW):
                    c = STRAIGHT + j
                    col = GLA_COL0 + (c - U_IN) * P + RAW * P * i
                    load_unit(sp, win[:, :, bass.ds(col, P)], c, i)
            with sp.Fori(0, (NB - GLA_BLOCKS) // RAW) as i:
                for j in range(RAW):
                    c = U_IN + GLA_BLOCKS + j
                    load_unit(sp, win[:, :, bass.ds(j * P + RAW * P * i, P)], c, i)
            for n in range(D // 512):
                for q in range(D // 512):
                    load_unit(sp, wout[q * 512:(q + 1) * 512, n * 512:(n + 1) * 512]
                              .rearrange("(k p) n -> p k n", p=P), U_OUT + n * (D // 512) + q)

            def expert(e, m):
                for w, first in ((wg, 0), (wu, 4)):
                    for q in range(4):
                        load_unit(sp, w[e, q * 512:(q + 1) * 512, :].rearrange("(k p) n -> p k n", p=P),
                                  U_EXP + first + q, m)
                for q in range(4):
                    load_unit(sp, wd[e, q * P:(q + 1) * P, :].rearrange("(k p) n -> p k n", p=P),
                              U_EXP + 8 + q, m)

            with sp.Fori(0, E) as e:
                expert(e, 2 * e)
            sp.wait_ge(routed, 1)
            n_rounds = sp.value_load(nrounds[0:1, 0:1], min_val=1, max_val=SEQ // SLOTS)
            with sp.If(n_rounds > 1):
                with sp.Fori(1, n_rounds) as r:
                    with sp.Fori(0, E) as e:
                        expert(e, 2 * E * r + 2 * e)
            sp.wait_ge(scattered, 16 * E * n_rounds + 16)
            rows = scratch[:, :].rearrange("(k t p) d -> p t k d", k=2, p=P)
            for t in range(TT):
                for k in range(2):
                    sp.dma_start(yk[:, t, k, :], rows[:, t, k, :]).then_inc(yk_in, 16)
            out_rows = out[0].rearrange("(t p) d -> p t d", p=P)
            for t in range(TT):
                sp.wait_ge(out_ready, t + 1)
                sp.dma_start(out_rows[:, t, :], u2[:, t, :]).then_inc(stored, 16)
            sp.wait_ge(stored, 16 * TT)

        @block.gpsimd
        def _(pool):
            pool.memset(ones[:, :], 1.0).then_inc(masks_ready, 1)
            pool.wait_ge(masks_ready, 1)
            pool.affine_select(out=ident[:, :], in_=ones[:, 0:P], pattern=[[1, P]], compare_op=ALU.is_equal,
                               fill=0.0, base=0, channel_multiplier=-1).then_inc(masks_ready, 1)
            pool.affine_select(out=above[:, :], in_=ones[:, 0:P], pattern=[[1, P]], compare_op=ALU.is_gt,
                               fill=0.0, base=0, channel_multiplier=-1).then_inc(masks_ready, 1)
            pool.affine_select(out=chunkm[:, :], in_=ones[:, 0:P], pattern=[[1, P]], compare_op=ALU.is_ge,
                               fill=0.0, base=0, channel_multiplier=-1).then_inc(masks_ready, 1)
            pool.wait_ge(masks_ready, 4)
            pool.memset(chunkm[0:CHUNK, CHUNK:P], 0.0).then_inc(masks_ready, 1)
            pool.iota(count[:, :], [[1, CHUNK + 1]], base=0, channel_multiplier=0,
                      allow_small_or_imprecise_dtypes=True).then_inc(masks_ready, 1)
            pool.iota(rowno[:, :], [[0, 1]], base=0, channel_multiplier=1,
                      allow_small_or_imprecise_dtypes=True).then_inc(masks_ready, 1)
            for dst, src in ((gbias[:, :], gla_b_gate[0].rearrange("(h p) -> p h", p=P)),
                             (ggain[:, :], gla_norm_g[0].rearrange("(h p) -> p h", p=P)),
                             (fgain[:, :], fox_norm_g[0].rearrange("(p a) -> p a", a=1)),
                             (wgate2[:, :], gla_w_gate2[0]),
                             (fbias[:, :], b_fox_f[0].rearrange("(p a) -> p a", a=1))):
                pool.dma_start(dst, src, allow_slow_non_contiguous=True).then_inc(params_in, 16)
            pool.dma_start(wr[:, :, 0:G], w_router_group[0].rearrange("(p k) n -> p k n", k=KD)).then_inc(routers_in, 16)
            for g in range(G):
                pool.dma_start(wr[:, :, G + g * E8:G + (g + 1) * E8],
                               w_router_expert[0, g].rearrange("(p k) n -> p k n", k=KD)).then_inc(routers_in, 16)
            pool.dma_start(br[:, 0:G], b_router_group[0:1, :].broadcast_to([P, G])).then_inc(routers_in, 16)
            pool.dma_start(br[:, G:G + E], b_router_expert[0].rearrange("(a g) e -> a (g e)", a=1)
                           .broadcast_to([P, E])).then_inc(routers_in, 16)
            pool.wait_ge(units_used, U_OUT)
            pool.memset(sel[:, :, :], 1.0).then_inc(heads_consts, 1)
            pool.memset(reset[:, :], 1.0).then_inc(heads_consts, 1)
            pool.memset(a2[0][:, :, :], 0.0).then_inc(heads_consts, 1)
            pool.memset(a2[1][:, :, :], 0.0).then_inc(heads_consts, 1)
            pool.wait_ge(heads_consts, 4)
            pool.affine_select(out=sel[:, :, :], in_=sel[:, :, :], pattern=[[1, FH], [0, P]],
                               compare_op=ALU.is_equal, fill=0.0, base=0,
                               channel_multiplier=-1).then_inc(heads_consts, 1)
            pool.memset(reset[:, 0:1], 0.0).then_inc(heads_consts, 1)
            for n in range(NCH):
                pool.memset(reset[:, META + n * CHUNK:META + n * CHUNK + 1], 0.0).then_inc(heads_consts, 1)
            pool.wait_ge(mixl_ready, KD)
            pool.dma_start(g2b[:, :], norm2_g[0:1, :].broadcast_to([P, D])).then_inc(routers_in, 16)
            pool.memset(rt["gp"][:, :, :], LOWEST).then_inc(masks_ready, 1)
            pool.memset(key[:, :, E:E + 1], 0.0).then_inc(masks_ready, 1)
            pool.memset(rowid[:, :, E:E + 1], 0.0).then_inc(masks_ready, 1)
            pool.memset(nil[:, :], 0).then_inc(masks_ready, 1)
            for i in range(4):
                pool.memset(limit[:, i:i + 1], float(SLOTS * i)).then_inc(masks_ready, 1)
            pool.wait_ge(u2_ready, TT)
            pool.dma_start(gfb[:, :], norm_f_g.rearrange("(a d) -> a d", a=1).broadcast_to([P, D])).then_inc(routers_in, 16)
            pool.wait_ge(routed, 1)
            pool.tensor_copy(idx[:, :], empty[0:SLOTS, :]).then_inc(idx_ready, 1)
            n_rounds = pool.value_load(nrounds[0:1, 0:1], min_val=1, max_val=SEQ // SLOTS)

            def scatter():
                pool.indirect_dma_start(scratch[:, :], bass.IndirectOffsetOnAxis(ap=idx[:, 0:1], axis=0),
                                        yrow[:, :], None, bounds_check=2 * SEQ - 1,
                                        oob_is_err=False).then_inc(scattered, 16)

            with pool.Fori(0, n_rounds) as r:
                with pool.Fori(0, E) as e:
                    n = E * r + e
                    pool.wait_ge(y_ready, 4 * n + 4)
                    pool.wait_ge(idx_ready, n + 1)
                    pool.sem_inc(scatters, 1)
                    scatter()
                    pool.wait_ge(scattered, 16 * n + 16)
                    pool.wait_ge(idn_ready, n + 1)
                    pool.tensor_tensor(idx[:, :], idn[:, :], nil[:, :], ALU.add).then_inc(idx_ready, 1)
            pool.wait_ge(y_ready, 4 * E * n_rounds + 4)
            pool.wait_ge(idx_ready, E * n_rounds + 1)
            pool.sem_inc(scatters, 1)
            scatter()

        @block.scalar
        def _(act):
            steps = [0]

            def own(ins):
                steps[0] += 1
                ins.then_inc(act_step, 1)
                act.wait_ge(act_step, steps[0])

            def root(n, src, dst):
                act.wait_ge(root_in, n)
                act.activation(dst, src, ACT.Sqrt).then_inc(root_out, 1)

            act.wait_ge(x_in, 48)
            act.wait_ge(stat_zero, 1)
            for t in range(TT):
                own(act.activation(xjunk[:, :], resid[:, t, :], ACT.Square, accum_out=stat[:, t:t + 1]))
            act.activation(xjunk[0:META, :], mn[:, :], ACT.Square, accum_out=stat[0:META, TT:TT + 1]).then_inc(sums_ready, 1)
            root(1, stat2[:, 0:TT + 1], stat[:, 0:TT + 1])
            hi_unit(act, 0)
            for k in range(KD):
                act.wait_ge(xt_ready, k + 1)
                act.activation(uh[:, k, :], bank[k % 4][:, 0:L], ACT.Copy,
                               scale=g1[:, k:k + 1]).then_inc(uh_ready, 1)
            hi_unit(act, 1)

            def proj_copy(c, m=0):
                act.wait_ge(units_used, nth(c + 1, m))
                act.copy(proj[:, c - U_IN + RAW * m, :] if isinstance(m, int) else
                         proj[:, bass.ds(c - U_IN + RAW * m, 1), :].rearrange("p a l -> p (a l)"),
                         bank[c % 2][:, 0:L]).then_inc(proj_out, 1)

            for c in range(2, STRAIGHT):
                if c - 2 >= U_IN:
                    proj_copy(c - 2)
                hi_unit(act, c)
            with act.Fori(0, LOOPS) as i:
                for j in range(RAW):
                    proj_copy(STRAIGHT + j - 2, i)
                    hi_unit(act, STRAIGHT + j, i)
            for c in (U_OUT, U_OUT + 1):
                proj_copy(c - 2)
                hi_unit(act, c)

            act.wait_ge(fgate_d, 1)
            own(act.activation(ct[:, 1, :], ct[:, 1, :], ACT.Exp, scale=-1.0))
            act.activation(ct[:, 1, :], ct[:, 1, :], ACT.Ln, bias=1.0).then_inc(fgate_a, 1)
            act.wait_ge(gate_d, 1)
            own(act.activation(gt[1][:, :, :], gt[1][:, :, :], ACT.Exp, scale=-1.0))
            act.activation(gt[1][:, :, :], gt[1][:, :, :], ACT.Ln, bias=1.0).then_inc(gate_a, 1)
            act.wait_ge(gate_d, 2)
            act.activation(gt[3][:, :, :], gt[2][:, :, :], ACT.Exp, scale=1.0 / GLA_TAU).then_inc(gate_a, 1)
            act.activation(dec[:, :, :], gt[2][:, :, META + CHUNK - 1::CHUNK], ACT.Exp,
                           scale=1.0 / GLA_TAU).then_inc(gate_a, 1)
            act.wait_ge(gate_d, 3)
            act.activation(gt[0][:, :, :], gt[0][:, :, :], ACT.Exp, scale=1.0 / GLA_TAU).then_inc(gate_a, 1)
            act.wait_ge(gate_d, 4)
            act.activation(gt[2][:, :, META:L], gt[0][:, :, META:L], ACT.Exp, scale=1.0 / GLA_TAU).then_inc(gate_a, 1)
            act.wait_ge(gate_a, 5)
            act.activation(gt[0][:, :, META:L], gt[0][:, :, META:L], ACT.Exp, scale=-1.0 / GLA_TAU).then_inc(gate_a, 1)

            def gla_v(h):
                act.wait_ge(kv_t, h + 1)
                if h:
                    act.wait_ge(o_g, h)
                own(act.copy(vn[0:META, 0, :], bank[2][0:META, 0:DV]))
                own(act.copy(vn[:, 1, :], bank[2][:, DV:2 * DV]))
                act.copy(vn[:, 2, :], bank[3][:, 0:DV]).then_inc(v_ready, 1)

            def gla_out(h):
                act.wait_ge(o_g, h + 1)
                o = proj[:, GV + VH * h:GV + VH * (h + 1), :].rearrange("p a l -> p (a l)")
                own(act.copy(o[:, 0:TT * DV], bank[6][:, :]))
                for t in range(TT):
                    ins = act.activation(junk[:, :], bank[6][:, t * DV:(t + 1) * DV], ACT.Square,
                                         accum_out=ss[:, TT * h + t:TT * h + t + 1])
                    if t < TT - 1:
                        own(ins)
                ins.then_inc(o_gout, 1)
                act.wait_ge(o_gout, h + 1)

            for h in range(GH + 1):
                if h < GH:
                    gla_v(h)
                if h:
                    gla_out(h - 1)

            def fox_exp(h):
                act.wait_ge(bias_f, h + 1)
                if h:
                    act.wait_ge(p_t, h)
                for t in range(TT):
                    w = META + (t + 1) * P
                    ins = act.activation(pr[:, t, 0:w], bank[2 + t][:, 0:w], ACT.Exp, bias=rs[:, h, 4 + t:5 + t],
                                         accum_out=rs[:, h, 6 + t:7 + t])
                ins.then_inc(p_ready, 1)

            def fox_v(h):
                act.wait_ge(vf_t, h + 1)
                if h >= 2:
                    act.wait_ge(o_f, h - 1)
                own(act.copy(vf[h % 2][0:META, 0, :], bank[6][0:META, 0:HD]))
                act.copy(vf[h % 2][:, 1:3, :].rearrange("p a b -> p (a b)"), bank[6][:, HD:3 * HD]).then_inc(vf_ready, 1)

            def fox_pt(h):
                act.wait_ge(p_t, h + 1)
                if h:
                    act.wait_ge(o_f, h)
                act.copy(pt[:, :, :].rearrange("p a b -> p (a b)"), bank[4][:, 0:3 * P]).then_inc(pt_a, 1)

            def fox_sq(h):
                act.wait_ge(o_fout, h + 1)
                for t in range(TT):
                    i = TT * (GH + h) + t
                    ins = act.activation(junk[:, 0:HD], proj[:, FQ + h, t * P:(t + 1) * P], ACT.Square,
                                         accum_out=ss[:, i:i + 1])
                    if t < TT - 1:
                        own(ins)
                ins.then_inc(sq_f, 1)
                act.wait_ge(sq_f, h + 1)

            for s in range(FH + 2):
                if s < FH:
                    fox_exp(s)
                    fox_v(s)
                if 1 <= s <= FH:
                    fox_pt(s - 1)
                if s >= 2:
                    fox_sq(s - 2)

            r_all = proj[:, GR:GR + GH * VH, META:L]
            act.activation(r_all, r_all, ACT.Silu).then_inc(silu_ready, 1)
            root(2, ss[:, :], rms[:, :])
            for k in range(KD):
                if k < GH * VH:
                    act.wait_ge(mix_f, k + 1)
                    act.copy(mixh[:, k, :], mtmp[k % 2][:, :]).then_inc(mixh_ready, 1)
                else:
                    act.wait_ge(mix_t, k + 1)
                    act.activation(mixh[:, k, :], bank[k % 4][:, 0:SEQ], ACT.Copy,
                                   scale=fgain[:, 0:1]).then_inc(mixh_ready, 1)

            for c in range(U_OUT + 2, U_EXP):
                hi_unit(act, c)

            act.wait_ge(resid_ready, D // 512)
            for t in range(TT):
                ins = act.activation(u2[:, t, :], resid[:, t, :], ACT.Square, accum_out=stat[:, t:t + 1])
                if t < TT - 1:
                    own(ins)
            ins.then_inc(sums_ready, 1)
            root(3, stat2[:, 0:TT], stat[:, 0:TT])
            for t in range(TT):
                act.wait_ge(u2_ready, t + 1)
                act.copy(u2h[:, t, :], u2[:, t, :]).then_inc(u2h_ready, 1)
            for i in range(KD // 2):
                act.wait_ge(u2_t, i + 1)
                act.copy(u2t[:, 2 * i:2 * i + 2, :].rearrange("p k l -> p (k l)"), bank[i % 4][:, :]).then_inc(u2t_a, 1)
            act.wait_ge(route_d, 1)
            for t in range(TT):
                ins = act.activation(rt["ge"][:, t, :], rt["gp"][:, t, :], ACT.Exp, bias=esum[:, t:t + 1],
                                     accum_out=esum[:, 2 + t:3 + t])
            ins.then_inc(route_a, 1)
            act.wait_ge(route_d, 2)
            for t in range(TT):
                ins = act.activation(rt["pe"][:, t, :], rt["sel8"][:, t, :], ACT.Exp, bias=esum[:, 4 + t:5 + t],
                                     accum_out=esum[:, 6 + t:7 + t])
            ins.then_inc(route_a, 1)

            def gathered(q, before):
                act.wait_ge(xs_mm, before + q + 1)
                act.copy(xs[:, 4 * q:4 * q + 4, :].rearrange("p k s -> p (k s)"),
                         bank[6 + q % 2][:, :]).then_inc(xs_ready, 1)

            def result_lo(n):
                act.wait_ge(units_used, nth(U_EXP, 2 * n))
                for q in range(4):
                    act.copy(ylo[:, 512 * q:512 * (q + 1)], bank[2 + q][SLOTS:P, :]).then_inc(ylo_ready, 1)

            act.wait_ge(routed, 1)
            act.wait_ge(stand_in, 1)
            n_rounds = act.value_load(nrounds[0:1, 0:1], min_val=1, max_val=SEQ // SLOTS)
            with act.Fori(0, n_rounds) as r:
                for q in range(4):
                    gathered(q, 4 * (E + 1) * r)
                with act.Fori(0, E) as e:
                    n = E * r + e
                    for j in range(PER):
                        if j == 9:
                            act.wait_ge(units_used, nth(U_EXP + 8, 2 * n))
                            act.copy(ulo[:, :], bank[1][SLOTS:P, :]).then_inc(ulo_ready, 1)
                        if j == 11:
                            gathered(2, 4 * (n + r + 1))
                            gathered(3, 4 * (n + r + 1))
                        hi_unit(act, U_EXP + j, 2 * n)
                        if j == 1:
                            result_lo(n)
                        if j == 5:
                            act.wait_ge(units_used, nth(U_EXP + 4, 2 * n))
                            act.copy(glo[:, :], bank[0][SLOTS:P, :]).then_inc(glo_ready, 1)
                        if j == 7:
                            act.wait_ge(gsum_ready, n + 1)
                            act.activation(glo[:, :], gsum[:, :], ACT.Silu).then_inc(silu_e, 1)
                        if j == 9:
                            act.wait_ge(h_t, n + 1)
                            act.copy(hs[:, :, 0:SLOTS], bank[0][:, 0:FE // P * SLOTS]
                                     .rearrange("p (k s) -> p k s", s=SLOTS)).then_inc(hsh_ready, 1)
                            gathered(0, 4 * (n + r + 1))
                            gathered(1, 4 * (n + r + 1))
            result_lo(E * n_rounds)
            for t in range(TT):
                act.wait_ge(summed, t + 1)
                act.activation(u2[:, t, :], resid[:, t, :], ACT.Square, accum_out=stat[:, t:t + 1]).then_inc(sums_ready, 1)
                root(4 + t, stat2[:, t:t + 1], stat[:, 2 + t:3 + t])

        @block.vector
        def _(dve):
            steps = [0]

            def own(ins):
                steps[0] += 1
                ins.then_inc(dve_step, 1)
                dve.wait_ge(dve_step, steps[0])

            def mean_eps(dst, src, n):
                dve.tensor_scalar(dst, src, 1.0 / n, EPS, ALU.mult, ALU.add).then_inc(root_in, 1)

            dve.memset(stat[:, :], 0.0).then_inc(stat_zero, 1)
            dve.memset(raw[0][:, :], 0.0).then_inc(raw_zero, 1)
            dve.wait_ge(sums_ready, 1)
            mean_eps(stat2[:, 0:TT + 1], stat[:, 0:TT + 1], D)
            dve.wait_ge(root_out, 1)
            own(dve.reciprocal(stat2[:, 0:TT + 1], stat[:, 0:TT + 1]))
            for t in range(TT):
                dve.tensor_scalar(xn[:, t, :], resid[:, t, :], stat2[:, t:t + 1], None, ALU.mult).then_inc(xn_ready, 1)
            dve.tensor_scalar(mn[:, :], mn[:, :], stat2[0:META, TT:TT + 1], None, ALU.mult).then_inc(xn_ready, 1)
            lo_unit(dve, 0)
            for k in range(KD):
                dve.wait_ge(uh_ready, k + 1)
                dve.scalar_tensor_tensor(out=ul[:, k, :], in0=bank[k % 4][:, 0:L], scalar=g1[:, k:k + 1],
                                         in1=uh[:, k, :].bitcast(F32), op0=ALU.mult,
                                         op1=ALU.subtract).then_inc(ul_ready, 1)
            for c in range(1, STRAIGHT):
                lo_unit(dve, c)
            with dve.Fori(0, LOOPS) as i:
                for j in range(RAW):
                    lo_unit(dve, STRAIGHT + j, i)
            for c in (U_OUT, U_OUT + 1):
                lo_unit(dve, c)

            dve.wait_ge(params_in, 16 * 5)
            dve.wait_ge(units_used, U_OUT)
            dve.wait_ge(proj_out, NB)
            dve.tensor_copy(zt[:, :], bank[7][Z_AT:Z_AT + RANK, 0:L]).then_inc(z_ready, 1)
            own(dve.tensor_scalar(ct[:, 0, :], bank[7][0:FH, 0:L], fbias[:, 0:1], None, ALU.add))
            own(dve.scalar_tensor_tensor(out=ct[:, 1, :], in0=ct[:, 0, :], scalar=-1.0, in1=ct[:, 0, :],
                                         op0=ALU.mult, op1=ALU.max))
            dve.tensor_scalar(ct[:, 0, :], ct[:, 0, :], 0.0, None, ALU.min).then_inc(fgate_d, 1)
            dve.wait_ge(gates_mm, 1)
            for h in range(GH):
                ins = dve.tensor_scalar(gt[0][:, h, :], bank[2 + h][:, 0:L], gbias[:, h:h + 1], None, ALU.add)
                if h < GH - 1:
                    ins.then_inc(dve_step, 1)
                    steps[0] += 1
                else:
                    own(ins)
            own(dve.scalar_tensor_tensor(out=gt[1][:, :, :], in0=gt[0][:, :, :], scalar=-1.0, in1=gt[0][:, :, :],
                                         op0=ALU.mult, op1=ALU.max))
            dve.tensor_scalar(gt[0][:, :, :], gt[0][:, :, :], 0.0, None, ALU.min).then_inc(gate_d, 1)
            dve.wait_ge(fgate_d, 1)
            dve.wait_ge(fgate_a, 1)
            own(dve.tensor_tensor(ct[:, 0, :], ct[:, 0, :], ct[:, 1, :], ALU.subtract))
            own(dve.tensor_tensor_scan(ct[:, 2, :], ones[0:FH, :], ct[:, 0, :], 0.0, ALU.mult, ALU.add))
            dve.tensor_scalar(ct[:, 3, :], ct[:, 2, :], -1.0, None, ALU.mult).then_inc(fgate_d, 1)
            dve.wait_ge(gate_d, 1)
            dve.wait_ge(gate_a, 1)
            own(dve.tensor_tensor(gt[0][:, :, :], gt[0][:, :, :], gt[1][:, :, :], ALU.subtract))
            dve.wait_ge(heads_consts, 6 + NCH)
            for h in range(GH):
                ins = dve.tensor_tensor_scan(gt[2][:, h, :], reset[:, :], gt[0][:, h, :], 0.0, ALU.mult, ALU.add)
                if h < GH - 1:
                    ins.then_inc(dve_step, 1)
                    steps[0] += 1
            ins.then_inc(gate_d, 1)
            dve.wait_ge(gate_d, 2)
            b_x = chunked(gt[2][:, :, META:L])
            d_x = chunked(gt[0][:, :, META:L])
            wide = [P, GH, NCH, CHUNK]
            dve.tensor_tensor(d_x, b_x[:, :, :, CHUNK - 1:CHUNK].broadcast_to(wide), b_x, ALU.subtract)\
               .then_inc(dve_step, 1)
            steps[0] += 1
            dve.tensor_tensor(gt[0][:, :, 0:META], gt[2][:, :, META - 1:META].broadcast_to([P, GH, META]),
                              gt[2][:, :, 0:META], ALU.subtract).then_inc(gate_d, 1)
            dve.wait_ge(gate_a, 2)
            own(dve.scalar_tensor_tensor(out=gt[3][:, :, :], in0=proj[:, GQ:GQ + GH, :], scalar=QSCALE,
                                         in1=gt[3][:, :, :], op0=ALU.mult, op1=ALU.mult))
            dve.wait_ge(gate_a, 4)
            own(dve.tensor_tensor(gt[1][:, :, :], proj[:, GK:GK + GH, :], gt[0][:, :, :], ALU.mult))
            dve.tensor_tensor(d_x, b_x, b_x[:, :, :, CHUNK // 2:CHUNK // 2 + 1].broadcast_to(wide),
                              ALU.subtract).then_inc(gate_d, 1)
            dve.wait_ge(gate_a, 5)
            q_x, k_x = proj[:, GQ:GQ + GH, META:L], proj[:, GK:GK + GH, META:L]
            dve.scalar_tensor_tensor(out=q_x, in0=q_x, scalar=QSCALE, in1=gt[2][:, :, META:L], op0=ALU.mult,
                                     op1=ALU.mult).then_inc(dve_step, 1)
            steps[0] += 1
            dve.wait_ge(gate_a, 6)
            dve.tensor_tensor(k_x, k_x, gt[0][:, :, META:L], ALU.mult).then_inc(gla_ops, 1)
            dve.wait_ge(fgate_t, 1)
            dve.tensor_copy(cq[:, :, :].rearrange("p t h -> p (t h)"), bank[6][:, 0:TT * FH]).then_inc(cq_ready, 1)

            def gla_masked(h):
                dve.wait_ge(scores_g, h + 1)
                if h >= 2:
                    dve.wait_ge(o_g, h - 1)
                for t in range(TT):
                    ins = dve.copy_predicated(a2[h % 2][:, t, :], chunkm[:, :].bitcast(U32),
                                              bank[0][:, t * P:(t + 1) * P])
                    if t < TT - 1:
                        ins.then_inc(dve_step, 1)
                        steps[0] += 1
                ins.then_inc(a_ready, 1)

            def gla_k(h):
                dve.wait_ge(kv_t, h + 1)
                if h:
                    dve.wait_ge(upd_g, h)
                own(dve.tensor_copy(kln[0:META, 0, :], bank[1][0:META, 0:P]))
                dve.tensor_copy(kln[:, 1:3, :].rearrange("p a b -> p (a b)"), bank[1][:, P:3 * P]).then_inc(k_ready, 1)

            def gla_states(h):
                dve.wait_ge(upd_g, h + 1)
                if h:
                    dve.wait_ge(o_g, h)
                own(dve.tensor_copy(st[:, 0, :], upd[0]))
                for n in range(1, NCH):
                    ins = dve.scalar_tensor_tensor(
                        out=st[:, n, :], in0=st[:, n - 1, :], scalar=dec[:, h, n - 1:n],
                        in1=upd[n], op0=ALU.mult, op1=ALU.add)
                    if n < NCH - 1:
                        own(ins)
                ins.then_inc(st_ready, 1)

            for h in range(GH):
                gla_masked(h)
                gla_k(h)
                gla_states(h)

            def fox_q(h):
                if h >= 2:
                    dve.wait_ge(scores_f, h - 1)
                dve.tensor_scalar(qs[h % 2][:, :], proj[:, FQ + h, META:L], QSCALE, None, ALU.mult).then_inc(q_ready, 1)

            def fox_mask(h):
                dve.wait_ge(scores_f, h + 1)
                for t in range(TT):
                    own(dve.copy_predicated(bank[2 + t][:, META + t * P:META + (t + 1) * P],
                                            above[:, :].bitcast(U32), lowest[:, :]))
                    own(dve.tensor_reduce(rs[:, h, t:t + 1], bank[2 + t][:, 0:META + (t + 1) * P], AX, ALU.max))
                own(dve.tensor_tensor(rs[:, h, 2:4], rs[:, h, 0:2], cq[:, :, h], ALU.add))
                dve.tensor_tensor(rs[:, h, 4:6], cq[:, :, h], rs[:, h, 2:4], ALU.subtract).then_inc(bias_f, 1)

            def fox_pt_meta(h):
                dve.wait_ge(p_t, h + 1)
                if h:
                    dve.wait_ge(o_f, h)
                dve.tensor_copy(ptm[:, :, :].rearrange("p a b -> p (a b)"), bank[5][0:META, 0:TT * P]).then_inc(pt_d, 1)

            def fox_out(h):
                dve.wait_ge(o_f, h + 1)
                dve.wait_ge(p_ready, h + 1)
                own(dve.reciprocal(rs[:, h, 0:2], rs[:, h, 6:8]))
                for t in range(TT):
                    ins = dve.tensor_scalar(proj[:, FQ + h, t * P:(t + 1) * P], bank[7][:, t * HD:(t + 1) * HD],
                                            rs[:, h, t:t + 1], None, ALU.mult)
                    if t < TT - 1:
                        ins.then_inc(dve_step, 1)
                        steps[0] += 1
                ins.then_inc(o_fout, 1)

            own(dve.memset(lowest[:, :], LOWEST))
            fox_q(0)
            for s in range(FH + 2):
                if s + 1 < FH:
                    fox_q(s + 1)
                if s < FH:
                    fox_mask(s)
                if 1 <= s <= FH:
                    fox_pt_meta(s - 1)
                if s >= 2:
                    fox_out(s - 2)

            dve.wait_ge(o_gout, GH)
            dve.wait_ge(sq_f, FH)
            own(dve.tensor_scalar(ss[:, 0:TT * GH], ss[:, 0:TT * GH], 1.0 / DV, EPS, ALU.mult, ALU.add))
            mean_eps(ss[:, TT * GH:], ss[:, TT * GH:], HD)
            dve.wait_ge(root_out, 2)
            own(dve.reciprocal(rms[:, :], rms[:, :]))
            for h in range(GH):
                o = proj[:, GV + VH * h:GV + VH * (h + 1), :].rearrange("p a l -> p (a l)")
                for t in range(TT):
                    dve.tensor_scalar(o[:, t * DV:(t + 1) * DV], o[:, t * DV:(t + 1) * DV],
                                      rms[:, TT * h + t:TT * h + t + 1], None, ALU.mult).then_inc(on_d, 1)
            for h in range(FH):
                for t in range(TT):
                    i = TT * (GH + h) + t
                    o = proj[:, FQ + h, t * P:(t + 1) * P]
                    dve.tensor_scalar(o, o, rms[:, i:i + 1], None, ALU.mult).then_inc(on_d, 1)
            dve.wait_ge(silu_ready, 1)
            for k in range(KD):
                dve.wait_ge(mix_t, k + 1)
                if k < GH * VH:
                    if k >= 2:
                        dve.wait_ge(mixl_ready, k - 1)
                    dve.scalar_tensor_tensor(out=mtmp[k % 2][:, :], in0=bank[k % 4][:, 0:SEQ],
                                             scalar=ggain[:, k % VH:k % VH + 1], in1=proj[:, GR + k, META:L],
                                             op0=ALU.mult, op1=ALU.mult).then_inc(mix_f, 1)
                    dve.wait_ge(mix_f, k + 1)
                    dve.wait_ge(mixh_ready, k + 1)
                    dve.tensor_tensor(mixl[:, k, :], mtmp[k % 2][:, :], mixh[:, k, :].bitcast(F32),
                                      ALU.subtract).then_inc(mixl_ready, 1)
                else:
                    dve.wait_ge(mixh_ready, k + 1)
                    dve.scalar_tensor_tensor(out=mixl[:, k, :], in0=bank[k % 4][:, 0:SEQ], scalar=fgain[:, 0:1],
                                             in1=mixh[:, k, :].bitcast(F32), op0=ALU.mult,
                                             op1=ALU.subtract).then_inc(mixl_ready, 1)

            def residual(n):
                dve.wait_ge(units_used, U_OUT + (D // 512) * (n + 1))
                for t in range(TT):
                    r = resid[:, t, 512 * n:512 * (n + 1)]
                    ins = dve.tensor_tensor(r, bank[2 * (n % 2) + t][:, :], r, ALU.add)
                    if t < TT - 1:
                        ins.then_inc(dve_step, 1)
                        steps[0] += 1
                ins.then_inc(resid_ready, 1)

            for c in range(U_OUT + 2, U_EXP):
                lo_unit(dve, c)
                if (c - U_OUT) % 4 == 1 and c - U_OUT > 4:
                    residual((c - U_OUT) // 4 - 1)
            residual(D // 512 - 1)

            dve.wait_ge(sums_ready, 2)
            mean_eps(stat2[:, 0:TT], stat[:, 0:TT], D)
            dve.wait_ge(root_out, 3)
            own(dve.reciprocal(stat2[:, 0:TT], stat[:, 0:TT]))
            dve.wait_ge(routers_in, 16 * (G + 4))
            for t in range(TT):
                dve.scalar_tensor_tensor(out=u2[:, t, :], in0=resid[:, t, :], scalar=stat2[:, t:t + 1],
                                         in1=g2b[:, :], op0=ALU.mult, op1=ALU.mult).then_inc(u2_ready, 1)
            for t in range(TT):
                dve.wait_ge(u2h_ready, t + 1)
                dve.wait_ge(u2_ready, t + 1)
                dve.tensor_tensor(u2l[:, t, :], u2[:, t, :], u2h[:, t, :].bitcast(F32),
                                  ALU.subtract).then_inc(u2l_ready, 1)

            dve.wait_ge(logits, 1)
            dve.wait_ge(masks_ready, 15)
            lg = rt["lg"]
            own(dve.tensor_tensor(lg[:, :, :], bank[5][:, 0:TT * 64].rearrange("p (t n) -> p t n", t=TT)[:, :, 0:G + E],
                                  br[:, None, :].broadcast_to([P, TT, G + E]), ALU.add))
            own(dve.tensor_copy(rt["gp"][:, :, 0:G], lg[:, :, 0:G]))
            for t in range(TT):
                own(dve.max(rt["gm"][:, t, :], rt["gp"][:, t, :]))
                own(dve.max_index(gix[:, t, :], rt["gm"][:, t, :], rt["gp"][:, t, :]))
            dve.tensor_scalar(esum[:, 0:TT], rt["gm"][:, :, 0], -1.0, None, ALU.mult).then_inc(route_d, 1)
            own(dve.tensor_copy(rt["gi"][:, :, :], gix[:, :, :]))
            for t in range(TT):
                own(dve.tensor_scalar(rt["oh"][:, t, :], count[:, 0:G], rt["gi"][:, t, 0:1], None, ALU.is_equal))
            own(dve.tensor_tensor(rt["t32"][:, :, :].rearrange("p t (g e) -> p t g e", g=G),
                                  lg[:, :, G:].rearrange("p t (g e) -> p t g e", g=G),
                                  rt["oh"][:, :, :, None].broadcast_to([P, TT, G, E8]), ALU.mult))
            own(dve.tensor_reduce(rt["sel8"][:, :, :], rt["t32"][:, :, :].rearrange("p t (g e) -> p t e g", g=G),
                                  AX, ALU.add))
            own(dve.tensor_reduce(esum[:, 8:10], rt["sel8"][:, :, :], AX, ALU.max))
            dve.tensor_scalar(esum[:, 4:6], esum[:, 8:10], -1.0, None, ALU.mult).then_inc(route_d, 1)
            dve.wait_ge(route_a, 2)
            own(dve.reciprocal(esum[:, 10:12], esum[:, 2:4]))
            own(dve.reciprocal(esum[:, 12:14], esum[:, 6:8]))
            own(dve.tensor_tensor(rt["pe"][:, :, :], rt["pe"][:, :, :],
                                  esum[:, 12:14][:, :, None].broadcast_to([P, TT, 8]), ALU.mult))
            for t in range(TT):
                own(dve.max(rt["top"][:, t, :], rt["pe"][:, t, :]))
                own(dve.max_index(tix[:, t, :], rt["top"][:, t, :], rt["pe"][:, t, :]))
            own(dve.tensor_copy(rt["ti"][:, :, :], tix[:, :, :]))
            own(dve.tensor_tensor(esum[:, 14:16], rt["top"][:, :, 0], rt["top"][:, :, 1], ALU.add))
            own(dve.reciprocal(esum[:, 16:18], esum[:, 14:16]))
            own(dve.tensor_tensor(cw[:, :, :], rt["top"][:, :, 0:2],
                                  esum[:, 16:18][:, :, None].broadcast_to([P, TT, 2]), ALU.mult))
            own(dve.tensor_tensor(cw[:, :, :], cw[:, :, :],
                                  esum[:, 10:12][:, :, None].broadcast_to([P, TT, 2]), ALU.mult))
            for t in range(TT):
                own(dve.scalar_tensor_tensor(out=rt["eid"][:, t, :], in0=rt["gi"][:, t, 0:1].broadcast_to([P, 2]),
                                             scalar=float(E8), in1=rt["ti"][:, t, 0:2], op0=ALU.mult, op1=ALU.add))
                for k in range(2):
                    own(dve.tensor_scalar(rt[f"m{k}"][:, t, :], count[:, 0:E], rt["eid"][:, t, k:k + 1], None,
                                          ALU.is_equal))
            dve.tensor_tensor(rt["mm"][:, :, :], rt["m0"][:, :, :], rt["m1"][:, :, :], ALU.add).then_inc(route_d, 1)
            for t in range(TT):
                for k in range(2):
                    own(dve.tensor_scalar(esum[:, 20 + 2 * t + k:21 + 2 * t + k], rowno[:, :],
                                          float(k * SEQ + t * P) - BIG, None, ALU.add))
                own(dve.tensor_scalar(rt["t32"][:, t, :], rt["m1"][:, t, :], esum[:, 21 + 2 * t:22 + 2 * t], None, ALU.mult))
                own(dve.scalar_tensor_tensor(out=rowid[:, t, 0:E], in0=rt["m0"][:, t, :],
                                             scalar=esum[:, 20 + 2 * t:21 + 2 * t], in1=rt["t32"][:, t, :],
                                             op0=ALU.mult, op1=ALU.add))
            own(dve.memset(empty[:, :], BIG))
            dve.wait_ge(ranks, 1)
            dve.wait_ge(route_d, 3)
            for t in range(TT):
                own(dve.scalar_tensor_tensor(out=key[:, t, 0:E], in0=bank[6][:, 64 * t:64 * t + E], scalar=1.0,
                                             in1=rt["mm"][:, t, :], op0=ALU.add, op1=ALU.mult))
            own(dve.tensor_reduce(esum[:, 18:19], bank[6][:, 2 * 64:2 * 64 + E], AX, ALU.max))
            own(dve.tensor_scalar(rounds[:, :], limit[:, :], esum[:, 18:19], None, ALU.is_lt))
            own(dve.tensor_reduce(esum[:, 19:20], rounds[:, :], AX, ALU.add))
            dve.tensor_copy(nrounds[:, :], esum[:, 19:20]).then_inc(routed, 1)
            dve.wait_ge(routed, 1)

            def picked(e):
                for t in range(TT):
                    ins = dve.tensor_scalar(pick[:, t, :], count[:, 1:SLOTS + 1], key[:, t, bass.ds(e, 1)], None,
                                            ALU.is_equal)
                    if t == TT - 1:
                        ins.then_inc(pick_ready, 1)

            def result(n, q):
                dve.wait_ge(ylo_ready, 4 * n + q + 1)
                s = slice(512 * q, 512 * (q + 1))
                dve.tensor_tensor(yrow[:, s], bank[2 + q][0:SLOTS, :], ylo[:, s], ALU.add).then_inc(y_ready, 1)

            n_rounds = dve.value_load(nrounds[0:1, 0:1], min_val=1, max_val=SEQ // SLOTS)
            with dve.Fori(0, n_rounds) as r:
                picked(0)
                with dve.Fori(0, E) as e:
                    n = E * r + e
                    for j in range(PER):
                        if j == 9:
                            dve.wait_ge(ulo_ready, n + 1)
                            dve.tensor_tensor(usum[:, :], bank[1][0:SLOTS, :], ulo[:, :], ALU.add).then_inc(usum_ready, 1)
                            dve.wait_ge(silu_e, n + 1)
                            dve.wait_ge(usum_ready, n + 1)
                            dve.tensor_tensor(gsum[:, :], glo[:, :], usum[:, :], ALU.mult).then_inc(h_ready, 1)
                        lo_unit(dve, U_EXP + j, 2 * n)
                        if j == 1:
                            dve.wait_ge(idx_ready, n + 1)
                            result(n, 0)
                            result(n, 1)
                        if j == 2:
                            result(n, 2)
                            result(n, 3)
                        if j == 5:
                            dve.wait_ge(glo_ready, n + 1)
                            dve.tensor_tensor(gsum[:, :], bank[0][0:SLOTS, :], glo[:, :], ALU.add).then_inc(gsum_ready, 1)
                        if j == 6:
                            dve.wait_ge(idn_mm, n + 1)
                            dve.tensor_tensor(idn[:, :], bank[7][0:SLOTS, 0:1], empty[0:SLOTS, :], ALU.add).then_inc(idn_ready, 1)
                            picked(e + 1)
                        if j == 9:
                            dve.wait_ge(hsh_ready, n + 1)
                            dve.tensor_tensor(hs[:, :, SLOTS:2 * SLOTS], bank[0][:, 0:FE // P * SLOTS]
                                              .rearrange("p (k s) -> p k s", s=SLOTS),
                                              hs[:, :, 0:SLOTS].bitcast(F32), ALU.subtract).then_inc(hsl_ready, 1)
                dve.wait_ge(xs_mm, 4 * (E + 1) * r + 4 * (E + 1))
                dve.wait_ge(pick_ready, (E + 1) * r + E + 1)
                dve.tensor_scalar(key[:, :, :], key[:, :, :], -float(SLOTS), None, ALU.add).then_inc(key_moved, 1)
                dve.wait_ge(key_moved, r + 1)
            dve.wait_ge(idx_ready, E * n_rounds + 1)
            for q in range(4):
                result(E * n_rounds, q)

            dve.wait_ge(routers_in, 16 * (G + 5))
            dve.wait_ge(yk_in, 16 * TT * 2)
            for t in range(TT):
                own(dve.scalar_tensor_tensor(out=resid[:, t, :], in0=yk[:, t, 0, :], scalar=cw[:, t, 0:1],
                                             in1=resid[:, t, :], op0=ALU.mult, op1=ALU.add))
                dve.scalar_tensor_tensor(out=resid[:, t, :], in0=yk[:, t, 1, :], scalar=cw[:, t, 1:2],
                                         in1=resid[:, t, :], op0=ALU.mult, op1=ALU.add).then_inc(summed, 1)
            for t in range(TT):
                dve.wait_ge(sums_ready, 3 + t)
                mean_eps(stat2[:, t:t + 1], stat[:, t:t + 1], D)
                dve.wait_ge(root_out, 4 + t)
                own(dve.reciprocal(stat2[:, 4 + t:5 + t], stat[:, 2 + t:3 + t]))
                dve.scalar_tensor_tensor(out=u2[:, t, :], in0=resid[:, t, :], scalar=stat2[:, 4 + t:5 + t],
                                         in1=gfb[:, :], op0=ALU.mult, op1=ALU.mult).then_inc(out_ready, 1)

        @block.tensor
        def _(pe):
            pe.wait_ge(masks_ready, 7)
            pe.wait_ge(xn_ready, TT + 1)
            for k in range(KD):
                if k >= 4:
                    pe.wait_ge(ul_ready, k - 3)
                o = bank[k % 4]
                pe.transpose(o[:, 0:META], mn[:, k::KD], ident[0:META, 0:META])
                for t in range(TT):
                    ins = pe.transpose(o[:, META + t * P:META + (t + 1) * P], xn[:, t, k::KD], ident[:, :])
                ins.then_inc(xt_ready, 1)

            def block_unit(c, m=0, out=None):
                pe.wait_ge(lo_ready, nth(c + 1, m))
                h, l = hi[c % SPLIT], lo[c % SPLIT]
                for k in range(KD):
                    pe.matmul(out, part(h, k, P), uh[:, k, :], start=(k == 0), stop=False)
                    pe.matmul(out, part(h, k, P), ul[:, k, :], start=False, stop=False)
                    ins = pe.matmul(out, part(l, k, P), uh[:, k, :], start=False, stop=(k == KD - 1))
                ins.then_inc(units_used, 1)

            pe.wait_ge(ul_ready, KD)
            block_unit(0, out=bank[7][:, 0:L])
            for c in range(U_IN, STRAIGHT):
                if c - U_IN >= 2:
                    pe.wait_ge(proj_out, c - U_IN - 1)
                block_unit(c, out=bank[c % 2][:, 0:L])
            with pe.Fori(0, LOOPS) as i:
                for j in range(RAW):
                    c = STRAIGHT + j
                    pe.wait_ge(proj_out, nth(c - U_IN - 1, i))
                    block_unit(c, i, out=bank[c % 2][:, 0:L])

            pe.wait_ge(params_in, 16 * 5)
            pe.wait_ge(z_ready, 1)
            for h in range(GH):
                ins = pe.matmul(bank[2 + h][:, 0:L], wgate2[:, h * P:(h + 1) * P], zt[:, :], start=True, stop=True)
            ins.then_inc(gates_mm, 1)
            pe.wait_ge(fgate_d, 2)
            for t in range(TT):
                ins = pe.transpose(bank[6][:, t * FH:(t + 1) * FH], ct[:, 2, META + t * P:META + (t + 1) * P],
                                   ident[0:FH, 0:FH])
            ins.then_inc(fgate_t, 1)
            pe.wait_ge(cq_ready, 1)

            def tokens(t):
                return slice(META + t * P, META + (t + 1) * P)

            def gla_first(h):
                if h:
                    pe.wait_ge(a_ready, h)
                for t in range(TT):
                    ins = pe.matmul(bank[0][:, t * P:(t + 1) * P], proj[:, GK + h, tokens(t)],
                                    proj[:, GQ + h, tokens(t)], start=True, stop=True)
                ins.then_inc(scores_g, 1)
                if h:
                    pe.wait_ge(k_ready, h)
                    pe.wait_ge(v_ready, h)
                pe.transpose(bank[1][0:META, 0:P], gt[1][:, h, 0:META], ident[:, :])
                for t in range(TT):
                    pe.transpose(bank[1][:, (t + 1) * P:(t + 2) * P], gt[1][:, h, tokens(t)], ident[:, :])
                for i in range(VH):
                    v = GV + VH * h + i
                    pe.transpose(bank[2][0:META, i * P:(i + 1) * P], proj[:, v, 0:META], ident[:, :])
                    pe.transpose(bank[2][:, DV + i * P:DV + (i + 1) * P], proj[:, v, tokens(0)], ident[:, :])
                    ins = pe.transpose(bank[3][:, i * P:(i + 1) * P], proj[:, v, tokens(1)], ident[:, :])
                ins.then_inc(kv_t, 1)

            def gla_update(h):
                pe.wait_ge(k_ready, h + 1)
                pe.wait_ge(v_ready, h + 1)
                if h:
                    pe.wait_ge(st_ready, h)
                for n in range(NCH):
                    rows = slice(0, META) if n == 0 else slice((n - 1) % 2 * CHUNK, ((n - 1) % 2 + 1) * CHUNK)
                    tile = 0 if n == 0 else 1 + (n - 1) // 2
                    ins = pe.matmul(upd[n], kln[rows, tile, :],
                                    vn[rows, tile, :], start=True, stop=True)
                ins.then_inc(upd_g, 1)

            def gla_output(h):
                pe.wait_ge(a_ready, h + 1)
                pe.wait_ge(st_ready, h + 1)
                if h:
                    pe.wait_ge(o_gout, h)
                for t in range(TT):
                    o = bank[6][:, t * DV:(t + 1) * DV]
                    pe.matmul(o, a2[h % 2][:, t, :], vn[:, 1 + t, :], start=True, stop=False, skip_group_check=True)
                    for i in range(2):
                        n = 2 * t + i
                        cols = slice(META + n * CHUNK, META + (n + 1) * CHUNK)
                        ins = pe.matmul(o[i * CHUNK:(i + 1) * CHUNK, :], gt[3][:, h, cols], st[:, n, :],
                                        start=False, stop=(i == 1), skip_group_check=True)
                ins.then_inc(o_g, 1)

            pe.wait_ge(gla_ops, 1)
            for h in range(GH):
                gla_first(h)
                gla_update(h)
                gla_output(h)

            def fox_scores(h):
                pe.wait_ge(q_ready, h + 1)
                if h:
                    pe.wait_ge(p_ready, h)
                else:
                    pe.wait_ge(heads_consts, 6 + NCH)
                for t in range(TT):
                    w = META + (t + 1) * P
                    pe.matmul(bank[2 + t][:, 0:w], qs[h % 2][:, t * P:(t + 1) * P], proj[:, FK + h, 0:w],
                              start=True, stop=False)
                    ins = pe.matmul(bank[2 + t][:, 0:w], sel[:, h, :], ct[:, 3, 0:w], start=False, stop=True)
                ins.then_inc(scores_f, 1)
                if h:
                    pe.wait_ge(vf_ready, h)
                pe.transpose(bank[6][0:META, 0:HD], proj[:, FV + h, 0:META], ident[:, :])
                for t in range(TT):
                    ins = pe.transpose(bank[6][:, (t + 1) * HD:(t + 2) * HD], proj[:, FV + h, tokens(t)], ident[:, :])
                ins.then_inc(vf_t, 1)

            def fox_transpose(h):
                pe.wait_ge(p_ready, h + 1)
                if h:
                    pe.wait_ge(pt_a, h)
                    pe.wait_ge(pt_d, h)
                for t in range(TT):
                    pe.transpose(bank[5][0:META, t * P:(t + 1) * P], pr[:, t, 0:META], ident[:, :])
                pe.transpose(bank[4][:, 0:P], pr[:, 0, tokens(0)], ident[:, :])
                pe.transpose(bank[4][:, P:2 * P], pr[:, 1, tokens(0)], ident[:, :])
                pe.transpose(bank[4][:, 2 * P:3 * P], pr[:, 1, tokens(1)], ident[:, :]).then_inc(p_t, 1)

            def fox_values(h):
                pe.wait_ge(pt_a, h + 1)
                pe.wait_ge(pt_d, h + 1)
                pe.wait_ge(vf_ready, h + 1)
                if h:
                    pe.wait_ge(o_fout, h)
                v = vf[h % 2]
                for t in range(TT):
                    o = bank[7][:, t * HD:(t + 1) * HD]
                    pe.matmul(o, ptm[:, t, :], v[0:META, 0, :], start=True, stop=False)
                    for i in range(t + 1):
                        ins = pe.matmul(o, pt[:, t + i, :], v[:, 1 + i, :], start=False, stop=(i == t))
                ins.then_inc(o_f, 1)

            for s in range(FH + 2):
                if s < FH:
                    if s == 0:
                        pe.wait_ge(st_ready, GH)
                        pe.wait_ge(o_gout, GH)
                        pe.wait_ge(v_ready, GH)
                    fox_scores(s)
                if 1 <= s <= FH:
                    fox_transpose(s - 1)
                if s >= 2:
                    fox_values(s - 2)

            for k in range(KD):
                if k >= 4:
                    pe.wait_ge(mixl_ready, k - 3)
                if k < GH * VH:
                    h, i = k // VH, k % VH
                    o = proj[:, GV + VH * h:GV + VH * (h + 1), :].rearrange("p a l -> p (a l)")
                    src = [o[:, t * DV + i * P:t * DV + (i + 1) * P] for t in range(TT)]
                    pe.wait_ge(on_d, TT * (h + 1))
                else:
                    src = [proj[:, FQ + k - GH * VH, t * P:(t + 1) * P] for t in range(TT)]
                    pe.wait_ge(on_d, TT * GH + TT * (k - GH * VH + 1))
                for t in range(TT):
                    ins = pe.transpose(bank[k % 4][:, t * P:(t + 1) * P], src[t], ident[:, :])
                ins.then_inc(mix_t, 1)

            pe.wait_ge(mixl_ready, KD)
            for n in range(D // 512):
                if n >= 2:
                    pe.wait_ge(resid_ready, n - 1)
                for q in range(D // 512):
                    c = U_OUT + n * (D // 512) + q
                    pe.wait_ge(lo_ready, c + 1)
                    for kk in range(4):
                        k = 4 * q + kk
                        for t in range(TT):
                            o = bank[2 * (n % 2) + t][:, :]
                            cols = slice(t * P, (t + 1) * P)
                            pe.matmul(o, mixh[:, k, cols], part(hi[c % SPLIT], kk, 512), start=(k == 0), stop=False)
                            pe.matmul(o, mixl[:, k, cols], part(hi[c % SPLIT], kk, 512), start=False, stop=False)
                            ins = pe.matmul(o, mixh[:, k, cols], part(lo[c % SPLIT], kk, 512), start=False,
                                            stop=(k == KD - 1))
                    ins.then_inc(units_used, 1)

            pe.wait_ge(u2_ready, TT)
            pe.wait_ge(resid_ready, D // 512)
            for i in range(KD // 2):
                if i >= 4:
                    pe.wait_ge(u2t_a, i - 3)
                for j in range(2):
                    for t in range(TT):
                        ins = pe.transpose(bank[i % 4][:, j * SEQ + t * P:j * SEQ + (t + 1) * P],
                                           u2[:, t, 2 * i + j::KD], ident[:, :])
                ins.then_inc(u2_t, 1)
            pe.wait_ge(u2t_a, KD // 2)
            pe.wait_ge(routers_in, 16 * (G + 4))
            for t in range(TT):
                for k in range(KD):
                    ins = pe.matmul(bank[5][:, t * 64:t * 64 + G + E], u2t[:, k, t * P:(t + 1) * P], wr[:, k, :],
                                    start=(k == 0), stop=(k == KD - 1))
            ins.then_inc(logits, 1)
            pe.wait_ge(route_d, 3)
            mm = rt["mm"]
            pe.matmul(bank[6][:, 0:E], above[:, :], mm[:, 0, :], start=True, stop=True)
            pe.matmul(bank[6][:, 64:64 + E], above[:, :], mm[:, 1, :], start=True, stop=False)
            pe.matmul(bank[6][:, 64:64 + E], ones[:, 0:P], mm[:, 0, :], start=False, stop=True)
            for t in range(TT):
                ins = pe.matmul(bank[6][:, 128:128 + E], ones[:, 0:P], mm[:, t, :], start=(t == 0), stop=(t == TT - 1))
            ins.then_inc(ranks, 1)

            def gather(q, before):
                if q >= 2:
                    pe.wait_ge(xs_ready, before + q - 1)
                for kk in range(4):
                    for lohi, u in enumerate((u2h, u2l)):
                        k = 4 * q + kk
                        for t in range(TT):
                            ins = pe.matmul(bank[6 + q % 2][:, (2 * kk + lohi) * SLOTS:(2 * kk + lohi + 1) * SLOTS],
                                            u[:, t, k * P:(k + 1) * P], pick[:, t, :], start=(t == 0), stop=(t == TT - 1))
                ins.then_inc(xs_mm, 1)

            def expert_unit(c, m, outs, lhs, first, last):
                pe.wait_ge(lo_ready, nth(c + 1, m))
                for i, (o, k) in enumerate(zip(outs, lhs)):
                    pe.matmul(o[:, :], k, part(hi[c % SPLIT], i, 512), start=first(i), stop=False)
                    ins = pe.matmul(o[:, :], k, part(lo[c % SPLIT], i, 512), start=False, stop=last(i))
                ins.then_inc(units_used, 1)

            pe.wait_ge(u2l_ready, TT)
            pe.wait_ge(routed, 1)
            for q in range(4):
                ins = pe.matmul(bank[2 + q][:, :], ident[:, :], u2[:, 0, 0:512], start=True, stop=True)
            ins.then_inc(stand_in, 1)
            n_rounds = pe.value_load(nrounds[0:1, 0:1], min_val=1, max_val=SEQ // SLOTS)
            with pe.Fori(0, n_rounds) as r:
                pe.wait_ge(pick_ready, (E + 1) * r + 1)
                for q in range(4):
                    gather(q, 4 * (E + 1) * r)
                with pe.Fori(0, E) as e:
                    n = E * r + e
                    m = 2 * n
                    pe.wait_ge(xs_ready, 4 * (n + r + 1))
                    for w in range(2):
                        for q in range(4):
                            expert_unit(U_EXP + 4 * w + q, m, [bank[w]] * 4,
                                        [xs[:, 4 * q + i, :] for i in range(4)],
                                        lambda i: q == 0 and i == 0, lambda i: q == 3 and i == 3)
                        if w == 0:
                            for t in range(TT):
                                ins = pe.matmul(bank[7][0:SLOTS, 0:1], pick[:, t, :].bitcast(F32),
                                                rowid[:, t, bass.ds(e, 1)], start=(t == 0), stop=(t == TT - 1))
                            ins.then_inc(idn_mm, 1)
                    pe.wait_ge(pick_ready, n + r + 2)
                    gather(0, 4 * (n + r + 1))
                    pe.wait_ge(idn_ready, n + 1)
                    gather(1, 4 * (n + r + 1))
                    pe.wait_ge(h_ready, n + 1)
                    for k in range(FE // P):
                        ins = pe.matmul(bank[0][:, k * SLOTS:(k + 1) * SLOTS], gsum[:, k * P:(k + 1) * P],
                                        ident[0:SLOTS, 0:SLOTS], start=True, stop=True)
                    ins.then_inc(h_t, 1)
                    pe.wait_ge(hsh_ready, n + 1)
                    pe.wait_ge(hsl_ready, n + 1)
                    pe.wait_ge(y_ready, 4 * n + 4)
                    for q in range(4):
                        expert_unit(U_EXP + 8 + q, m, bank[2:6], [hs[:, q, :]] * 4,
                                    lambda i: q == 0, lambda i: q == 3)
                        if q == 0:
                            gather(2, 4 * (n + r + 1))
                            gather(3, 4 * (n + r + 1))
                pe.wait_ge(xs_ready, 4 * (E + 1) * r + 4 * (E + 1))


_INS = ['x', 'meta_tokens', 'norm1_g', 'w_in', 'b_fox_f', 'gla_w_gate2', 'gla_b_gate', 'gla_norm_g',
        'fox_norm_g', 'w_out', 'norm2_g', 'w_router_group', 'b_router_group', 'w_router_expert',
        'b_router_expert', 'w_exp_gate', 'w_exp_up', 'w_exp_down', 'norm_f_g']


def kernel(**inputs):
    import numpy as _np
    import concourse.bacc as _bacc
    from concourse import mybir as _mybir
    from concourse.bass_utils import run_bass_kernel_spmd as _run

    nc = _bacc.Bacc("TRN2", target_bir_lowering=False, num_devices=1)
    arrays, args = {}, []
    for name in _INS:
        a = _np.ascontiguousarray(inputs[name])
        arrays[f"in_{name}_dram"] = a
        args.append(nc.dram_tensor(f"in_{name}_dram", a.shape, _mybir.dt.from_np(a.dtype), kind="ExternalInput").ap())
    shape = inputs["x"].shape
    args.append(nc.dram_tensor("out_dram", shape, _mybir.dt.float32, kind="ExternalOutput").ap())
    hybrid_layer(nc, *args)
    r = _run(nc, [arrays], core_ids=[0])
    return r.results[0]["out_dram"]
```

```python
from contextlib import ExitStack

import concourse.bass as bass
from concourse import mybir

F32 = mybir.dt.float32
F32R = mybir.dt.float32r
U32 = mybir.dt.uint32
ALU = mybir.AluOpType
ACT = mybir.ActivationFunctionType
AX = mybir.AxisListType.X

P = 128
EPS = 1e-6
GLA_TAU = 16.0
CHUNK = 64
SLOTS = 64
RAW = 6
UNIT = 2048
HALF = UNIT // 2
SPLIT = 4
BIG = 4096.0
LOWEST = -3.4028234663852886e38


def hybrid_layer(nc, x, meta_tokens, norm1_g, w_in, b_fox_f, gla_w_gate2, gla_b_gate, gla_norm_g,
                 fox_norm_g, w_out, norm2_g, w_router_group, b_router_group, w_router_expert,
                 b_router_expert, w_exp_gate, w_exp_up, w_exp_down, norm_f_g, out):
    _, SEQ, D = x.shape
    META = meta_tokens.shape[0]
    L = META + SEQ
    KD = D // P
    TT = SEQ // P
    GH = gla_w_gate2.shape[2] // P
    DV = gla_norm_g.shape[1]
    VH = DV // P
    FH = b_fox_f.shape[1]
    HD = fox_norm_g.shape[1]
    G, E8 = w_router_expert.shape[1], w_router_expert.shape[3]
    E = G * E8
    FE = w_exp_gate.shape[4]
    RANK = gla_w_gate2.shape[1]
    NCH = SEQ // CHUNK
    QSCALE = float(P) ** -0.5

    FOX_COLS = 3 * FH * HD
    GLA_COL0 = FOX_COLS + FH
    GLA_BLOCKS = GH + GH + GH * VH + GH * VH
    Z_COL = GLA_COL0 + GLA_BLOCKS * P
    NB = GLA_BLOCKS + FOX_COLS // P
    GQ, GK, GV, GR = 0, GH, 2 * GH, 2 * GH + GH * VH
    FQ = GLA_BLOCKS
    FK, FV = FQ + FH, FQ + 2 * FH
    Z_AT = 32

    U_IN = 1
    U_OUT = U_IN + NB
    NOUT = (D // 512) * (D // 512)
    U_EXP = U_OUT + NOUT
    PER = 12
    U_STEP = U_EXP + 8
    assert GLA_BLOCKS % RAW == 0 and NB % RAW == 0 and PER % RAW == 0
    assert KD * P == UNIT and FE == 512 and D == 2048 and 2 * RAW % SPLIT == 0

    win = w_in[0].rearrange("(p k) n -> p k n", k=KD)
    wout = w_out[0]
    wg = w_exp_gate[0].rearrange("g e d f -> (g e) d f")
    wu = w_exp_up[0].rearrange("g e d f -> (g e) d f")
    wd = w_exp_down[0].rearrange("g e f d -> (g e) f d")

    with ExitStack() as ctx:
        def sem(name):
            return ctx.enter_context(nc.semaphore(name))

        class Area:

            def __init__(self, at):
                self.at = at

            def __call__(self, name, shape, dt=F32):
                size = 4
                for n in shape[1:]:
                    size *= n
                t = nc.alloc_sbuf_tensor_at(name, shape, dt, offset=self.at)
                self.at += (size + 31) // 32 * 32
                assert self.at <= SBUF_END, name
                return t

        SBUF_END = nc.sbuf_top
        keep = Area((nc.sbuf_base + 31) // 32 * 32)
        raw = [keep(f"raw{i}", [P, UNIT]) for i in range(RAW)]
        hi = [keep(f"hi{i}", [P, HALF], F32R) for i in range(SPLIT)]
        lo = [keep(f"lo{i}", [P, HALF], F32R) for i in range(SPLIT)]
        resid = keep("resid", [P, TT, D])
        ident = keep("ident", [P, P])
        above = keep("above", [P, P])
        chunkm = keep("chunkm", [P, P])
        ones = keep("ones", [P, L])
        count = keep("count", [P, CHUNK + 1])
        rowno = keep("rowno", [P, 1])
        g1 = keep("g1", [P, KD])
        wr = keep("wr", [P, KD, G + E])
        br = keep("br", [P, G + E])
        gbias = keep("gbias", [P, GH])
        ggain = keep("ggain", [P, VH])
        fgain = keep("fgain", [P, 1])
        wgate2 = keep("wgate2", [RANK, GH * P])
        fbias = keep("fbias", [FH, 1])
        stat = keep("stat", [P, 8])
        stat2 = keep("stat2", [P, 8])

        proj_area = Area(keep.at)
        proj = proj_area("proj", [P, NB, L])
        temp = Area(proj_area.at)
        gt = [temp(f"gt{i}", [P, GH, L]) for i in range(4)]
        dec = temp("dec", [P, GH, NCH])
        ss = temp("ss", [P, 2 * (GH + FH)])
        rms = temp("rms", [P, 2 * (GH + FH)])
        rs = temp("rs", [P, FH, 8])
        mtmp_area = Area(proj_area.at)
        mtmp = [mtmp_area(f"mtmp{i}", [P, SEQ]) for i in range(2)]
        xn_area = Area(keep.at)
        xn = xn_area("xn", [P, TT, D])
        mn = xn_area("mn", [META, D])
        xjunk = xn_area("xjunk", [P, D])
        u_area = Area(temp.at)
        uh = u_area("uh", [P, KD, L], F32R)
        ul = u_area("ul", [P, KD, L], F32R)
        head = Area(temp.at)
        sel = head("sel", [FH, FH, P])
        ct = head("ct", [FH, 4, L])
        cq = head("cq", [P, TT, FH])
        a2 = [head(f"a2_{i}", [P, TT, P]) for i in range(2)]
        kln = head("kln", [P, 1 + TT, P])
        vn = head("vn", [P, 1 + TT, DV])
        st = head("st", [P, NCH, DV])
        qs = [head(f"qs{i}", [P, SEQ]) for i in range(2)]
        pr = head("pr", [P, TT, L])
        pt = head("pt", [P, 3, P])
        ptm = head("ptm", [META, TT, P])
        vf = [head(f"vf{i}", [P, 1 + TT, HD]) for i in range(2)]
        junk = head("junk", [P, DV])
        zt = head("zt", [RANK, L])
        lowest = head("lowest", [P, P])
        reset = head("reset", [P, L])
        mix_area = Area(temp.at)
        mixh = mix_area("mixh", [P, KD, SEQ], F32R)
        mixl = mix_area("mixl", [P, KD, SEQ], F32R)

        ex = Area(keep.at)
        g2b = ex("g2b", [P, D])
        u2 = ex("u2", [P, TT, D])
        key = ex("key", [P, TT, E + 1])
        rowid = ex("rowid", [P, TT, E + 1])
        pick = ex("pick", [P, TT, 3 * SLOTS], F32R)
        idn = ex("idn", [SLOTS, 1], U32)
        idx = ex("idx", [SLOTS, 1], U32)
        nil = ex("nil", [SLOTS, 1], U32)
        empty = ex("empty", [P, 1])
        cw = ex("cw", [P, TT, 2])
        rounds = ex("rounds", [P, 4])
        limit = ex("limit", [P, 4])
        nrounds = ex("nrounds", [P, 1], U32)
        rt = {}
        for name, n in (("lg", G + E), ("gp", 8), ("gm", 8), ("gi", 8), ("ge", 8), ("oh", G), ("sel8", 8),
                        ("pe", 8), ("top", 8), ("ti", 8), ("eid", 2), ("m0", E), ("m1", E), ("mm", E), ("t32", E)):
            rt[name] = ex("rt_" + name, [P, TT, n])
        gix = ex("gix", [P, TT, 8], U32)
        tix = ex("tix", [P, TT, 8], U32)
        esum = ex("esum", [P, 32])
        sq2 = ex("sq2", [P, TT, D // 512])
        u2_area = Area(ex.at)
        u2h = u2_area("u2h", [P, TT, D], F32R)
        u2l = u2_area("u2l", [P, TT, D], F32R)
        ex2 = Area(u2_area.at)
        yrow = ex2("yrow", [SLOTS, D])
        ylo = ex2("ylo", [SLOTS, D])
        xs = ex2("xs", [P, KD, 2 * SLOTS], F32R)
        hs = ex2("hs", [P, FE // P, 2 * SLOTS], F32R)
        xg = ex2("xg", [P, 512])
        glo = ex2("glo", [SLOTS, FE])
        gsum = ex2("gsum", [SLOTS, FE])
        ulo = ex2("ulo", [SLOTS, FE])
        usum = ex2("usum", [SLOTS, FE])
        u2t = Area(u2_area.at)("u2t", [P, KD, SEQ])
        fin = Area(ex.at)
        yk = fin("yk", [P, TT, 2, D])
        gfb = Area(keep.at)("gfb", [P, D])

        scratch = nc.dram_tensor("expert_rows", [2 * SEQ, D], F32)
        bank = [ctx.enter_context(nc.psum_tensor(f"bank{i}", [P, 512], F32)) for i in range(8)]
        masks_ready = sem("masks_ready")
        heads_consts = sem("heads_consts")
        params_in = sem("params_in")
        routers_in = sem("routers_in")
        x_in = sem("x_in")
        raw_zero = sem("raw_zero")
        narrow_in = sem("narrow_in")
        raw_in = [sem(f"raw_in{i}") for i in range(RAW)]
        hi_ready = sem("hi_ready")
        lo_ready = sem("lo_ready")
        halves_used = sem("halves_used")
        proj_out = sem("proj_out")
        act_step = sem("act_step")
        dve_step = sem("dve_step")
        quarters_sq = sem("quarters_sq")
        sums_ready = sem("sums_ready")
        root_in = sem("root_in")
        root_out = sem("root_out")
        xn_ready = sem("xn_ready")
        xt_ready = sem("xt_ready")
        uh_ready = sem("uh_ready")
        ul_ready = sem("ul_ready")
        z_ready = sem("z_ready")
        gates_mm = sem("gates_mm")
        gate_d = sem("gate_d")
        gate_a = sem("gate_a")
        fgate_d = sem("fgate_d")
        fgate_a = sem("fgate_a")
        fgate_t = sem("fgate_t")
        cq_ready = sem("cq_ready")
        gla_ops = sem("gla_ops")
        scores_g = sem("scores_g")
        kv_t = sem("kv_t")
        a_ready = sem("a_ready")
        k_ready = sem("k_ready")
        v_ready = sem("v_ready")
        upd_g = sem("upd_g")
        st_ready = sem("st_ready")
        o_g = sem("o_g")
        o_gout = sem("o_gout")
        q_ready = sem("q_ready")
        scores_f = sem("scores_f")
        bias_f = sem("bias_f")
        p_ready = sem("p_ready")
        vf_t = sem("vf_t")
        vf_ready = sem("vf_ready")
        p_t = sem("p_t")
        pt_a = sem("pt_a")
        pt_d = sem("pt_d")
        o_f = sem("o_f")
        o_fout = sem("o_fout")
        sq_f = sem("sq_f")
        silu_ready = sem("silu_ready")
        rms_ready = sem("rms_ready")
        on_d = sem("on_d")
        on_p = sem("on_p")
        mix_t = sem("mix_t")
        mix_f = sem("mix_f")
        mixh_ready = sem("mixh_ready")
        mixl_ready = sem("mixl_ready")
        resid_ready = sem("resid_ready")
        u2_ready = sem("u2_ready")
        u2h_ready = sem("u2h_ready")
        u2l_ready = sem("u2l_ready")
        u2_t = sem("u2_t")
        u2t_a = sem("u2t_a")
        logits = sem("logits")
        route_d = sem("route_d")
        route_a = sem("route_a")
        ranks = sem("ranks")
        rows_ready = sem("rows_ready")
        routed = sem("routed")
        pick_ready = sem("pick_ready")
        xg_mm = sem("xg_mm")
        xg_ready = sem("xg_ready")
        xs_t = sem("xs_t")
        xs_ready = sem("xs_ready")
        glo_ready = sem("glo_ready")
        gsum_ready = sem("gsum_ready")
        silu_e = sem("silu_e")
        ulo_ready = sem("ulo_ready")
        usum_ready = sem("usum_ready")
        h_ready = sem("h_ready")
        h_t = sem("h_t")
        hsh_ready = sem("hsh_ready")
        hsl_ready = sem("hsl_ready")
        idn_ready = sem("idn_ready")
        idx_ready = sem("idx_ready")
        ylo_ready = sem("ylo_ready")
        y_ready = sem("y_ready")
        scattered = sem("scattered")
        scatters = sem("scatters")
        yk_in = [sem(f"yk_in{t}") for t in range(TT)]
        out_ready = sem("out_ready")
        stat_zero = sem("stat_zero")
        summed = sem("summed")
        idn_mm = sem("idn_mm")
        key_moved = sem("key_moved")
        stored = sem("stored")

        def slot(c):
            return c % RAW

        def turn(c, m):
            return m + c // RAW

        def nth(c, m):
            return RAW * m + c

        def halves(c, m=0):
            return 2 * RAW * m + 2 * c

        def hi_unit(act, c, m=0):
            act.wait_ge(raw_in[slot(c)], 16 * (turn(c, m) + 1))
            if c == 0:
                act.wait_ge(narrow_in, 16)
            for s in range(2):
                g = 2 * c + s
                if g >= SPLIT:
                    act.wait_ge(halves_used, halves(c, m) + s - SPLIT + 1)
                act.copy(hi[g % SPLIT][:, :], raw[slot(c)][:, s * HALF:(s + 1) * HALF]).then_inc(hi_ready, 1)

        def lo_unit(dve, c, m=0):
            for s in range(2):
                g = 2 * c + s
                dve.wait_ge(hi_ready, halves(c, m) + s + 1)
                if g >= SPLIT:
                    dve.wait_ge(halves_used, halves(c, m) + s - SPLIT + 1)
                dve.tensor_tensor(lo[g % SPLIT][:, :], raw[slot(c)][:, s * HALF:(s + 1) * HALF],
                                  hi[g % SPLIT][:, :].bitcast(F32), ALU.subtract).then_inc(lo_ready, 1)

        def load_unit(sp, source, c, m=0):
            if c >= RAW:
                sp.wait_ge(lo_ready, halves(c - RAW + 1, m))
            n = source.shape[-1]
            sp.dma_start(raw[slot(c)][:, :].rearrange("p (k n) -> p k n", n=n),
                         source).then_inc(raw_in[slot(c)], 16)

        STRAIGHT = U_IN + RAW
        LOOPS = (NB - RAW) // RAW

        def part(w, k, n):
            return w[:, k * n:(k + 1) * n]

        def chunked(t):
            return t.rearrange("p h (c i) -> p h c i", i=CHUNK)

        upd = [bank[5][:, 0:DV], bank[4][:, 0:DV], bank[7][:, 0:DV], bank[4][:, DV:2 * DV]]

        block = ctx.enter_context(nc.Block())

        @block.sync
        def _(sp):
            sp.dma_start(resid[:, :, :], x[0].rearrange("(t p) d -> p t d", p=P)).then_inc(x_in, 16)
            sp.dma_start(mn[:, :], meta_tokens).then_inc(x_in, 16)
            sp.dma_start(g1[:, :], norm1_g[0].rearrange("(p k) -> p k", k=KD)).then_inc(x_in, 16)
            sp.wait_ge(raw_zero, 1)
            narrow = raw[0][:, :].rearrange("p (k n) -> p k n", n=P)
            sp.dma_start(narrow[:, :, 0:FH], win[:, :, FOX_COLS:FOX_COLS + FH]).then_inc(raw_in[0], 16)
            sp.dma_start(narrow[:, :, Z_AT:Z_AT + RANK],
                         win[:, :, Z_COL:Z_COL + RANK]).then_inc(narrow_in, 16)
            for c in range(U_IN, STRAIGHT):
                load_unit(sp, win[:, :, GLA_COL0 + (c - U_IN) * P:GLA_COL0 + (c - U_IN + 1) * P], c)
            with sp.Fori(0, (GLA_BLOCKS - RAW) // RAW) as i:
                for j in range(RAW):
                    c = STRAIGHT + j
                    col = GLA_COL0 + (c - U_IN) * P + RAW * P * i
                    load_unit(sp, win[:, :, bass.ds(col, P)], c, i)
            with sp.Fori(0, (NB - GLA_BLOCKS) // RAW) as i:
                for j in range(RAW):
                    c = U_IN + GLA_BLOCKS + j
                    load_unit(sp, win[:, :, bass.ds(j * P + RAW * P * i, P)], c, i)
            for n in range(D // 512):
                for q in range(D // 512):
                    load_unit(sp, wout[q * 512:(q + 1) * 512, n * 512:(n + 1) * 512]
                              .rearrange("(k p) n -> p k n", p=P), U_OUT + n * (D // 512) + q)

            def gate_or_up(w, e, c, m):
                for q in range(4):
                    load_unit(sp, w[e, q * 512:(q + 1) * 512, :].rearrange("(k p) n -> p k n", p=P), c + q, m)

            def down(e, c, m):
                for q in range(4):
                    load_unit(sp, wd[e, q * P:(q + 1) * P, :].rearrange("(k p) n -> p k n", p=P), c + q, m)

            def one_round(m):
                gate_or_up(wg, 0, U_EXP, m)
                gate_or_up(wu, 0, U_EXP + 4, m)
                with sp.Fori(1, E) as e:
                    gate_or_up(wg, e, U_STEP, 2 * e - 2 + m)
                    down(e - 1, U_STEP + 4, 2 * e - 2 + m)
                    gate_or_up(wu, e, U_STEP + 8, 2 * e - 2 + m)
                down(E - 1, U_STEP, 2 * (E - 1) + m)

            one_round(0)
            sp.wait_ge(routed, 1)
            n_rounds = sp.value_load(nrounds[0:1, 0:1], min_val=1, max_val=SEQ // SLOTS)
            with sp.If(n_rounds > 1):
                with sp.Fori(1, n_rounds) as r:
                    one_round(2 * E * r)
            sp.wait_ge(scattered, 16 * E * n_rounds)
            rows = scratch[:, :].rearrange("(k t p) d -> p t k d", k=2, p=P)
            for t in range(TT):
                for k in range(2):
                    sp.dma_start(yk[:, t, k, :], rows[:, t, k, :]).then_inc(yk_in[t], 16)
            out_rows = out[0].rearrange("(t p) d -> p t d", p=P)
            for t in range(TT):
                for s in range(2):
                    cols = slice(s * D // 2, (s + 1) * D // 2)
                    sp.wait_ge(out_ready, 2 * t + s + 1)
                    sp.dma_start(out_rows[:, t, cols], u2[:, t, cols]).then_inc(stored, 16)
            sp.wait_ge(stored, 16 * TT * 2)

        @block.gpsimd
        def _(pool):
            pool.memset(ones[:, :], 1.0).then_inc(masks_ready, 1)
            pool.wait_ge(masks_ready, 1)
            pool.affine_select(out=ident[:, :], in_=ones[:, 0:P], pattern=[[1, P]], compare_op=ALU.is_equal,
                               fill=0.0, base=0, channel_multiplier=-1).then_inc(masks_ready, 1)
            pool.affine_select(out=above[:, :], in_=ones[:, 0:P], pattern=[[1, P]], compare_op=ALU.is_gt,
                               fill=0.0, base=0, channel_multiplier=-1).then_inc(masks_ready, 1)
            pool.affine_select(out=chunkm[:, :], in_=ones[:, 0:P], pattern=[[1, P]], compare_op=ALU.is_ge,
                               fill=0.0, base=0, channel_multiplier=-1).then_inc(masks_ready, 1)
            pool.wait_ge(masks_ready, 4)
            pool.memset(chunkm[0:CHUNK, CHUNK:P], 0.0).then_inc(masks_ready, 1)
            pool.iota(count[:, :], [[1, CHUNK + 1]], base=0, channel_multiplier=0,
                      allow_small_or_imprecise_dtypes=True).then_inc(masks_ready, 1)
            pool.iota(rowno[:, :], [[0, 1]], base=0, channel_multiplier=1,
                      allow_small_or_imprecise_dtypes=True).then_inc(masks_ready, 1)
            for dst, src in ((gbias[:, :], gla_b_gate[0].rearrange("(h p) -> p h", p=P)),
                             (ggain[:, :], gla_norm_g[0].rearrange("(h p) -> p h", p=P)),
                             (fgain[:, :], fox_norm_g[0].rearrange("(p a) -> p a", a=1)),
                             (wgate2[:, :], gla_w_gate2[0]),
                             (fbias[:, :], b_fox_f[0].rearrange("(p a) -> p a", a=1))):
                pool.dma_start(dst, src, allow_slow_non_contiguous=True).then_inc(params_in, 16)
            pool.dma_start(wr[:, :, 0:G], w_router_group[0].rearrange("(k p) n -> p k n", p=P)).then_inc(routers_in, 16)
            for g in range(G):
                pool.dma_start(wr[:, :, G + g * E8:G + (g + 1) * E8],
                               w_router_expert[0, g].rearrange("(k p) n -> p k n", p=P)).then_inc(routers_in, 16)
            pool.dma_start(br[:, 0:G], b_router_group[0:1, :].broadcast_to([P, G])).then_inc(routers_in, 16)
            pool.dma_start(br[:, G:G + E], b_router_expert[0].rearrange("(a g) e -> a (g e)", a=1)
                           .broadcast_to([P, E])).then_inc(routers_in, 16)
            pool.wait_ge(halves_used, halves(U_OUT))
            pool.memset(sel[:, :, :], 1.0).then_inc(heads_consts, 1)
            pool.memset(reset[:, :], 1.0).then_inc(heads_consts, 1)
            pool.memset(a2[0][:, :, :], 0.0).then_inc(heads_consts, 1)
            pool.memset(a2[1][:, :, :], 0.0).then_inc(heads_consts, 1)
            pool.wait_ge(heads_consts, 4)
            pool.affine_select(out=sel[:, :, :], in_=sel[:, :, :], pattern=[[1, FH], [0, P]],
                               compare_op=ALU.is_equal, fill=0.0, base=0,
                               channel_multiplier=-1).then_inc(heads_consts, 1)
            pool.memset(reset[:, 0:1], 0.0).then_inc(heads_consts, 1)
            for n in range(NCH):
                pool.memset(reset[:, META + n * CHUNK:META + n * CHUNK + 1], 0.0).then_inc(heads_consts, 1)
            pool.wait_ge(rms_ready, 1)
            for h in range(FH):
                for t in range(TT):
                    i = TT * (GH + h) + t
                    o = proj[:, FQ + h, t * P:(t + 1) * P]
                    pool.tensor_scalar(o, o, rms[:, i:i + 1], None, ALU.mult).then_inc(on_p, 1)
            pool.wait_ge(mixl_ready, KD)
            pool.dma_start(g2b[:, :], norm2_g[0:1, :].broadcast_to([P, D])).then_inc(routers_in, 16)
            pool.memset(rt["gp"][:, :, :], LOWEST).then_inc(masks_ready, 1)
            pool.memset(key[:, :, E:E + 1], 0.0).then_inc(masks_ready, 1)
            pool.memset(rowid[:, :, E:E + 1], 0.0).then_inc(masks_ready, 1)
            pool.memset(nil[:, :], 0).then_inc(masks_ready, 1)
            for i in range(4):
                pool.memset(limit[:, i:i + 1], float(SLOTS * i)).then_inc(masks_ready, 1)
            pool.wait_ge(u2_ready, TT * (D // 512))
            pool.dma_start(gfb[:, :], norm_f_g.rearrange("(a d) -> a d", a=1).broadcast_to([P, D])).then_inc(routers_in, 16)
            pool.wait_ge(routed, 1)
            n_rounds = pool.value_load(nrounds[0:1, 0:1], min_val=1, max_val=SEQ // SLOTS)

            def named(n):
                pool.wait_ge(idn_ready, n + 1)
                pool.tensor_tensor(idx[:, :], idn[:, :], nil[:, :], ALU.add).then_inc(idx_ready, 1)

            def scatter(n):
                pool.wait_ge(y_ready, 4 * n + 4)
                pool.wait_ge(idx_ready, n + 1)
                pool.sem_inc(scatters, 1)
                pool.indirect_dma_start(scratch[:, :], bass.IndirectOffsetOnAxis(ap=idx[:, 0:1], axis=0),
                                        yrow[:, :], None, bounds_check=2 * SEQ - 1,
                                        oob_is_err=False).then_inc(scattered, 16)
                pool.wait_ge(scattered, 16 * n + 16)

            with pool.Fori(0, n_rounds) as r:
                named(E * r)
                with pool.Fori(1, E) as e:
                    scatter(E * r + e - 1)
                    named(E * r + e)
                scatter(E * r + E - 1)

        @block.scalar
        def _(act):
            steps = [0]

            def own(ins):
                steps[0] += 1
                ins.then_inc(act_step, 1)
                act.wait_ge(act_step, steps[0])

            def root(n, src, dst):
                act.wait_ge(root_in, n)
                act.activation(dst, src, ACT.Sqrt).then_inc(root_out, 1)

            act.wait_ge(x_in, 48)
            act.wait_ge(stat_zero, 1)
            for t in range(TT):
                own(act.activation(xjunk[:, :], resid[:, t, :], ACT.Square, accum_out=stat[:, t:t + 1]))
            act.activation(xjunk[0:META, :], mn[:, :], ACT.Square, accum_out=stat[0:META, TT:TT + 1]).then_inc(sums_ready, 1)
            root(1, stat2[:, 0:TT + 1], stat[:, 0:TT + 1])
            hi_unit(act, 0)
            for k in range(KD):
                act.wait_ge(xt_ready, k + 1)
                act.activation(uh[:, k, :], bank[k % 4][:, 0:L], ACT.Copy,
                               scale=g1[:, k:k + 1]).then_inc(uh_ready, 1)
            hi_unit(act, 1)

            def proj_copy(c, m=0):
                act.wait_ge(halves_used, halves(c + 1, m))
                act.copy(proj[:, c - U_IN + RAW * m, :] if isinstance(m, int) else
                         proj[:, bass.ds(c - U_IN + RAW * m, 1), :].rearrange("p a l -> p (a l)"),
                         bank[c % 2][:, 0:L]).then_inc(proj_out, 1)

            for c in range(2, STRAIGHT):
                if c - 2 >= U_IN:
                    proj_copy(c - 2)
                hi_unit(act, c)
            with act.Fori(0, LOOPS) as i:
                for j in range(RAW):
                    proj_copy(STRAIGHT + j - 2, i)
                    hi_unit(act, STRAIGHT + j, i)
            for c in (U_OUT, U_OUT + 1):
                proj_copy(c - 2)
                hi_unit(act, c)

            act.wait_ge(fgate_d, 1)
            own(act.activation(ct[:, 1, :], ct[:, 1, :], ACT.Exp, scale=-1.0))
            act.activation(ct[:, 1, :], ct[:, 1, :], ACT.Ln, bias=1.0).then_inc(fgate_a, 1)
            act.wait_ge(proj_out, NB)
            r_all = proj[:, GR:GR + GH * VH, META:L]
            act.activation(r_all, r_all, ACT.Silu).then_inc(silu_ready, 1)
            act.wait_ge(gate_d, 1)
            own(act.activation(gt[1][:, :, :], gt[1][:, :, :], ACT.Exp, scale=-1.0))
            act.activation(gt[1][:, :, :], gt[1][:, :, :], ACT.Ln, bias=1.0).then_inc(gate_a, 1)
            act.wait_ge(gate_d, 2)
            act.activation(gt[3][:, :, :], gt[2][:, :, :], ACT.Exp, scale=1.0 / GLA_TAU).then_inc(gate_a, 1)
            act.activation(dec[:, :, :], gt[2][:, :, META + CHUNK - 1::CHUNK], ACT.Exp,
                           scale=1.0 / GLA_TAU).then_inc(gate_a, 1)
            act.wait_ge(gate_d, 3)
            act.activation(gt[0][:, :, :], gt[0][:, :, :], ACT.Exp, scale=1.0 / GLA_TAU).then_inc(gate_a, 1)
            act.wait_ge(gate_d, 4)
            act.activation(gt[2][:, :, META:L], gt[0][:, :, META:L], ACT.Exp, scale=1.0 / GLA_TAU).then_inc(gate_a, 1)
            act.wait_ge(gate_a, 5)
            act.activation(gt[0][:, :, META:L], gt[0][:, :, META:L], ACT.Exp, scale=-1.0 / GLA_TAU).then_inc(gate_a, 1)

            def gla_v(h):
                act.wait_ge(kv_t, h + 1)
                if h:
                    act.wait_ge(o_g, h)
                own(act.copy(vn[0:META, 0, :], bank[2][0:META, 0:DV]))
                own(act.copy(vn[:, 1, :], bank[2][:, DV:2 * DV]))
                act.copy(vn[:, 2, :], bank[3][:, 0:DV]).then_inc(v_ready, 1)

            def gla_out(h):
                act.wait_ge(o_g, h + 1)
                o = proj[:, GV + VH * h:GV + VH * (h + 1), :].rearrange("p a l -> p (a l)")
                own(act.copy(o[:, 0:TT * DV], bank[6][:, :]))
                for t in range(TT):
                    ins = act.activation(junk[:, :], bank[6][:, t * DV:(t + 1) * DV], ACT.Square,
                                         accum_out=ss[:, TT * h + t:TT * h + t + 1])
                    if t < TT - 1:
                        own(ins)
                ins.then_inc(o_gout, 1)
                act.wait_ge(o_gout, h + 1)

            for h in range(GH + 1):
                if h < GH:
                    gla_v(h)
                if h:
                    gla_out(h - 1)

            def fox_exp(h):
                act.wait_ge(bias_f, h + 1)
                if h:
                    act.wait_ge(p_t, h)
                for t in range(TT):
                    w = META + (t + 1) * P
                    ins = act.activation(pr[:, t, 0:w], bank[2 + t][:, 0:w], ACT.Exp, bias=rs[:, h, 4 + t:5 + t],
                                         accum_out=rs[:, h, 6 + t:7 + t])
                ins.then_inc(p_ready, 1)

            def fox_v(h):
                act.wait_ge(vf_t, h + 1)
                if h >= 2:
                    act.wait_ge(o_f, h - 1)
                own(act.copy(vf[h % 2][0:META, 0, :], bank[6][0:META, 0:HD]))
                act.copy(vf[h % 2][:, 1:3, :].rearrange("p a b -> p (a b)"), bank[6][:, HD:3 * HD]).then_inc(vf_ready, 1)

            def fox_pt(h):
                act.wait_ge(p_t, h + 1)
                if h:
                    act.wait_ge(o_f, h)
                act.copy(pt[:, :, :].rearrange("p a b -> p (a b)"), bank[4][:, 0:3 * P]).then_inc(pt_a, 1)

            def fox_sq(h):
                act.wait_ge(o_fout, h + 1)
                for t in range(TT):
                    i = TT * (GH + h) + t
                    ins = act.activation(junk[:, 0:HD], proj[:, FQ + h, t * P:(t + 1) * P], ACT.Square,
                                         accum_out=ss[:, i:i + 1])
                    if t < TT - 1:
                        own(ins)
                ins.then_inc(sq_f, 1)
                act.wait_ge(sq_f, h + 1)

            for s in range(FH + 2):
                if s < FH:
                    fox_exp(s)
                    fox_v(s)
                if 1 <= s <= FH:
                    fox_pt(s - 1)
                if s >= 2:
                    fox_sq(s - 2)

            root(2, ss[:, :], rms[:, :])
            for k in range(KD):
                if k < GH * VH:
                    act.wait_ge(mix_f, k + 1)
                    act.copy(mixh[:, k, :], mtmp[k % 2][:, :]).then_inc(mixh_ready, 1)
                else:
                    act.wait_ge(mix_t, k + 1)
                    act.activation(mixh[:, k, :], bank[k % 4][:, 0:SEQ], ACT.Copy,
                                   scale=fgain[:, 0:1]).then_inc(mixh_ready, 1)

            def squares(n):
                act.wait_ge(resid_ready, n + 1)
                for t in range(TT):
                    ins = act.activation(u2[:, t, 512 * n:512 * (n + 1)], resid[:, t, 512 * n:512 * (n + 1)],
                                         ACT.Square, accum_out=sq2[:, t, n:n + 1])
                ins.then_inc(quarters_sq, 1)

            for c in range(U_OUT + 2, U_EXP):
                hi_unit(act, c)
                if (c - U_OUT) % 4 == 2 and c - U_OUT > 4:
                    squares((c - U_OUT) // 4 - 1)
            squares(D // 512 - 1)

            root(3, stat2[:, 0:TT], stat[:, 0:TT])
            for i in range(KD // 2):
                act.wait_ge(u2_t, i + 1)
                act.copy(u2t[:, 2 * i:2 * i + 2, :].rearrange("p k l -> p (k l)"), bank[i % 4][:, :]).then_inc(u2t_a, 1)
                if i % 4 == 3:
                    t = i // 4
                    act.wait_ge(u2_ready, TT * (D // 512))
                    act.copy(u2h[:, t, :], u2[:, t, :]).then_inc(u2h_ready, 1)
            act.wait_ge(route_d, 1)
            for t in range(TT):
                ins = act.activation(rt["ge"][:, t, :], rt["gp"][:, t, :], ACT.Exp, bias=esum[:, t:t + 1],
                                     accum_out=esum[:, 2 + t:3 + t])
            ins.then_inc(route_a, 1)
            act.wait_ge(route_d, 2)
            for t in range(TT):
                ins = act.activation(rt["pe"][:, t, :], rt["sel8"][:, t, :], ACT.Exp, bias=esum[:, 4 + t:5 + t],
                                     accum_out=esum[:, 6 + t:7 + t])
            ins.then_inc(route_a, 1)

            def picked_rows(q, before, b=6):
                act.wait_ge(xg_mm, before + q + 1)
                act.copy(xg[:, :], bank[b][:, :]).then_inc(xg_ready, 1)

            def gathered(q, before):
                act.wait_ge(xs_t, before + q + 1)
                act.copy(xs[:, 4 * q:4 * q + 4, :].rearrange("p k s -> p (k s)"),
                         bank[7][:, :]).then_inc(xs_ready, 1)

            def result_lo(n):
                for q in range(4):
                    act.copy(ylo[:, 512 * q:512 * (q + 1)], bank[2 + q][SLOTS:P, :]).then_inc(ylo_ready, 1)

            def gate_lo(n):
                act.copy(glo[:, :], bank[0][SLOTS:P, :]).then_inc(glo_ready, 1)

            def gate_silu(n):
                act.wait_ge(gsum_ready, n + 1)
                act.activation(glo[:, :], gsum[:, :], ACT.Silu).then_inc(silu_e, 1)

            def up_lo(n):
                act.copy(ulo[:, :], bank[1][SLOTS:P, :]).then_inc(ulo_ready, 1)

            def hidden_hi(n):
                act.wait_ge(h_t, n + 1)
                act.copy(hs[:, :, 0:SLOTS], bank[1][:, 0:FE // P * SLOTS]
                         .rearrange("p (k s) -> p k s", s=SLOTS)).then_inc(hsh_ready, 1)

            act.wait_ge(routed, 1)
            n_rounds = act.value_load(nrounds[0:1, 0:1], min_val=1, max_val=SEQ // SLOTS)
            with act.Fori(0, n_rounds) as r:
                gathers = 4 * (E + 1) * r
                m = 2 * E * r
                for j in range(8):
                    hi_unit(act, U_EXP + j, m)
                    if j < 3:
                        picked_rows(j, gathers, 2 + j)
                        gathered(j, gathers)
                    if j == 2:
                        picked_rows(3, gathers, 5)
                        gathered(3, gathers)
                    if j == 5:
                        act.wait_ge(halves_used, halves(U_EXP + 4, m))
                        gate_lo(E * r)
                        picked_rows(0, gathers + 4)
                    if j == 6:
                        gate_silu(E * r)
                        gathered(0, gathers + 4)
                        picked_rows(1, gathers + 4)
                    if j == 7:
                        gathered(1, gathers + 4)
                        picked_rows(2, gathers + 4)
                with act.Fori(1, E) as e:
                    n = E * r + e
                    m = 2 * n - 2
                    before = 4 * (n + r)
                    for j in range(PER):
                        hi_unit(act, U_STEP + j, m)
                        if j == 0:
                            gathered(2, before)
                            picked_rows(3, before)
                        if j == 1:
                            act.wait_ge(halves_used, halves(U_STEP, m))
                            up_lo(n - 1)
                            gathered(3, before)
                        if j == 3:
                            hidden_hi(n - 1)
                        if j == 5:
                            act.wait_ge(halves_used, halves(U_STEP + 4, m))
                            gate_lo(n)
                        if j == 6:
                            gate_silu(n)
                        if j == 9:
                            act.wait_ge(halves_used, halves(U_STEP + 8, m))
                            picked_rows(0, before + 4)
                            result_lo(n - 1)
                        if j == 10:
                            gathered(0, before + 4)
                            picked_rows(1, before + 4)
                        if j == 11:
                            gathered(1, before + 4)
                            picked_rows(2, before + 4)
                            act.wait_ge(y_ready, 4 * n)
                m = 2 * E * r + 2 * E - 2
                for j in range(4):
                    hi_unit(act, U_STEP + j, m)
                    if j == 1:
                        act.wait_ge(halves_used, halves(U_STEP, m))
                        up_lo(E * r + E - 1)
                        gathered(2, gathers + 4 * E)
                        picked_rows(3, gathers + 4 * E)
                        gathered(3, gathers + 4 * E)
                        hidden_hi(E * r + E - 1)
                act.wait_ge(halves_used, halves(U_STEP + 4, m))
                result_lo(E * r + E - 1)
                act.wait_ge(y_ready, 4 * E * r + 4 * E)
            for t in range(TT):
                for s in range(2):
                    cols = slice(s * D // 2, (s + 1) * D // 2)
                    act.wait_ge(summed, 2 * t + s + 1)
                    act.activation(u2[:, t, cols], resid[:, t, cols], ACT.Square,
                                   accum_out=sq2[:, t, s:s + 1]).then_inc(sums_ready, 1)
                root(4 + t, stat2[:, t:t + 1], stat[:, 2 + t:3 + t])

        @block.vector
        def _(dve):
            steps = [0]

            def own(ins):
                steps[0] += 1
                ins.then_inc(dve_step, 1)
                dve.wait_ge(dve_step, steps[0])

            def mean_eps(dst, src, n):
                dve.tensor_scalar(dst, src, 1.0 / n, EPS, ALU.mult, ALU.add).then_inc(root_in, 1)

            dve.memset(stat[:, :], 0.0).then_inc(stat_zero, 1)
            dve.memset(raw[0][:, :], 0.0).then_inc(raw_zero, 1)
            dve.wait_ge(sums_ready, 1)
            mean_eps(stat2[:, 0:TT + 1], stat[:, 0:TT + 1], D)
            dve.wait_ge(root_out, 1)
            own(dve.reciprocal(stat2[:, 0:TT + 1], stat[:, 0:TT + 1]))
            for t in range(TT):
                dve.tensor_scalar(xn[:, t, :], resid[:, t, :], stat2[:, t:t + 1], None, ALU.mult).then_inc(xn_ready, 1)
            dve.tensor_scalar(mn[:, :], mn[:, :], stat2[0:META, TT:TT + 1], None, ALU.mult).then_inc(xn_ready, 1)
            lo_unit(dve, 0)
            for k in range(KD):
                dve.wait_ge(uh_ready, k + 1)
                dve.scalar_tensor_tensor(out=ul[:, k, :], in0=bank[k % 4][:, 0:L], scalar=g1[:, k:k + 1],
                                         in1=uh[:, k, :].bitcast(F32), op0=ALU.mult,
                                         op1=ALU.subtract).then_inc(ul_ready, 1)
            for c in range(1, STRAIGHT):
                lo_unit(dve, c)
            with dve.Fori(0, LOOPS) as i:
                for j in range(RAW):
                    lo_unit(dve, STRAIGHT + j, i)
            for c in (U_OUT, U_OUT + 1):
                lo_unit(dve, c)

            dve.wait_ge(params_in, 16 * 5)
            dve.wait_ge(halves_used, halves(U_OUT))
            dve.wait_ge(proj_out, NB)
            dve.tensor_copy(zt[:, :], bank[7][Z_AT:Z_AT + RANK, 0:L]).then_inc(z_ready, 1)
            own(dve.tensor_scalar(ct[:, 0, :], bank[7][0:FH, 0:L], fbias[:, 0:1], None, ALU.add))
            own(dve.scalar_tensor_tensor(out=ct[:, 1, :], in0=ct[:, 0, :], scalar=-1.0, in1=ct[:, 0, :],
                                         op0=ALU.mult, op1=ALU.max))
            dve.tensor_scalar(ct[:, 0, :], ct[:, 0, :], 0.0, None, ALU.min).then_inc(fgate_d, 1)
            dve.wait_ge(gates_mm, 1)
            for h in range(GH):
                ins = dve.tensor_scalar(gt[0][:, h, :], bank[2 + h][:, 0:L], gbias[:, h:h + 1], None, ALU.add)
                if h < GH - 1:
                    ins.then_inc(dve_step, 1)
                    steps[0] += 1
                else:
                    own(ins)
            own(dve.scalar_tensor_tensor(out=gt[1][:, :, :], in0=gt[0][:, :, :], scalar=-1.0, in1=gt[0][:, :, :],
                                         op0=ALU.mult, op1=ALU.max))
            dve.tensor_scalar(gt[0][:, :, :], gt[0][:, :, :], 0.0, None, ALU.min).then_inc(gate_d, 1)
            dve.wait_ge(fgate_d, 1)
            dve.wait_ge(fgate_a, 1)
            own(dve.tensor_tensor(ct[:, 0, :], ct[:, 0, :], ct[:, 1, :], ALU.subtract))
            own(dve.tensor_tensor_scan(ct[:, 2, :], ones[0:FH, :], ct[:, 0, :], 0.0, ALU.mult, ALU.add))
            dve.tensor_scalar(ct[:, 3, :], ct[:, 2, :], -1.0, None, ALU.mult).then_inc(fgate_d, 1)
            dve.wait_ge(gate_d, 1)
            dve.wait_ge(gate_a, 1)
            own(dve.tensor_tensor(gt[0][:, :, :], gt[0][:, :, :], gt[1][:, :, :], ALU.subtract))
            dve.wait_ge(heads_consts, 6 + NCH)
            for h in range(GH):
                ins = dve.tensor_tensor_scan(gt[2][:, h, :], reset[:, :], gt[0][:, h, :], 0.0, ALU.mult, ALU.add)
                if h < GH - 1:
                    ins.then_inc(dve_step, 1)
                    steps[0] += 1
            ins.then_inc(gate_d, 1)
            dve.wait_ge(gate_d, 2)
            b_x = chunked(gt[2][:, :, META:L])
            d_x = chunked(gt[0][:, :, META:L])
            wide = [P, GH, NCH, CHUNK]
            dve.tensor_tensor(d_x, b_x[:, :, :, CHUNK - 1:CHUNK].broadcast_to(wide), b_x, ALU.subtract)\
               .then_inc(dve_step, 1)
            steps[0] += 1
            dve.tensor_tensor(gt[0][:, :, 0:META], gt[2][:, :, META - 1:META].broadcast_to([P, GH, META]),
                              gt[2][:, :, 0:META], ALU.subtract).then_inc(gate_d, 1)
            dve.wait_ge(gate_a, 2)
            own(dve.scalar_tensor_tensor(out=gt[3][:, :, :], in0=proj[:, GQ:GQ + GH, :], scalar=QSCALE,
                                         in1=gt[3][:, :, :], op0=ALU.mult, op1=ALU.mult))
            dve.wait_ge(gate_a, 4)
            own(dve.tensor_tensor(gt[1][:, :, :], proj[:, GK:GK + GH, :], gt[0][:, :, :], ALU.mult))
            dve.tensor_tensor(d_x, b_x, b_x[:, :, :, CHUNK // 2:CHUNK // 2 + 1].broadcast_to(wide),
                              ALU.subtract).then_inc(gate_d, 1)
            dve.wait_ge(gate_a, 5)
            q_x, k_x = proj[:, GQ:GQ + GH, META:L], proj[:, GK:GK + GH, META:L]
            dve.scalar_tensor_tensor(out=q_x, in0=q_x, scalar=QSCALE, in1=gt[2][:, :, META:L], op0=ALU.mult,
                                     op1=ALU.mult).then_inc(dve_step, 1)
            steps[0] += 1
            dve.wait_ge(gate_a, 6)
            dve.tensor_tensor(k_x, k_x, gt[0][:, :, META:L], ALU.mult).then_inc(gla_ops, 1)
            dve.wait_ge(fgate_t, 1)
            dve.tensor_copy(cq[:, :, :].rearrange("p t h -> p (t h)"), bank[6][:, 0:TT * FH]).then_inc(cq_ready, 1)

            def gla_masked(h):
                dve.wait_ge(scores_g, h + 1)
                if h >= 2:
                    dve.wait_ge(o_g, h - 1)
                for t in range(TT):
                    ins = dve.copy_predicated(a2[h % 2][:, t, :], chunkm[:, :].bitcast(U32),
                                              bank[0][:, t * P:(t + 1) * P])
                    if t < TT - 1:
                        ins.then_inc(dve_step, 1)
                        steps[0] += 1
                ins.then_inc(a_ready, 1)

            def gla_k(h):
                dve.wait_ge(kv_t, h + 1)
                if h:
                    dve.wait_ge(upd_g, h)
                own(dve.tensor_copy(kln[0:META, 0, :], bank[1][0:META, 0:P]))
                dve.tensor_copy(kln[:, 1:3, :].rearrange("p a b -> p (a b)"), bank[1][:, P:3 * P]).then_inc(k_ready, 1)

            def gla_states(h):
                dve.wait_ge(upd_g, h + 1)
                if h:
                    dve.wait_ge(o_g, h)
                own(dve.tensor_copy(st[:, 0, :], upd[0]))
                for n in range(1, NCH):
                    ins = dve.scalar_tensor_tensor(
                        out=st[:, n, :], in0=st[:, n - 1, :], scalar=dec[:, h, n - 1:n],
                        in1=upd[n], op0=ALU.mult, op1=ALU.add)
                    if n < NCH - 1:
                        own(ins)
                ins.then_inc(st_ready, 1)

            for h in range(GH):
                gla_masked(h)
                gla_k(h)
                gla_states(h)

            def fox_q(h):
                if h >= 2:
                    dve.wait_ge(scores_f, h - 1)
                dve.tensor_scalar(qs[h % 2][:, :], proj[:, FQ + h, META:L], QSCALE, None, ALU.mult).then_inc(q_ready, 1)

            def fox_mask(h):
                dve.wait_ge(scores_f, h + 1)
                for t in range(TT):
                    own(dve.copy_predicated(bank[2 + t][:, META + t * P:META + (t + 1) * P],
                                            above[:, :].bitcast(U32), lowest[:, :]))
                    own(dve.tensor_reduce(rs[:, h, t:t + 1], bank[2 + t][:, 0:META + (t + 1) * P], AX, ALU.max))
                own(dve.tensor_tensor(rs[:, h, 2:4], rs[:, h, 0:2], cq[:, :, h], ALU.add))
                dve.tensor_tensor(rs[:, h, 4:6], cq[:, :, h], rs[:, h, 2:4], ALU.subtract).then_inc(bias_f, 1)

            def fox_pt_meta(h):
                dve.wait_ge(p_t, h + 1)
                if h:
                    dve.wait_ge(o_f, h)
                dve.tensor_copy(ptm[:, :, :].rearrange("p a b -> p (a b)"), bank[5][0:META, 0:TT * P]).then_inc(pt_d, 1)

            def fox_out(h):
                dve.wait_ge(o_f, h + 1)
                dve.wait_ge(p_ready, h + 1)
                own(dve.reciprocal(rs[:, h, 0:2], rs[:, h, 6:8]))
                for t in range(TT):
                    ins = dve.tensor_scalar(proj[:, FQ + h, t * P:(t + 1) * P], bank[7][:, t * HD:(t + 1) * HD],
                                            rs[:, h, t:t + 1], None, ALU.mult)
                    if t < TT - 1:
                        ins.then_inc(dve_step, 1)
                        steps[0] += 1
                ins.then_inc(o_fout, 1)

            own(dve.memset(lowest[:, :], LOWEST))
            fox_q(0)
            for s in range(FH + 2):
                if s + 1 < FH:
                    fox_q(s + 1)
                if s < FH:
                    fox_mask(s)
                if 1 <= s <= FH:
                    fox_pt_meta(s - 1)
                if s >= 2:
                    fox_out(s - 2)

            dve.wait_ge(o_gout, GH)
            dve.wait_ge(sq_f, FH)
            own(dve.tensor_scalar(ss[:, 0:TT * GH], ss[:, 0:TT * GH], 1.0 / DV, EPS, ALU.mult, ALU.add))
            mean_eps(ss[:, TT * GH:], ss[:, TT * GH:], HD)
            dve.wait_ge(root_out, 2)
            dve.reciprocal(rms[:, :], rms[:, :]).then_inc(rms_ready, 1)
            dve.wait_ge(rms_ready, 1)
            for h in range(GH):
                o = proj[:, GV + VH * h:GV + VH * (h + 1), :].rearrange("p a l -> p (a l)")
                for t in range(TT):
                    dve.tensor_scalar(o[:, t * DV:(t + 1) * DV], o[:, t * DV:(t + 1) * DV],
                                      rms[:, TT * h + t:TT * h + t + 1], None, ALU.mult).then_inc(on_d, 1)
            dve.wait_ge(silu_ready, 1)

            def gated(k):
                dve.wait_ge(mix_t, k + 1)
                if k >= 2:
                    dve.wait_ge(mixl_ready, k - 1)
                dve.scalar_tensor_tensor(out=mtmp[k % 2][:, :], in0=bank[k % 4][:, 0:SEQ],
                                         scalar=ggain[:, k % VH:k % VH + 1], in1=proj[:, GR + k, META:L],
                                         op0=ALU.mult, op1=ALU.mult).then_inc(mix_f, 1)

            gated(0)
            for k in range(KD):
                if k + 1 < GH * VH:
                    gated(k + 1)
                dve.wait_ge(mixh_ready, k + 1)
                if k < GH * VH:
                    dve.wait_ge(mix_f, k + 1)
                    dve.tensor_tensor(mixl[:, k, :], mtmp[k % 2][:, :], mixh[:, k, :].bitcast(F32),
                                      ALU.subtract).then_inc(mixl_ready, 1)
                else:
                    dve.scalar_tensor_tensor(out=mixl[:, k, :], in0=bank[k % 4][:, 0:SEQ], scalar=fgain[:, 0:1],
                                             in1=mixh[:, k, :].bitcast(F32), op0=ALU.mult,
                                             op1=ALU.subtract).then_inc(mixl_ready, 1)

            def residual(n):
                dve.wait_ge(halves_used, halves(U_OUT + (D // 512) * (n + 1)))
                for t in range(TT):
                    r = resid[:, t, 512 * n:512 * (n + 1)]
                    ins = dve.tensor_tensor(r, bank[2 * (n % 2) + t][:, :], r, ALU.add)
                    if t < TT - 1:
                        ins.then_inc(dve_step, 1)
                        steps[0] += 1
                ins.then_inc(resid_ready, 1)

            for c in range(U_OUT + 2, U_EXP):
                lo_unit(dve, c)
                if (c - U_OUT) % 4 == 1 and c - U_OUT > 4:
                    residual((c - U_OUT) // 4 - 1)
            residual(D // 512 - 1)

            dve.wait_ge(quarters_sq, D // 512)
            own(dve.tensor_reduce(stat[:, 0:TT], sq2[:, :, :], AX, ALU.add))
            mean_eps(stat2[:, 0:TT], stat[:, 0:TT], D)
            dve.wait_ge(root_out, 3)
            own(dve.reciprocal(stat2[:, 0:TT], stat[:, 0:TT]))
            dve.wait_ge(routers_in, 16 * (G + 4))
            for n in range(D // 512):
                s = slice(512 * n, 512 * (n + 1))
                for t in range(TT):
                    dve.scalar_tensor_tensor(out=u2[:, t, s], in0=resid[:, t, s], scalar=stat2[:, t:t + 1],
                                             in1=g2b[:, s], op0=ALU.mult, op1=ALU.mult).then_inc(u2_ready, 1)
            for t in range(TT):
                dve.wait_ge(u2h_ready, t + 1)
                dve.wait_ge(u2_ready, TT * (D // 512))
                dve.tensor_tensor(u2l[:, t, :], u2[:, t, :], u2h[:, t, :].bitcast(F32),
                                  ALU.subtract).then_inc(u2l_ready, 1)

            dve.wait_ge(masks_ready, 7)
            for first in (0, 2 * SLOTS):
                own(dve.tensor_scalar(pick[:, :, first:first + SLOTS], count[:, None, 0:SLOTS].broadcast_to([P, TT, SLOTS]),
                                      0.0, None, ALU.mult))

            dve.wait_ge(logits, 1)
            dve.wait_ge(masks_ready, 15)
            lg = rt["lg"]
            for t in range(TT):
                own(dve.tensor_tensor(lg[:, t, :], bank[4 + t][:, 0:G + E], br[:, :], ALU.add))
            own(dve.tensor_copy(rt["gp"][:, :, 0:G], lg[:, :, 0:G]))
            for t in range(TT):
                own(dve.max(rt["gm"][:, t, :], rt["gp"][:, t, :]))
                own(dve.max_index(gix[:, t, :], rt["gm"][:, t, :], rt["gp"][:, t, :]))
            dve.tensor_scalar(esum[:, 0:TT], rt["gm"][:, :, 0], -1.0, None, ALU.mult).then_inc(route_d, 1)
            own(dve.tensor_copy(rt["gi"][:, :, :], gix[:, :, :]))
            own(dve.tensor_tensor(rt["oh"][:, :, :], count[:, None, 0:G].broadcast_to([P, TT, G]),
                                  rt["gi"][:, :, 0:1].broadcast_to([P, TT, G]), ALU.is_equal))
            own(dve.tensor_tensor(rt["t32"][:, :, :].rearrange("p t (g e) -> p t g e", g=G),
                                  lg[:, :, G:].rearrange("p t (g e) -> p t g e", g=G),
                                  rt["oh"][:, :, :, None].broadcast_to([P, TT, G, E8]), ALU.mult))
            own(dve.tensor_reduce(rt["sel8"][:, :, :], rt["t32"][:, :, :].rearrange("p t (g e) -> p t e g", g=G),
                                  AX, ALU.add))
            own(dve.tensor_reduce(esum[:, 8:10], rt["sel8"][:, :, :], AX, ALU.max))
            dve.tensor_scalar(esum[:, 4:6], esum[:, 8:10], -1.0, None, ALU.mult).then_inc(route_d, 1)
            dve.wait_ge(route_a, 2)
            own(dve.reciprocal(esum[:, 10:12], esum[:, 2:4]))
            own(dve.reciprocal(esum[:, 12:14], esum[:, 6:8]))
            own(dve.tensor_tensor(rt["pe"][:, :, :], rt["pe"][:, :, :],
                                  esum[:, 12:14][:, :, None].broadcast_to([P, TT, 8]), ALU.mult))
            for t in range(TT):
                own(dve.max(rt["top"][:, t, :], rt["pe"][:, t, :]))
                own(dve.max_index(tix[:, t, :], rt["top"][:, t, :], rt["pe"][:, t, :]))
            own(dve.tensor_copy(rt["ti"][:, :, :], tix[:, :, :]))
            own(dve.scalar_tensor_tensor(out=rt["eid"][:, :, :], in0=rt["gi"][:, :, 0:1].broadcast_to([P, TT, 2]),
                                         scalar=float(E8), in1=rt["ti"][:, :, 0:2], op0=ALU.mult, op1=ALU.add))
            for k in range(2):
                ins = dve.tensor_tensor(rt[f"m{k}"][:, :, :], count[:, None, 0:E].broadcast_to([P, TT, E]),
                                        rt["eid"][:, :, k:k + 1].broadcast_to([P, TT, E]), ALU.is_equal)
                if k == 0:
                    ins.then_inc(dve_step, 1)
                    steps[0] += 1
            own(ins)
            dve.tensor_tensor(rt["mm"][:, :, :], rt["m0"][:, :, :], rt["m1"][:, :, :], ALU.add).then_inc(route_d, 1)
            dve.wait_ge(ranks, 1)
            dve.wait_ge(route_d, 3)
            for t in range(TT):
                own(dve.scalar_tensor_tensor(out=key[:, t, 0:E], in0=bank[6][:, 64 * t:64 * t + E], scalar=1.0,
                                             in1=rt["mm"][:, t, :], op0=ALU.add, op1=ALU.mult))
            own(dve.tensor_reduce(esum[:, 18:19], bank[6][:, 2 * 64:2 * 64 + E], AX, ALU.max))
            own(dve.tensor_scalar(rounds[:, :], limit[:, :], esum[:, 18:19], None, ALU.is_lt))
            own(dve.tensor_reduce(esum[:, 19:20], rounds[:, :], AX, ALU.add))
            dve.tensor_copy(nrounds[:, :], esum[:, 19:20]).then_inc(routed, 1)
            dve.wait_ge(routed, 1)

            def picked(e):
                for t in range(TT):
                    ins = dve.tensor_scalar(pick[:, t, SLOTS:2 * SLOTS], count[:, 1:SLOTS + 1], key[:, t, bass.ds(e, 1)], None,
                                            ALU.is_equal)
                    if t == TT - 1:
                        ins.then_inc(pick_ready, 1)

            def results(n, quarters):
                for q in quarters:
                    dve.wait_ge(ylo_ready, 4 * n + q + 1)
                    s = slice(512 * q, 512 * (q + 1))
                    dve.tensor_tensor(yrow[:, s], bank[2 + q][0:SLOTS, :], ylo[:, s], ALU.add).then_inc(y_ready, 1)

            def gate_sum(n):
                dve.wait_ge(glo_ready, n + 1)
                dve.tensor_tensor(gsum[:, :], bank[0][0:SLOTS, :], glo[:, :], ALU.add).then_inc(gsum_ready, 1)

            def hidden(n):
                dve.wait_ge(ulo_ready, n + 1)
                dve.tensor_tensor(usum[:, :], bank[1][0:SLOTS, :], ulo[:, :], ALU.add).then_inc(usum_ready, 1)
                dve.wait_ge(silu_e, n + 1)
                dve.wait_ge(usum_ready, n + 1)
                dve.tensor_tensor(gsum[:, :], glo[:, :], usum[:, :], ALU.mult).then_inc(h_ready, 1)

            def hidden_lo(n):
                dve.wait_ge(hsh_ready, n + 1)
                dve.tensor_tensor(hs[:, :, SLOTS:2 * SLOTS], bank[1][:, 0:FE // P * SLOTS]
                                  .rearrange("p (k s) -> p k s", s=SLOTS),
                                  hs[:, :, 0:SLOTS].bitcast(F32), ALU.subtract).then_inc(hsl_ready, 1)

            def slots_rows(n):
                dve.wait_ge(idn_mm, n + 1)
                dve.tensor_tensor(idn[:, :], bank[7][0:SLOTS, 0:1], empty[0:SLOTS, :], ALU.add).then_inc(idn_ready, 1)

            n_rounds = dve.value_load(nrounds[0:1, 0:1], min_val=1, max_val=SEQ // SLOTS)
            picked(0)
            for t in range(TT):
                for k in range(2):
                    own(dve.tensor_scalar(esum[:, 20 + 2 * t + k:21 + 2 * t + k], rowno[:, :],
                                          float(k * SEQ + t * P) - BIG, None, ALU.add))
                own(dve.tensor_scalar(rt["t32"][:, t, :], rt["m1"][:, t, :], esum[:, 21 + 2 * t:22 + 2 * t], None, ALU.mult))
                own(dve.scalar_tensor_tensor(out=rowid[:, t, 0:E], in0=rt["m0"][:, t, :],
                                             scalar=esum[:, 20 + 2 * t:21 + 2 * t], in1=rt["t32"][:, t, :],
                                             op0=ALU.mult, op1=ALU.add))
            dve.memset(empty[:, :], BIG).then_inc(rows_ready, 1)
            dve.wait_ge(rows_ready, 1)
            with dve.Fori(0, n_rounds) as r:
                m = 2 * E * r
                for j in range(8):
                    lo_unit(dve, U_EXP + j, m)
                    if j == 4:
                        slots_rows(E * r)
                        picked(1)
                    if j == 5:
                        gate_sum(E * r)
                with dve.Fori(1, E) as e:
                    n = E * r + e
                    for j in range(PER):
                        lo_unit(dve, U_STEP + j, 2 * n - 2)
                        if j == 1:
                            hidden(n - 1)
                        if j == 3:
                            hidden_lo(n - 1)
                        if j == 5:
                            gate_sum(n)
                            dve.wait_ge(idx_ready, n)
                            slots_rows(n)
                            picked(e + 1)
                        if j == 9:
                            dve.wait_ge(idx_ready, n)
                            results(n - 1, (0, 1))
                        if j == 10:
                            results(n - 1, (2, 3))
                for j in range(4):
                    lo_unit(dve, U_STEP + j, 2 * E * r + 2 * E - 2)
                    if j == 1:
                        hidden(E * r + E - 1)
                        hidden_lo(E * r + E - 1)
                dve.wait_ge(idx_ready, E * r + E)
                results(E * r + E - 1, range(4))
                dve.wait_ge(xg_mm, 4 * (E + 1) * r + 4 * (E + 1))
                dve.wait_ge(pick_ready, (E + 1) * r + E + 1)
                dve.tensor_scalar(key[:, :, :], key[:, :, :], -float(SLOTS), None, ALU.add).then_inc(key_moved, 1)
                dve.wait_ge(key_moved, r + 1)
                picked(0)

            dve.wait_ge(routers_in, 16 * (G + 5))
            own(dve.tensor_tensor(esum[:, 14:16], rt["top"][:, :, 0], rt["top"][:, :, 1], ALU.add))
            own(dve.reciprocal(esum[:, 16:18], esum[:, 14:16]))
            own(dve.tensor_tensor(cw[:, :, :], rt["top"][:, :, 0:2],
                                  esum[:, 16:18][:, :, None].broadcast_to([P, TT, 2]), ALU.mult))
            own(dve.tensor_tensor(cw[:, :, :], cw[:, :, :],
                                  esum[:, 10:12][:, :, None].broadcast_to([P, TT, 2]), ALU.mult))
            for t in range(TT):
                dve.wait_ge(yk_in[t], 16 * 2)
                for s in range(2):
                    cols = slice(s * D // 2, (s + 1) * D // 2)
                    own(dve.scalar_tensor_tensor(out=resid[:, t, cols], in0=yk[:, t, 0, cols], scalar=cw[:, t, 0:1],
                                                 in1=resid[:, t, cols], op0=ALU.mult, op1=ALU.add))
                    dve.scalar_tensor_tensor(out=resid[:, t, cols], in0=yk[:, t, 1, cols], scalar=cw[:, t, 1:2],
                                             in1=resid[:, t, cols], op0=ALU.mult, op1=ALU.add).then_inc(summed, 1)
            for t in range(TT):
                dve.wait_ge(sums_ready, 1 + 2 * (t + 1))
                own(dve.tensor_tensor(stat2[:, 6 + t:7 + t], sq2[:, t, 0:1], sq2[:, t, 1:2], ALU.add))
                mean_eps(stat2[:, t:t + 1], stat2[:, 6 + t:7 + t], D)
                dve.wait_ge(root_out, 4 + t)
                own(dve.reciprocal(stat2[:, 4 + t:5 + t], stat[:, 2 + t:3 + t]))
                for s in range(2):
                    cols = slice(s * D // 2, (s + 1) * D // 2)
                    dve.scalar_tensor_tensor(out=u2[:, t, cols], in0=resid[:, t, cols], scalar=stat2[:, 4 + t:5 + t],
                                             in1=gfb[:, cols], op0=ALU.mult, op1=ALU.mult).then_inc(out_ready, 1)

        @block.tensor
        def _(pe):
            pe.wait_ge(masks_ready, 7)
            pe.wait_ge(xn_ready, TT + 1)
            for k in range(KD):
                if k >= 4:
                    pe.wait_ge(ul_ready, k - 3)
                o = bank[k % 4]
                pe.transpose(o[:, 0:META], mn[:, k::KD], ident[0:META, 0:META])
                for t in range(TT):
                    ins = pe.transpose(o[:, META + t * P:META + (t + 1) * P], xn[:, t, k::KD], ident[:, :])
                ins.then_inc(xt_ready, 1)

            def block_unit(c, m=0, out=None):
                for s in range(2):
                    pe.wait_ge(lo_ready, halves(c, m) + s + 1)
                    h, l = hi[(2 * c + s) % SPLIT], lo[(2 * c + s) % SPLIT]
                    for kk in range(KD // 2):
                        k = KD // 2 * s + kk
                        pe.matmul(out, part(h, kk, P), uh[:, k, :], start=(k == 0), stop=False)
                        pe.matmul(out, part(h, kk, P), ul[:, k, :], start=False, stop=False)
                        ins = pe.matmul(out, part(l, kk, P), uh[:, k, :], start=False, stop=(k == KD - 1))
                    ins.then_inc(halves_used, 1)

            pe.wait_ge(ul_ready, KD)
            block_unit(0, out=bank[7][:, 0:L])
            for c in range(U_IN, STRAIGHT):
                if c - U_IN >= 2:
                    pe.wait_ge(proj_out, c - U_IN - 1)
                block_unit(c, out=bank[c % 2][:, 0:L])
            with pe.Fori(0, LOOPS) as i:
                for j in range(RAW):
                    c = STRAIGHT + j
                    pe.wait_ge(proj_out, nth(c - U_IN - 1, i))
                    block_unit(c, i, out=bank[c % 2][:, 0:L])

            pe.wait_ge(params_in, 16 * 5)
            pe.wait_ge(z_ready, 1)
            for h in range(GH):
                ins = pe.matmul(bank[2 + h][:, 0:L], wgate2[:, h * P:(h + 1) * P], zt[:, :], start=True, stop=True)
            ins.then_inc(gates_mm, 1)
            pe.wait_ge(fgate_d, 2)
            for t in range(TT):
                ins = pe.transpose(bank[6][:, t * FH:(t + 1) * FH], ct[:, 2, META + t * P:META + (t + 1) * P],
                                   ident[0:FH, 0:FH])
            ins.then_inc(fgate_t, 1)
            pe.wait_ge(cq_ready, 1)

            def tokens(t):
                return slice(META + t * P, META + (t + 1) * P)

            def gla_first(h):
                if h:
                    pe.wait_ge(a_ready, h)
                for t in range(TT):
                    ins = pe.matmul(bank[0][:, t * P:(t + 1) * P], proj[:, GK + h, tokens(t)],
                                    proj[:, GQ + h, tokens(t)], start=True, stop=True)
                ins.then_inc(scores_g, 1)
                if h:
                    pe.wait_ge(k_ready, h)
                    pe.wait_ge(v_ready, h)
                pe.transpose(bank[1][0:META, 0:P], gt[1][:, h, 0:META], ident[:, :])
                for t in range(TT):
                    pe.transpose(bank[1][:, (t + 1) * P:(t + 2) * P], gt[1][:, h, tokens(t)], ident[:, :])
                for i in range(VH):
                    v = GV + VH * h + i
                    pe.transpose(bank[2][0:META, i * P:(i + 1) * P], proj[:, v, 0:META], ident[:, :])
                    pe.transpose(bank[2][:, DV + i * P:DV + (i + 1) * P], proj[:, v, tokens(0)], ident[:, :])
                    ins = pe.transpose(bank[3][:, i * P:(i + 1) * P], proj[:, v, tokens(1)], ident[:, :])
                ins.then_inc(kv_t, 1)

            def gla_update(h):
                pe.wait_ge(k_ready, h + 1)
                pe.wait_ge(v_ready, h + 1)
                if h:
                    pe.wait_ge(st_ready, h)
                for n in range(NCH):
                    rows = slice(0, META) if n == 0 else slice((n - 1) % 2 * CHUNK, ((n - 1) % 2 + 1) * CHUNK)
                    tile = 0 if n == 0 else 1 + (n - 1) // 2
                    ins = pe.matmul(upd[n], kln[rows, tile, :],
                                    vn[rows, tile, :], start=True, stop=True)
                ins.then_inc(upd_g, 1)

            def gla_output(h):
                pe.wait_ge(a_ready, h + 1)
                pe.wait_ge(st_ready, h + 1)
                if h:
                    pe.wait_ge(o_gout, h)
                for t in range(TT):
                    o = bank[6][:, t * DV:(t + 1) * DV]
                    pe.matmul(o, a2[h % 2][:, t, :], vn[:, 1 + t, :], start=True, stop=False, skip_group_check=True)
                    for i in range(2):
                        n = 2 * t + i
                        cols = slice(META + n * CHUNK, META + (n + 1) * CHUNK)
                        ins = pe.matmul(o[i * CHUNK:(i + 1) * CHUNK, :], gt[3][:, h, cols], st[:, n, :],
                                        start=False, stop=(i == 1), skip_group_check=True)
                ins.then_inc(o_g, 1)

            pe.wait_ge(gla_ops, 1)
            for h in range(GH):
                gla_first(h)
                gla_update(h)
                gla_output(h)

            def fox_scores(h):
                pe.wait_ge(q_ready, h + 1)
                if h:
                    pe.wait_ge(p_ready, h)
                else:
                    pe.wait_ge(heads_consts, 6 + NCH)
                for t in range(TT):
                    w = META + (t + 1) * P
                    pe.matmul(bank[2 + t][:, 0:w], qs[h % 2][:, t * P:(t + 1) * P], proj[:, FK + h, 0:w],
                              start=True, stop=False)
                    ins = pe.matmul(bank[2 + t][:, 0:w], sel[:, h, :], ct[:, 3, 0:w], start=False, stop=True)
                ins.then_inc(scores_f, 1)
                if h:
                    pe.wait_ge(vf_ready, h)
                pe.transpose(bank[6][0:META, 0:HD], proj[:, FV + h, 0:META], ident[:, :])
                for t in range(TT):
                    ins = pe.transpose(bank[6][:, (t + 1) * HD:(t + 2) * HD], proj[:, FV + h, tokens(t)], ident[:, :])
                ins.then_inc(vf_t, 1)

            def fox_transpose(h):
                pe.wait_ge(p_ready, h + 1)
                if h:
                    pe.wait_ge(pt_a, h)
                    pe.wait_ge(pt_d, h)
                for t in range(TT):
                    pe.transpose(bank[5][0:META, t * P:(t + 1) * P], pr[:, t, 0:META], ident[:, :])
                pe.transpose(bank[4][:, 0:P], pr[:, 0, tokens(0)], ident[:, :])
                pe.transpose(bank[4][:, P:2 * P], pr[:, 1, tokens(0)], ident[:, :])
                pe.transpose(bank[4][:, 2 * P:3 * P], pr[:, 1, tokens(1)], ident[:, :]).then_inc(p_t, 1)

            def fox_values(h):
                pe.wait_ge(pt_a, h + 1)
                pe.wait_ge(pt_d, h + 1)
                pe.wait_ge(vf_ready, h + 1)
                if h:
                    pe.wait_ge(o_fout, h)
                v = vf[h % 2]
                for t in range(TT):
                    o = bank[7][:, t * HD:(t + 1) * HD]
                    pe.matmul(o, ptm[:, t, :], v[0:META, 0, :], start=True, stop=False)
                    for i in range(t + 1):
                        ins = pe.matmul(o, pt[:, t + i, :], v[:, 1 + i, :], start=False, stop=(i == t))
                ins.then_inc(o_f, 1)

            for s in range(FH + 2):
                if s < FH:
                    if s == 0:
                        pe.wait_ge(st_ready, GH)
                        pe.wait_ge(o_gout, GH)
                        pe.wait_ge(v_ready, GH)
                    fox_scores(s)
                if 1 <= s <= FH:
                    fox_transpose(s - 1)
                if s >= 2:
                    fox_values(s - 2)

            for k in range(KD):
                if k >= 4:
                    pe.wait_ge(mixl_ready, k - 3)
                if k < GH * VH:
                    h, i = k // VH, k % VH
                    o = proj[:, GV + VH * h:GV + VH * (h + 1), :].rearrange("p a l -> p (a l)")
                    src = [o[:, t * DV + i * P:t * DV + (i + 1) * P] for t in range(TT)]
                    pe.wait_ge(on_d, TT * (h + 1))
                else:
                    src = [proj[:, FQ + k - GH * VH, t * P:(t + 1) * P] for t in range(TT)]
                    pe.wait_ge(on_p, TT * (k - GH * VH + 1))
                for t in range(TT):
                    ins = pe.transpose(bank[k % 4][:, t * P:(t + 1) * P], src[t], ident[:, :])
                ins.then_inc(mix_t, 1)

            pe.wait_ge(mixl_ready, KD)
            for n in range(D // 512):
                if n >= 2:
                    pe.wait_ge(resid_ready, n - 1)
                for q in range(D // 512):
                    c = U_OUT + n * (D // 512) + q
                    for kk in range(4):
                        g, k = 2 * c + kk // 2, 4 * q + kk
                        h, l = hi[g % SPLIT], lo[g % SPLIT]
                        pe.wait_ge(lo_ready, g + 1)
                        for t in range(TT):
                            o = bank[2 * (n % 2) + t][:, :]
                            cols = slice(t * P, (t + 1) * P)
                            pe.matmul(o, mixh[:, k, cols], part(h, kk % 2, 512), start=(k == 0), stop=False)
                            pe.matmul(o, mixl[:, k, cols], part(h, kk % 2, 512), start=False, stop=False)
                            ins = pe.matmul(o, mixh[:, k, cols], part(l, kk % 2, 512), start=False,
                                            stop=(k == KD - 1))
                        if kk % 2 == 1:
                            ins.then_inc(halves_used, 1)

            pe.wait_ge(resid_ready, D // 512)
            pe.wait_ge(routers_in, 16 * (G + 4))

            def some_logits(i):
                pe.wait_ge(u2t_a, i + 1)
                for k in (2 * i, 2 * i + 1):
                    for t in range(TT):
                        ins = pe.matmul(bank[4 + t][:, 0:G + E], u2t[:, k, t * P:(t + 1) * P], wr[:, k, :],
                                        start=(k == 0), stop=(k == KD - 1))
                return ins

            for i in range(KD // 2):
                pe.wait_ge(u2_ready, TT * (i // 2 + 1))
                if i >= 4:
                    pe.wait_ge(u2t_a, i - 3)
                for j in range(2):
                    for t in range(TT):
                        k = 2 * i + j
                        ins = pe.transpose(bank[i % 4][:, j * SEQ + t * P:j * SEQ + (t + 1) * P],
                                           u2[:, t, k * P:(k + 1) * P], ident[:, :])
                ins.then_inc(u2_t, 1)
                if i >= 2:
                    some_logits(i - 2)
            some_logits(KD // 2 - 2)
            some_logits(KD // 2 - 1).then_inc(logits, 1)
            pe.wait_ge(route_d, 3)
            mm = rt["mm"]
            pe.matmul(bank[6][:, 0:E], above[:, :], mm[:, 0, :], start=True, stop=True)
            pe.matmul(bank[6][:, 64:64 + E], above[:, :], mm[:, 1, :], start=True, stop=False)
            pe.matmul(bank[6][:, 64:64 + E], ones[:, 0:P], mm[:, 0, :], start=False, stop=True)
            for t in range(TT):
                ins = pe.matmul(bank[6][:, 128:128 + E], ones[:, 0:P], mm[:, t, :], start=(t == 0), stop=(t == TT - 1))
            ins.then_inc(ranks, 1)

            def pick_rows(q, before, b=6):
                if q and b == 6:
                    pe.wait_ge(xg_ready, before + q)
                for first, u in ((SLOTS, u2h), (0, u2l)):
                    for t in range(TT):
                        ins = pe.matmul(bank[b][:, :], pick[:, t, first:first + 2 * SLOTS],
                                        u[:, t, 512 * q:512 * (q + 1)], start=(first > 0 and t == 0),
                                        stop=(first == 0 and t == TT - 1))
                ins.then_inc(xg_mm, 1)

            def gather(q, before):
                pe.wait_ge(xg_ready, before + q + 1)
                if q:
                    pe.wait_ge(xs_ready, before + q)
                for kk in range(4):
                    ins = pe.transpose(bank[7][:, kk * 2 * SLOTS:(kk + 1) * 2 * SLOTS], xg[:, kk * P:(kk + 1) * P],
                                       ident[:, :])
                ins.then_inc(xs_t, 1)

            def expert_unit(c, m, outs, lhs, first, last):
                for i, (o, k) in enumerate(zip(outs, lhs)):
                    g = 2 * c + i // 2
                    if i % 2 == 0:
                        pe.wait_ge(lo_ready, halves(c, m) + i // 2 + 1)
                    pe.matmul(o[:, :], k, part(hi[g % SPLIT], i % 2, 512), start=first(i), stop=False)
                    ins = pe.matmul(o[:, :], k, part(lo[g % SPLIT], i % 2, 512), start=False, stop=last(i))
                    if i % 2 == 1:
                        ins.then_inc(halves_used, 1)

            pe.wait_ge(u2l_ready, TT)
            pe.wait_ge(routed, 1)
            n_rounds = pe.value_load(nrounds[0:1, 0:1], min_val=1, max_val=SEQ // SLOTS)
            def gate_or_up(w, q, c, m):
                expert_unit(c + q, m, [bank[w]] * 4, [xs[:, 4 * q + i, :] for i in range(4)],
                            lambda i: q == 0 and i == 0, lambda i: q == 3 and i == 3)

            def down(c, m):
                for q in range(4):
                    expert_unit(c + q, m, bank[2:6], [hs[:, q, :]] * 4, lambda i: q == 0, lambda i: q == 3)

            def slots_rows(e):
                for t in range(TT):
                    ins = pe.matmul(bank[7][0:SLOTS, 0:1], pick[:, t, SLOTS:2 * SLOTS].bitcast(F32),
                                    rowid[:, t, bass.ds(e, 1)], start=(t == 0), stop=(t == TT - 1))
                ins.then_inc(idn_mm, 1)

            def up_and_gather(n, before, c, m):
                pe.wait_ge(idn_ready, n + 1)
                pe.wait_ge(pick_ready, n + r + 2)
                for q in range(4):
                    pick_rows(q, before)
                    gate_or_up(1, q, c, m)
                    gather(q, before)

            def hidden_t(n):
                pe.wait_ge(h_ready, n + 1)
                for k in range(FE // P):
                    ins = pe.matmul(bank[1][:, k * SLOTS:(k + 1) * SLOTS], gsum[:, k * P:(k + 1) * P],
                                    ident[0:SLOTS, 0:SLOTS], start=True, stop=True)
                ins.then_inc(h_t, 1)

            def hidden_split(n):
                pe.wait_ge(hsh_ready, n + 1)
                pe.wait_ge(hsl_ready, n + 1)

            with pe.Fori(0, n_rounds) as r:
                pe.wait_ge(pick_ready, (E + 1) * r + 1)
                m = 2 * E * r
                for q in range(4):
                    pick_rows(q, 4 * (E + 1) * r, 2 + q)
                gather(0, 4 * (E + 1) * r)
                for q in range(4):
                    if q + 1 < 4:
                        gather(q + 1, 4 * (E + 1) * r)
                    pe.wait_ge(xs_ready, 4 * (E + 1) * r + q + 1)
                    gate_or_up(0, q, U_EXP, m)
                pe.wait_ge(rows_ready, 1)
                slots_rows(0)
                up_and_gather(E * r, 4 * (E + 1) * r + 4, U_EXP + 4, m)
                with pe.Fori(1, E) as e:
                    n = E * r + e
                    m = 2 * n - 2
                    before = 4 * (n + r)
                    for q in range(4):
                        pe.wait_ge(xs_ready, before + q + 1)
                        gate_or_up(0, q, U_STEP, m)
                        if q == 2:
                            hidden_t(n - 1)
                    slots_rows(e)
                    hidden_split(n - 1)
                    down(U_STEP + 4, m)
                    up_and_gather(n, before + 4, U_STEP + 8, m)
                    pe.wait_ge(y_ready, 4 * n)
                hidden_t(E * r + E - 1)
                hidden_split(E * r + E - 1)
                down(U_STEP, 2 * E * r + 2 * E - 2)
                pe.wait_ge(xs_ready, 4 * (E + 1) * r + 4 * (E + 1))
                pe.wait_ge(y_ready, 4 * E * r + 4 * E)


_INS = ['x', 'meta_tokens', 'norm1_g', 'w_in', 'b_fox_f', 'gla_w_gate2', 'gla_b_gate', 'gla_norm_g',
        'fox_norm_g', 'w_out', 'norm2_g', 'w_router_group', 'b_router_group', 'w_router_expert',
        'b_router_expert', 'w_exp_gate', 'w_exp_up', 'w_exp_down', 'norm_f_g']


def kernel(**inputs):
    import numpy as _np
    import concourse.bacc as _bacc
    from concourse import mybir as _mybir
    from concourse.bass_utils import run_bass_kernel_spmd as _run

    nc = _bacc.Bacc("TRN2", target_bir_lowering=False, num_devices=1)
    arrays, args = {}, []
    for name in _INS:
        a = _np.ascontiguousarray(inputs[name])
        arrays[f"in_{name}_dram"] = a
        args.append(nc.dram_tensor(f"in_{name}_dram", a.shape, _mybir.dt.from_np(a.dtype), kind="ExternalInput").ap())
    shape = inputs["x"].shape
    args.append(nc.dram_tensor("out_dram", shape, _mybir.dt.float32, kind="ExternalOutput").ap())
    hybrid_layer(nc, *args)
    r = _run(nc, [arrays], core_ids=[0])
    return r.results[0]["out_dram"]
```

```python
from contextlib import ExitStack

import concourse.bass as bass
from concourse import mybir

F32 = mybir.dt.float32
F32R = mybir.dt.float32r
U32 = mybir.dt.uint32
ALU = mybir.AluOpType
ACT = mybir.ActivationFunctionType
AX = mybir.AxisListType.X

P = 128
EPS = 1e-6
GLA_TAU = 16.0
CHUNK = 64
SLOTS = 64
RAW = 6
UNIT = 2048
HALF = UNIT // 2
SPLIT = 4
BIG = 4096.0
LOWEST = -3.4028234663852886e38


def hybrid_layer(nc, x, meta_tokens, norm1_g, w_in, b_fox_f, gla_w_gate2, gla_b_gate, gla_norm_g,
                 fox_norm_g, w_out, norm2_g, w_router_group, b_router_group, w_router_expert,
                 b_router_expert, w_exp_gate, w_exp_up, w_exp_down, norm_f_g, out):
    _, SEQ, D = x.shape
    META = meta_tokens.shape[0]
    L = META + SEQ
    KD = D // P
    TT = SEQ // P
    GH = gla_w_gate2.shape[2] // P
    DV = gla_norm_g.shape[1]
    VH = DV // P
    FH = b_fox_f.shape[1]
    HD = fox_norm_g.shape[1]
    G, E8 = w_router_expert.shape[1], w_router_expert.shape[3]
    E = G * E8
    FE = w_exp_gate.shape[4]
    RANK = gla_w_gate2.shape[1]
    NCH = SEQ // CHUNK
    QSCALE = float(P) ** -0.5

    FOX_COLS = 3 * FH * HD
    GLA_COL0 = FOX_COLS + FH
    GLA_BLOCKS = GH + GH + GH * VH + GH * VH
    Z_COL = GLA_COL0 + GLA_BLOCKS * P
    NB = GLA_BLOCKS + FOX_COLS // P
    GQ, GK, GV, GR = 0, GH, 2 * GH, 2 * GH + GH * VH
    FQ = GLA_BLOCKS
    FK, FV = FQ + FH, FQ + 2 * FH
    Z_AT = 32

    U_IN = 1
    U_OUT = U_IN + NB
    NOUT = (D // 512) * (D // 512)
    U_EXP = U_OUT + NOUT
    PER = 12
    U_STEP = U_EXP + 8
    assert GLA_BLOCKS % RAW == 0 and NB % RAW == 0 and PER % RAW == 0
    assert KD * P == UNIT and FE == 512 and D == 2048 and 2 * RAW % SPLIT == 0

    win = w_in[0].rearrange("(p k) n -> p k n", k=KD)
    wout = w_out[0]
    wg = w_exp_gate[0].rearrange("g e d f -> (g e) d f")
    wu = w_exp_up[0].rearrange("g e d f -> (g e) d f")
    wd = w_exp_down[0].rearrange("g e f d -> (g e) f d")

    with ExitStack() as ctx:
        def sem(name):
            return ctx.enter_context(nc.semaphore(name))

        class Area:

            def __init__(self, at):
                self.at = at

            def __call__(self, name, shape, dt=F32):
                size = 4
                for n in shape[1:]:
                    size *= n
                t = nc.alloc_sbuf_tensor_at(name, shape, dt, offset=self.at)
                self.at += (size + 31) // 32 * 32
                assert self.at <= SBUF_END, name
                return t

        SBUF_END = nc.sbuf_top
        keep = Area((nc.sbuf_base + 31) // 32 * 32)
        raw = [keep(f"raw{i}", [P, UNIT]) for i in range(RAW)]
        hi = [keep(f"hi{i}", [P, HALF], F32R) for i in range(SPLIT)]
        lo = [keep(f"lo{i}", [P, HALF], F32R) for i in range(SPLIT)]
        early = Area(keep.at)
        resid = keep("resid", [P, TT, D])
        keep_resid_end = keep.at
        ident = keep("ident", [P, P])
        above = keep("above", [P, P])
        chunkm = keep("chunkm", [P, P])
        ones = keep("ones", [P, P])
        rstd = keep("rstd", [P, L])
        count = keep("count", [P, CHUNK + 1])
        rowno = keep("rowno", [P, 1])
        g1 = keep("g1", [P, KD])
        wr = keep("wr", [P, KD, G + E])
        br = keep("br", [P, G + E])
        gbias = keep("gbias", [P, GH])
        g2 = keep("g2", [P, KD])
        ggain = keep("ggain", [P, VH])
        fgain = keep("fgain", [P, 1])
        wgate2 = keep("wgate2", [RANK, GH * P])
        fbias = keep("fbias", [FH, 1])
        stat = keep("stat", [P, 8])
        stat2 = keep("stat2", [P, 8])

        ct = early("ct", [FH, 4, L])
        cq = early("cq", [P, TT, FH])
        zt = early("zt", [RANK, L])
        a2 = [early(f"a2_{i}", [P, TT, P]) for i in range(2)]
        kln = early("kln", [P, 1 + TT, P])
        vn = early("vn", [P, 1 + TT, DV])
        st = early("st", [P, NCH, DV])
        assert early.at <= keep_resid_end
        proj_area = Area(keep.at)
        proj = proj_area("proj", [P, NB, L])
        temp = Area(proj_area.at)
        gt = [temp(f"gt{i}", [P, GH, L]) for i in range(4)]
        dec = temp("dec", [P, GH, NCH])
        ss = temp("ss", [P, 2 * (GH + FH)])
        rms = temp("rms", [P, 2 * (GH + FH)])
        rs = temp("rs", [P, FH, 8])
        junk = temp("junk", [P, DV])
        reset = gt[1][:, 0, :]
        mtmp_area = Area(proj_area.at)
        mtmp = [mtmp_area(f"mtmp{i}", [P, SEQ]) for i in range(2)]
        xn_area = Area(keep.at)
        diag = xn_area("diag", [P, 1 + TT, P])
        mn = xn_area("mn", [META, D])
        xjunk = xn_area("xjunk", [P, D])
        u_area = Area(temp.at)
        uh = u_area("uh", [P, KD, L], F32R)
        ul = u_area("ul", [P, KD, L], F32R)
        head = Area(temp.at)
        sel = head("sel", [FH, FH, P])
        pr = head("pr", [P, TT, L])
        pt = head("pt", [P, 3, P])
        ptm = head("ptm", [META, TT, P])
        vf = [head(f"vf{i}", [P, 1 + TT, HD]) for i in range(2)]
        lowest = head("lowest", [P, P])
        mix_area = Area(temp.at)
        mixh = mix_area("mixh", [P, KD, SEQ], F32R)
        mixl = mix_area("mixl", [P, KD, SEQ], F32R)

        ex = Area(keep.at)
        g2b = ex("g2b", [P, D])
        u2 = ex("u2", [P, TT, D])
        key = ex("key", [P, TT, E + 1])
        rowid = ex("rowid", [P, TT, E + 1])
        pick = ex("pick", [P, TT, 3 * SLOTS], F32R)
        idn = ex("idn", [SLOTS, 1], U32)
        idx = ex("idx", [SLOTS, 1], U32)
        nil = ex("nil", [SLOTS, 1], U32)
        empty = ex("empty", [P, 1])
        cw = ex("cw", [P, TT, 2])
        rounds = ex("rounds", [P, 4])
        limit = ex("limit", [P, 4])
        nrounds = ex("nrounds", [P, 1], U32)
        rt = {}
        for name, n in (("lg", G + E), ("gp", 8), ("gm", 8), ("gi", 8), ("ge", 8), ("oh", G), ("sel8", 8),
                        ("pe", 8), ("top", 8), ("ti", 8), ("eid", 2), ("m0", E), ("m1", E), ("mm", E), ("t32", E)):
            rt[name] = ex("rt_" + name, [P, TT, n])
        gix = ex("gix", [P, TT, 8], U32)
        tix = ex("tix", [P, TT, 8], U32)
        esum = ex("esum", [P, 32])
        sq2 = ex("sq2", [P, TT, D // 512])
        u2_area = Area(ex.at)
        u2h = u2_area("u2h", [P, TT, D], F32R)
        u2l = u2_area("u2l", [P, TT, D], F32R)
        ex2 = Area(u2_area.at)
        yrow = ex2("yrow", [SLOTS, D])
        ylo = ex2("ylo", [SLOTS, D])
        xs = ex2("xs", [P, KD, 2 * SLOTS], F32R)
        hs = ex2("hs", [P, FE // P, 2 * SLOTS], F32R)
        xg = ex2("xg", [P, 512])
        glo = ex2("glo", [SLOTS, FE])
        gsum = ex2("gsum", [SLOTS, FE])
        ulo = ex2("ulo", [SLOTS, FE])
        usum = ex2("usum", [SLOTS, FE])
        u2t = Area(u2_area.at - 4 * TT * D)("u2t", [P, KD, SEQ])
        fin = Area(ex.at)
        yk = fin("yk", [P, TT, 2, D])
        gfb = Area(keep.at)("gfb", [P, D])

        scratch = nc.dram_tensor("expert_rows", [2 * SEQ, D], F32)
        bank = [ctx.enter_context(nc.psum_tensor(f"bank{i}", [P, 512], F32)) for i in range(8)]
        masks_ready = sem("masks_ready")
        a2_zero = sem("a2_zero")
        heads_consts = sem("heads_consts")
        x_again = sem("x_again")
        params_in = sem("params_in")
        routers_in = sem("routers_in")
        wr_ready = sem("wr_ready")
        x_in = sem("x_in")
        diag_ready = sem("diag_ready")
        rstd_mm = sem("rstd_mm")
        rstd_ready = sem("rstd_ready")
        raw_zero = sem("raw_zero")
        narrow_in = sem("narrow_in")
        raw_in = [sem(f"raw_in{i}") for i in range(RAW)]
        hi_ready = sem("hi_ready")
        lo_ready = sem("lo_ready")
        halves_used = sem("halves_used")
        proj_out = sem("proj_out")
        act_step = sem("act_step")
        dve_step = sem("dve_step")
        quarters_sq = sem("quarters_sq")
        sums_ready = sem("sums_ready")
        root_in = sem("root_in")
        root_out = sem("root_out")
        xt_ready = sem("xt_ready")
        uh_ready = sem("uh_ready")
        ul_ready = sem("ul_ready")
        z_ready = sem("z_ready")
        gates_mm = sem("gates_mm")
        gate_d = sem("gate_d")
        gate_a = sem("gate_a")
        fgate_d = sem("fgate_d")
        fgate_a = sem("fgate_a")
        fgate_t = sem("fgate_t")
        cq_ready = sem("cq_ready")
        gla_ops = sem("gla_ops")
        kv_t = sem("kv_t")
        a_ready = sem("a_ready")
        k_ready = sem("k_ready")
        v_ready = sem("v_ready")
        upd_g = sem("upd_g")
        st_ready = sem("st_ready")
        o_g = sem("o_g")
        o_gout = sem("o_gout")
        scores_f = sem("scores_f")
        bias_f = sem("bias_f")
        p_ready = sem("p_ready")
        vf_t = sem("vf_t")
        vf_ready = sem("vf_ready")
        p_t = sem("p_t")
        pt_a = sem("pt_a")
        pt_d = sem("pt_d")
        o_f = sem("o_f")
        o_fout = sem("o_fout")
        sq_f = sem("sq_f")
        silu_ready = sem("silu_ready")
        rms_ready = sem("rms_ready")
        on_d = sem("on_d")
        on_p = sem("on_p")
        mix_t = sem("mix_t")
        mix_f = sem("mix_f")
        mixh_ready = sem("mixh_ready")
        mixl_ready = sem("mixl_ready")
        resid_ready = sem("resid_ready")
        u2_ready = sem("u2_ready")
        u2h_ready = sem("u2h_ready")
        u2l_ready = sem("u2l_ready")
        u2_t = sem("u2_t")
        u2t_a = sem("u2t_a")
        logits = sem("logits")
        route_d = sem("route_d")
        route_a = sem("route_a")
        ranks = sem("ranks")
        rows_ready = sem("rows_ready")
        routed = sem("routed")
        pick_ready = sem("pick_ready")
        xg_mm = sem("xg_mm")
        xg_ready = sem("xg_ready")
        xs_t = sem("xs_t")
        xs_ready = sem("xs_ready")
        glo_ready = sem("glo_ready")
        gsum_ready = sem("gsum_ready")
        silu_e = sem("silu_e")
        ulo_ready = sem("ulo_ready")
        usum_ready = sem("usum_ready")
        h_ready = sem("h_ready")
        h_t = sem("h_t")
        hsh_ready = sem("hsh_ready")
        hsl_ready = sem("hsl_ready")
        idn_ready = sem("idn_ready")
        idx_ready = sem("idx_ready")
        ylo_ready = sem("ylo_ready")
        y_ready = sem("y_ready")
        scattered = sem("scattered")
        scatters = sem("scatters")
        yk_in = [sem(f"yk_in{i}") for i in range(2 * TT)]
        out_ready = sem("out_ready")
        stat_zero = sem("stat_zero")
        summed = sem("summed")
        idn_mm = sem("idn_mm")
        key_moved = sem("key_moved")
        stored = sem("stored")

        def slot(c):
            return c % RAW

        def turn(c, m):
            return m + c // RAW

        def nth(c, m):
            return RAW * m + c

        def halves(c, m=0):
            return 2 * RAW * m + 2 * c

        def hi_unit(act, c, m=0):
            act.wait_ge(raw_in[slot(c)], 16 * (turn(c, m) + 1))
            if c == 0:
                act.wait_ge(narrow_in, 16)
            for s in range(2):
                g = 2 * c + s
                if g >= SPLIT:
                    act.wait_ge(halves_used, halves(c, m) + s - SPLIT + 1)
                act.copy(hi[g % SPLIT][:, :], raw[slot(c)][:, s * HALF:(s + 1) * HALF]).then_inc(hi_ready, 1)

        def lo_unit(dve, c, m=0):
            for s in range(2):
                g = 2 * c + s
                dve.wait_ge(hi_ready, halves(c, m) + s + 1)
                if g >= SPLIT:
                    dve.wait_ge(halves_used, halves(c, m) + s - SPLIT + 1)
                dve.tensor_tensor(lo[g % SPLIT][:, :], raw[slot(c)][:, s * HALF:(s + 1) * HALF],
                                  hi[g % SPLIT][:, :].bitcast(F32), ALU.subtract).then_inc(lo_ready, 1)

        def load_unit(sp, source, c, m=0):
            if c >= RAW:
                sp.wait_ge(lo_ready, halves(c - RAW + 1, m))
            n = source.shape[-1]
            sp.dma_start(raw[slot(c)][:, :].rearrange("p (k n) -> p k n", n=n),
                         source).then_inc(raw_in[slot(c)], 16)

        STRAIGHT = U_IN + RAW
        LOOPS = (GLA_BLOCKS - RAW) // RAW

        def part(w, k, n):
            return w[:, k * n:(k + 1) * n]

        def chunked(t):
            return t.rearrange("p h (c i) -> p h c i", i=CHUNK)

        upd = [bank[5][:, 0:DV], bank[2][:, 0:DV], bank[7][:, 0:DV], bank[2][:, DV:2 * DV]]

        FOX0 = U_IN + GLA_BLOCKS
        HEAD0, PER_HEAD = 7, 4

        def scores(h, t, keys):
            first = t * (META + P)
            return bank[2 + h % 2][:, first + keys.start:first + keys.stop]

        def bank_of(c):
            return bank[c if c < 5 else c % 2]

        def start_of(c):
            b = c - U_IN
            return META if GQ <= b < GQ + GH or FQ <= b < FQ + FH else 0

        EARLY_OUT = 4
        EARLY_UNITS = {10: U_OUT + 2, 14: U_OUT + 3}

        def head_at(i, later):
            h, rest = divmod(i - HEAD0 - later, PER_HEAD)
            return h if rest == 0 and 0 <= h < GH else None

        block = ctx.enter_context(nc.Block())

        @block.sync
        def _(sp):
            sp.dma_start(resid[:, :, :], x[0].rearrange("(t p) d -> p t d", p=P)).then_inc(x_in, 16)
            sp.dma_start(mn[:, :], meta_tokens).then_inc(x_in, 16)
            sp.dma_start(g1[:, :], norm1_g[0].rearrange("(p k) -> p k", k=KD)).then_inc(x_in, 16)
            sp.wait_ge(raw_zero, 1)
            narrow = raw[0][:, :].rearrange("p (k n) -> p k n", n=P)
            sp.dma_start(narrow[:, :, 0:FH], win[:, :, FOX_COLS:FOX_COLS + FH]).then_inc(raw_in[0], 16)
            sp.dma_start(narrow[:, :, Z_AT:Z_AT + RANK],
                         win[:, :, Z_COL:Z_COL + RANK]).then_inc(narrow_in, 16)
            for c in range(U_IN, STRAIGHT):
                load_unit(sp, win[:, :, GLA_COL0 + (c - U_IN) * P:GLA_COL0 + (c - U_IN + 1) * P], c)
            with sp.Fori(0, (GLA_BLOCKS - RAW) // RAW) as i:
                for j in range(RAW):
                    c = STRAIGHT + j
                    col = GLA_COL0 + (c - U_IN) * P + RAW * P * i
                    load_unit(sp, win[:, :, bass.ds(col, P)], c, i)
            with sp.Fori(0, (NB - GLA_BLOCKS) // RAW) as i:
                for j in range(RAW):
                    c = U_IN + GLA_BLOCKS + j
                    load_unit(sp, win[:, :, bass.ds(j * P + RAW * P * i, P)], c, i)
            for n in range(D // 512):
                for q in range(D // 512):
                    load_unit(sp, wout[q * 512:(q + 1) * 512, n * 512:(n + 1) * 512]
                              .rearrange("(k p) n -> p k n", p=P), U_OUT + n * (D // 512) + q)

            def gate_or_up(w, e, c, m):
                for q in range(4):
                    load_unit(sp, w[e, q * 512:(q + 1) * 512, :].rearrange("(k p) n -> p k n", p=P), c + q, m)

            def down(e, c, m):
                for q in range(4):
                    load_unit(sp, wd[e, q * P:(q + 1) * P, :].rearrange("(k p) n -> p k n", p=P), c + q, m)

            def one_round(m):
                gate_or_up(wg, 0, U_EXP, m)
                gate_or_up(wu, 0, U_EXP + 4, m)
                with sp.Fori(1, E) as e:
                    gate_or_up(wg, e, U_STEP, 2 * e - 2 + m)
                    down(e - 1, U_STEP + 4, 2 * e - 2 + m)
                    gate_or_up(wu, e, U_STEP + 8, 2 * e - 2 + m)
                down(E - 1, U_STEP, 2 * (E - 1) + m)

            one_round(0)
            sp.wait_ge(routed, 1)
            n_rounds = sp.value_load(nrounds[0:1, 0:1], min_val=1, max_val=SEQ // SLOTS)
            with sp.If(n_rounds > 1):
                with sp.Fori(1, n_rounds) as r:
                    one_round(2 * E * r)
            sp.wait_ge(scattered, 16 * E * n_rounds)
            rows = scratch[:, :].rearrange("(k t p) d -> p t k d", k=2, p=P)
            for t in range(TT):
                for s in range(2):
                    cols = slice(s * D // 2, (s + 1) * D // 2)
                    for k in range(2):
                        sp.dma_start(yk[:, t, k, cols], rows[:, t, k, cols]).then_inc(yk_in[2 * t + s], 16)
            out_rows = out[0].rearrange("(t p) d -> p t d", p=P)
            for t in range(TT):
                for s in range(2):
                    cols = slice(s * D // 2, (s + 1) * D // 2)
                    sp.wait_ge(out_ready, 2 * t + s + 1)
                    sp.dma_start(out_rows[:, t, cols], u2[:, t, cols]).then_inc(stored, 16)
            sp.wait_ge(stored, 16 * TT * 2)

        @block.gpsimd
        def _(pool):
            pool.memset(ones[:, :], 1.0).then_inc(masks_ready, 1)
            pool.wait_ge(masks_ready, 1)
            pool.affine_select(out=ident[:, :], in_=ones[:, 0:P], pattern=[[1, P]], compare_op=ALU.is_equal,
                               fill=0.0, base=0, channel_multiplier=-1).then_inc(masks_ready, 1)
            pool.affine_select(out=above[:, :], in_=ones[:, 0:P], pattern=[[1, P]], compare_op=ALU.is_gt,
                               fill=0.0, base=0, channel_multiplier=-1).then_inc(masks_ready, 1)
            pool.affine_select(out=chunkm[:, :], in_=ones[:, 0:P], pattern=[[1, P]], compare_op=ALU.is_ge,
                               fill=0.0, base=0, channel_multiplier=-1).then_inc(masks_ready, 1)
            pool.wait_ge(masks_ready, 4)
            pool.memset(chunkm[0:CHUNK, CHUNK:P], 0.0).then_inc(masks_ready, 1)
            pool.iota(count[:, :], [[1, CHUNK + 1]], base=0, channel_multiplier=0,
                      allow_small_or_imprecise_dtypes=True).then_inc(masks_ready, 1)
            pool.iota(rowno[:, :], [[0, 1]], base=0, channel_multiplier=1,
                      allow_small_or_imprecise_dtypes=True).then_inc(masks_ready, 1)
            for dst, src in ((gbias[:, :], gla_b_gate[0].rearrange("(h p) -> p h", p=P)),
                             (ggain[:, :], gla_norm_g[0].rearrange("(h p) -> p h", p=P)),
                             (fgain[:, :], fox_norm_g[0].rearrange("(p a) -> p a", a=1)),
                             (wgate2[:, :], gla_w_gate2[0]),
                             (fbias[:, :], b_fox_f[0].rearrange("(p a) -> p a", a=1))):
                pool.dma_start(dst, src, allow_slow_non_contiguous=True).then_inc(params_in, 16)
            pool.dma_start(wr[:, :, 0:G], w_router_group[0].rearrange("(k p) n -> p k n", p=P)).then_inc(routers_in, 16)
            for g in range(G):
                pool.dma_start(wr[:, :, G + g * E8:G + (g + 1) * E8],
                               w_router_expert[0, g].rearrange("(k p) n -> p k n", p=P)).then_inc(routers_in, 16)
            pool.dma_start(br[:, 0:G], b_router_group[0:1, :].broadcast_to([P, G])).then_inc(routers_in, 16)
            pool.dma_start(br[:, G:G + E], b_router_expert[0].rearrange("(a g) e -> a (g e)", a=1)
                           .broadcast_to([P, E])).then_inc(routers_in, 16)
            pool.dma_start(g2[:, :], norm2_g[0].rearrange("(k p) -> p k", p=P),
                           allow_slow_non_contiguous=True).then_inc(routers_in, 16)
            pool.wait_ge(routers_in, 16 * (G + 4))
            pool.tensor_tensor(wr[:, :, :], wr[:, :, :], g2[:, :, None].broadcast_to([P, KD, G + E]),
                               ALU.mult).then_inc(wr_ready, 1)
            pool.wait_ge(xt_ready, KD)
            pool.wait_ge(sums_ready, 1)
            pool.memset(a2[0][:, :, :], 0.0).then_inc(a2_zero, 1)
            pool.memset(a2[1][:, :, :], 0.0).then_inc(a2_zero, 1)
            pool.wait_ge(halves_used, halves(U_OUT))
            pool.memset(sel[:, :, :], 1.0).then_inc(heads_consts, 1)
            pool.wait_ge(heads_consts, 1)
            pool.affine_select(out=sel[:, :, :], in_=sel[:, :, :], pattern=[[1, FH], [0, P]],
                               compare_op=ALU.is_equal, fill=0.0, base=0,
                               channel_multiplier=-1).then_inc(heads_consts, 1)
            pool.wait_ge(scores_f, FH)
            pool.wait_ge(bias_f, FH)
            pool.wait_ge(o_g, GH)
            pool.dma_start(resid[:, :, :], x[0].rearrange("(t p) d -> p t d", p=P)).then_inc(x_again, 16)
            pool.wait_ge(rms_ready, 1)
            for h in range(FH):
                for t in range(TT):
                    i = TT * (GH + h) + t
                    o = proj[:, FQ + h, t * P:(t + 1) * P]
                    pool.tensor_scalar(o, o, rms[:, i:i + 1], None, ALU.mult).then_inc(on_p, 1)
            pool.wait_ge(mixl_ready, KD)
            pool.dma_start(g2b[:, :], norm2_g[0:1, :].broadcast_to([P, D])).then_inc(routers_in, 16)
            pool.memset(rt["gp"][:, :, :], LOWEST).then_inc(masks_ready, 1)
            pool.memset(key[:, :, E:E + 1], 0.0).then_inc(masks_ready, 1)
            pool.memset(rowid[:, :, E:E + 1], 0.0).then_inc(masks_ready, 1)
            pool.memset(nil[:, :], 0).then_inc(masks_ready, 1)
            for i in range(4):
                pool.memset(limit[:, i:i + 1], float(SLOTS * i)).then_inc(masks_ready, 1)
            pool.wait_ge(u2_ready, TT * (D // 512))
            pool.dma_start(gfb[:, :], norm_f_g.rearrange("(a d) -> a d", a=1).broadcast_to([P, D])).then_inc(routers_in, 16)
            pool.wait_ge(routed, 1)
            n_rounds = pool.value_load(nrounds[0:1, 0:1], min_val=1, max_val=SEQ // SLOTS)

            def named(n):
                pool.wait_ge(idn_ready, n + 1)
                pool.tensor_tensor(idx[:, :], idn[:, :], nil[:, :], ALU.add).then_inc(idx_ready, 1)

            def scatter(n):
                pool.wait_ge(y_ready, 4 * n + 4)
                pool.wait_ge(idx_ready, n + 1)
                pool.sem_inc(scatters, 1)
                pool.indirect_dma_start(scratch[:, :], bass.IndirectOffsetOnAxis(ap=idx[:, 0:1], axis=0),
                                        yrow[:, :], None, bounds_check=2 * SEQ - 1,
                                        oob_is_err=False).then_inc(scattered, 16)
                pool.wait_ge(scattered, 16 * n + 16)

            with pool.Fori(0, n_rounds) as r:
                named(E * r)
                with pool.Fori(1, E) as e:
                    scatter(E * r + e - 1)
                    named(E * r + e)
                scatter(E * r + E - 1)

        @block.scalar
        def _(act):
            steps = [0]

            def own(ins):
                steps[0] += 1
                ins.then_inc(act_step, 1)
                act.wait_ge(act_step, steps[0])

            def root(n, src, dst):
                act.wait_ge(root_in, n)
                act.activation(dst, src, ACT.Sqrt).then_inc(root_out, 1)

            act.wait_ge(x_in, 48)
            for k in range(KD):
                act.wait_ge(xt_ready, k + 1)
                act.activation(uh[:, k, :], bank[k % 4][:, 0:L], ACT.Copy,
                               scale=g1[:, k:k + 1]).then_inc(uh_ready, 1)
            hi_unit(act, 0)
            hi_unit(act, 1)
            act.wait_ge(stat_zero, 1)
            own(act.activation(xjunk[:, :], resid[:, 0, :], ACT.Square, accum_out=stat[:, 0:1]))
            hi_unit(act, 2)
            own(act.activation(xjunk[:, :], resid[:, 1, :], ACT.Square, accum_out=stat[:, 1:2]))
            act.activation(xjunk[0:META, :], mn[:, :], ACT.Square, accum_out=stat[0:META, TT:TT + 1]).then_inc(sums_ready, 1)
            root(1, stat2[:, 0:TT + 1], stat[:, 0:TT + 1])
            for c in range(3, STRAIGHT):
                hi_unit(act, c)
            with act.Fori(0, LOOPS) as i:
                for j in range(RAW):
                    hi_unit(act, STRAIGHT + j, i)

            def fox_gates():
                act.wait_ge(fgate_d, 1)
                own(act.activation(ct[:, 1, :], ct[:, 1, :], ACT.Exp, scale=-1.0))
                act.activation(ct[:, 1, :], ct[:, 1, :], ACT.Ln, bias=1.0).then_inc(fgate_a, 1)

            def silu_r():
                act.wait_ge(proj_out, GLA_BLOCKS)
                r_all = proj[:, GR:GR + GH * VH, META:L]
                act.activation(r_all, r_all, ACT.Silu).then_inc(silu_ready, 1)

            def gla_gates():
                act.wait_ge(gate_d, 1)
                own(act.activation(gt[1][:, :, :], gt[1][:, :, :], ACT.Exp, scale=-1.0))
                act.activation(gt[1][:, :, :], gt[1][:, :, :], ACT.Ln, bias=1.0).then_inc(gate_a, 1)

            def decays():
                act.wait_ge(gate_d, 2)
                act.activation(gt[3][:, :, META:L], gt[2][:, :, META:L], ACT.Exp, scale=1.0 / GLA_TAU).then_inc(gate_a, 1)
                act.activation(dec[:, :, :], gt[2][:, :, META + CHUNK - 1::CHUNK], ACT.Exp,
                               scale=1.0 / GLA_TAU).then_inc(gate_a, 1)
                act.wait_ge(gate_d, 3)
                act.activation(gt[0][:, :, :], gt[0][:, :, :], ACT.Exp, scale=1.0 / GLA_TAU).then_inc(gate_a, 1)

            def decays_middle():
                act.wait_ge(gate_d, 4)
                act.activation(gt[2][:, :, META:L], gt[0][:, :, META:L], ACT.Exp, scale=1.0 / GLA_TAU).then_inc(gate_a, 1)
                act.wait_ge(gate_a, 5)
                act.activation(gt[0][:, :, META:L], gt[0][:, :, META:L], ACT.Exp, scale=-1.0 / GLA_TAU).then_inc(gate_a, 1)

            gate_steps = {1: fox_gates, 2: silu_r, 4: gla_gates, 5: decays, 6: decays_middle}

            def gla_v(h):
                act.wait_ge(kv_t, h + 1)
                if h:
                    act.wait_ge(o_g, h)
                own(act.copy(vn[0:META, 0, :], bank[3][0:META, 0:DV]))
                own(act.copy(vn[:, 1, :], bank[3][:, DV:2 * DV]))
                act.copy(vn[:, 2, :], bank[5][:, 0:DV]).then_inc(v_ready, 1)

            def gla_out(h):
                act.wait_ge(o_g, h + 1)
                o = proj[:, GV + VH * h:GV + VH * (h + 1), :].rearrange("p a l -> p (a l)")
                own(act.copy(o[:, 0:TT * DV], bank[6][:, :]))
                for t in range(TT):
                    ins = act.activation(junk[:, :], bank[6][:, t * DV:(t + 1) * DV], ACT.Square,
                                         accum_out=ss[:, TT * h + t:TT * h + t + 1])
                    if t < TT - 1:
                        own(ins)
                ins.then_inc(o_gout, 1)
                act.wait_ge(o_gout, h + 1)

            for i in range(NB - GLA_BLOCKS + 2):
                hi_unit(act, FOX0 + i)
                if i in gate_steps:
                    gate_steps[i]()
                if (h := head_at(i, 2)) is not None:
                    gla_v(h)
                if (h := head_at(i, 6)) is not None:
                    gla_out(h)

            def fox_exp(h):
                act.wait_ge(bias_f, h + 1)
                if h:
                    act.wait_ge(p_t, h)
                for t in range(TT):
                    w = META + (t + 1) * P
                    ins = act.activation(pr[:, t, 0:w], scores(h, t, slice(0, w)), ACT.Exp, bias=rs[:, h, 4 + t:5 + t],
                                         accum_out=rs[:, h, 6 + t:7 + t])
                ins.then_inc(p_ready, 1)

            def fox_v(h):
                act.wait_ge(vf_t, h + 1)
                if h >= 2:
                    act.wait_ge(o_f, h - 1)
                own(act.copy(vf[h % 2][0:META, 0, :], bank[6][0:META, 0:HD]))
                act.copy(vf[h % 2][:, 1:3, :].rearrange("p a b -> p (a b)"), bank[6][:, HD:3 * HD]).then_inc(vf_ready, 1)

            def fox_pt(h):
                act.wait_ge(p_t, h + 1)
                if h:
                    act.wait_ge(o_f, h)
                act.copy(pt[:, :, :].rearrange("p a b -> p (a b)"), bank[4][:, 0:3 * P]).then_inc(pt_a, 1)

            def fox_sq(h):
                act.wait_ge(o_fout, h + 1)
                for t in range(TT):
                    i = TT * (GH + h) + t
                    ins = act.activation(junk[:, 0:HD], proj[:, FQ + h, t * P:(t + 1) * P], ACT.Square,
                                         accum_out=ss[:, i:i + 1])
                    if t < TT - 1:
                        own(ins)
                ins.then_inc(sq_f, 1)
                act.wait_ge(sq_f, h + 1)

            for s in range(FH + 2):
                if s < FH:
                    fox_exp(s)
                    fox_v(s)
                if 1 <= s <= FH:
                    fox_pt(s - 1)
                if s >= 2:
                    fox_sq(s - 2)

            root(2, ss[:, :], rms[:, :])
            for k in range(KD):
                if k < GH * VH:
                    act.wait_ge(mix_f, k + 1)
                    act.copy(mixh[:, k, :], mtmp[k % 2][:, :]).then_inc(mixh_ready, 1)
                else:
                    act.wait_ge(mix_t, k + 1)
                    act.activation(mixh[:, k, :], bank[4 + k % 4][:, 0:SEQ], ACT.Copy,
                                   scale=fgain[:, 0:1]).then_inc(mixh_ready, 1)
                if k in EARLY_UNITS:
                    hi_unit(act, EARLY_UNITS[k])

            def squares(n):
                act.wait_ge(resid_ready, n + 1)
                for t in range(TT):
                    ins = act.activation(u2[:, t, 512 * n:512 * (n + 1)], resid[:, t, 512 * n:512 * (n + 1)],
                                         ACT.Square, accum_out=sq2[:, t, n:n + 1])
                ins.then_inc(quarters_sq, 1)

            def resid_t(n):
                for i in (2 * n, 2 * n + 1):
                    act.wait_ge(u2_t, i + 1)
                    act.copy(u2t[:, 2 * i:2 * i + 2, :].rearrange("p k l -> p (k l)"),
                             bank[4 + i % 2][:, :]).then_inc(u2t_a, 1)

            for c in range(U_OUT + 4, U_EXP):
                hi_unit(act, c)
                if (c - U_OUT) % 4 == 2 and c - U_OUT > 4:
                    squares((c - U_OUT) // 4 - 1)
                if (c - U_OUT) % 4 == 0 and c - U_OUT >= 8:
                    resid_t((c - U_OUT) // 4 - 2)
            resid_t(D // 512 - 2)
            squares(D // 512 - 1)
            root(3, stat2[:, 0:TT], stat[:, 0:TT])
            resid_t(D // 512 - 1)
            hi_unit(act, U_EXP)
            hi_unit(act, U_EXP + 1)
            act.wait_ge(route_d, 1)
            for t in range(TT):
                ins = act.activation(rt["ge"][:, t, :], rt["gp"][:, t, :], ACT.Exp, bias=esum[:, t:t + 1],
                                     accum_out=esum[:, 2 + t:3 + t])
            ins.then_inc(route_a, 1)
            act.wait_ge(logits, 1)
            act.wait_ge(route_d, 2)
            for t in range(TT):
                ins = act.activation(rt["pe"][:, t, :], rt["sel8"][:, t, :], ACT.Exp, bias=esum[:, 4 + t:5 + t],
                                     accum_out=esum[:, 6 + t:7 + t])
            ins.then_inc(route_a, 1)
            for n in range(D // 512):
                act.wait_ge(u2_ready, TT * (n + 1))
                for t in range(TT):
                    act.copy(u2h[:, t, 512 * n:512 * (n + 1)], u2[:, t, 512 * n:512 * (n + 1)]).then_inc(u2h_ready, 1)

            def picked_rows(q, before, b=6):
                act.wait_ge(xg_mm, before + q + 1)
                act.copy(xg[:, :], bank[b][:, :]).then_inc(xg_ready, 1)

            def gathered(q, before):
                act.wait_ge(xs_t, before + q + 1)
                act.copy(xs[:, 4 * q:4 * q + 4, :].rearrange("p k s -> p (k s)"),
                         bank[7][:, :]).then_inc(xs_ready, 1)

            def result_lo(n):
                for q in range(4):
                    act.copy(ylo[:, 512 * q:512 * (q + 1)], bank[2 + q][SLOTS:P, :]).then_inc(ylo_ready, 1)

            def gate_lo(n):
                act.copy(glo[:, :], bank[0][SLOTS:P, :]).then_inc(glo_ready, 1)

            def gate_silu(n):
                act.wait_ge(gsum_ready, n + 1)
                act.activation(glo[:, :], gsum[:, :], ACT.Silu).then_inc(silu_e, 1)

            def up_lo(n):
                act.copy(ulo[:, :], bank[1][SLOTS:P, :]).then_inc(ulo_ready, 1)

            def hidden_hi(n):
                act.wait_ge(h_t, n + 1)
                act.copy(hs[:, :, 0:SLOTS], bank[1][:, 0:FE // P * SLOTS]
                         .rearrange("p (k s) -> p k s", s=SLOTS)).then_inc(hsh_ready, 1)

            act.wait_ge(routed, 1)
            n_rounds = act.value_load(nrounds[0:1, 0:1], min_val=1, max_val=SEQ // SLOTS)
            with act.Fori(0, n_rounds) as r:
                gathers = 4 * (E + 1) * r
                m = 2 * E * r
                with act.If(r > 0):
                    hi_unit(act, U_EXP, m)
                    hi_unit(act, U_EXP + 1, m)
                picked_rows(0, gathers, 2)
                gathered(0, gathers)
                picked_rows(1, gathers, 3)
                gathered(1, gathers)
                for j in range(2, 8):
                    hi_unit(act, U_EXP + j, m)
                    if j < 4:
                        picked_rows(j, gathers, 2 + j)
                        gathered(j, gathers)
                    if j == 5:
                        act.wait_ge(halves_used, halves(U_EXP + 4, m))
                        gate_lo(E * r)
                        picked_rows(0, gathers + 4)
                    if j == 6:
                        gate_silu(E * r)
                        gathered(0, gathers + 4)
                        picked_rows(1, gathers + 4)
                    if j == 7:
                        gathered(1, gathers + 4)
                        picked_rows(2, gathers + 4)
                with act.Fori(1, E) as e:
                    n = E * r + e
                    m = 2 * n - 2
                    before = 4 * (n + r)
                    for j in range(PER):
                        hi_unit(act, U_STEP + j, m)
                        if j == 0:
                            gathered(2, before)
                            picked_rows(3, before)
                        if j == 1:
                            act.wait_ge(halves_used, halves(U_STEP, m))
                            up_lo(n - 1)
                            gathered(3, before)
                        if j == 3:
                            hidden_hi(n - 1)
                        if j == 5:
                            act.wait_ge(halves_used, halves(U_STEP + 4, m))
                            gate_lo(n)
                        if j == 6:
                            gate_silu(n)
                        if j == 9:
                            act.wait_ge(halves_used, halves(U_STEP + 8, m))
                            picked_rows(0, before + 4)
                            result_lo(n - 1)
                        if j == 10:
                            gathered(0, before + 4)
                            picked_rows(1, before + 4)
                        if j == 11:
                            gathered(1, before + 4)
                            picked_rows(2, before + 4)
                            act.wait_ge(y_ready, 4 * n)
                m = 2 * E * r + 2 * E - 2
                for j in range(4):
                    hi_unit(act, U_STEP + j, m)
                    if j == 1:
                        act.wait_ge(halves_used, halves(U_STEP, m))
                        up_lo(E * r + E - 1)
                        gathered(2, gathers + 4 * E)
                        picked_rows(3, gathers + 4 * E)
                        gathered(3, gathers + 4 * E)
                        hidden_hi(E * r + E - 1)
                act.wait_ge(halves_used, halves(U_STEP + 4, m))
                result_lo(E * r + E - 1)
                act.wait_ge(y_ready, 4 * E * r + 4 * E)
            for t in range(TT):
                for s in range(2):
                    cols = slice(s * D // 2, (s + 1) * D // 2)
                    act.wait_ge(summed, 2 * t + s + 1)
                    act.activation(u2[:, t, cols], resid[:, t, cols], ACT.Square,
                                   accum_out=sq2[:, t, s:s + 1]).then_inc(sums_ready, 1)
                root(4 + t, stat2[:, t:t + 1], stat[:, 2 + t:3 + t])

        @block.vector
        def _(dve):
            steps = [0]

            def own(ins):
                steps[0] += 1
                ins.then_inc(dve_step, 1)
                dve.wait_ge(dve_step, steps[0])

            def mean_eps(dst, src, n):
                dve.tensor_scalar(dst, src, 1.0 / n, EPS, ALU.mult, ALU.add).then_inc(root_in, 1)

            dve.memset(stat[:, :], 0.0).then_inc(stat_zero, 1)
            dve.memset(raw[0][:, :], 0.0).then_inc(raw_zero, 1)
            dve.wait_ge(x_in, 48)
            for k in range(KD):
                dve.wait_ge(uh_ready, k + 1)
                dve.scalar_tensor_tensor(out=ul[:, k, :], in0=bank[k % 4][:, 0:L], scalar=g1[:, k:k + 1],
                                         in1=uh[:, k, :].bitcast(F32), op0=ALU.mult,
                                         op1=ALU.subtract).then_inc(ul_ready, 1)
            for c in range(3):
                lo_unit(dve, c)
            dve.wait_ge(sums_ready, 1)
            mean_eps(stat2[:, 0:TT + 1], stat[:, 0:TT + 1], D)
            dve.wait_ge(root_out, 1)
            own(dve.reciprocal(stat2[:, 0:TT + 1], stat[:, 0:TT + 1]))
            dve.wait_ge(masks_ready, 7)
            for t in range(TT + 1):
                dve.tensor_scalar(diag[:, t, :], ident[:, :], stat2[:, t:t + 1], None, ALU.mult).then_inc(diag_ready, 1)
            lo_unit(dve, 3)
            dve.wait_ge(rstd_mm, 1)
            dve.tensor_copy(rstd[:, :], bank[6][:, 0:L]).then_inc(rstd_ready, 1)
            dve.wait_ge(rstd_ready, 1)

            def proj_scaled(c, m=0):
                dve.wait_ge(halves_used, halves(c + 1, m))
                a = start_of(c) if isinstance(m, int) else 0
                out = (proj[:, c - U_IN, a:L] if isinstance(m, int) else
                       proj[:, bass.ds(c - U_IN + RAW * m, 1), :].rearrange("p a l -> p (a l)"))
                if isinstance(m, int) and FQ <= c - U_IN < FQ + FH:
                    ins = dve.scalar_tensor_tensor(out=out, in0=bank_of(c)[:, a:L], scalar=QSCALE, in1=rstd[:, a:L],
                                                   op0=ALU.mult, op1=ALU.mult)
                else:
                    ins = dve.tensor_tensor(out, bank_of(c)[:, a:L], rstd[:, a:L], ALU.mult)
                ins.then_inc(proj_out, 1)

            proj_scaled(1)
            for c in range(4, STRAIGHT):
                lo_unit(dve, c)
                proj_scaled(c - 2)
            with dve.Fori(0, LOOPS) as i:
                for j in range(RAW):
                    lo_unit(dve, STRAIGHT + j, i)
                    proj_scaled(STRAIGHT + j - 2, i)

            def gates_in():
                dve.wait_ge(params_in, 16 * 5)
                dve.wait_ge(halves_used, halves(1))
                dve.tensor_tensor(zt[:, :], bank[7][Z_AT:Z_AT + RANK, 0:L], rstd[Z_AT:Z_AT + RANK, :],
                                  ALU.mult).then_inc(z_ready, 1)
                own(dve.tensor_tensor(ct[:, 0, :], bank[7][0:FH, 0:L], rstd[0:FH, :], ALU.mult))
                own(dve.tensor_scalar(ct[:, 0, :], ct[:, 0, :], fbias[:, 0:1], None, ALU.add))
                own(dve.scalar_tensor_tensor(out=ct[:, 1, :], in0=ct[:, 0, :], scalar=-1.0, in1=ct[:, 0, :],
                                             op0=ALU.mult, op1=ALU.max))
                dve.tensor_scalar(ct[:, 0, :], ct[:, 0, :], 0.0, None, ALU.min).then_inc(fgate_d, 1)

            def fox_cumulated():
                dve.wait_ge(fgate_d, 1)
                dve.wait_ge(fgate_a, 1)
                own(dve.tensor_tensor(ct[:, 0, :], ct[:, 0, :], ct[:, 1, :], ALU.subtract))
                own(dve.tensor_tensor_scan(ct[:, 2, :], ones[0:FH, 0:1].broadcast_to([FH, L]), ct[:, 0, :], 0.0,
                                           ALU.mult, ALU.add))
                dve.tensor_scalar(ct[:, 3, :], ct[:, 2, :], -1.0, None, ALU.mult).then_inc(fgate_d, 1)

            def gla_in():
                dve.wait_ge(gates_mm, 1)
                for h in range(GH):
                    ins = dve.tensor_scalar(gt[0][:, h, :], bank[2 + h][:, 0:L], gbias[:, h:h + 1], None, ALU.add)
                    if h < GH - 1:
                        ins.then_inc(dve_step, 1)
                        steps[0] += 1
                    else:
                        own(ins)
                own(dve.scalar_tensor_tensor(out=gt[1][:, :, :], in0=gt[0][:, :, :], scalar=-1.0, in1=gt[0][:, :, :],
                                             op0=ALU.mult, op1=ALU.max))
                dve.tensor_scalar(gt[0][:, :, :], gt[0][:, :, :], 0.0, None, ALU.min).then_inc(gate_d, 1)

            b_x = chunked(gt[2][:, :, META:L])
            d_x = chunked(gt[0][:, :, META:L])
            wide = [P, GH, NCH, CHUNK]

            def gla_cumulated():
                dve.wait_ge(gate_d, 1)
                dve.wait_ge(gate_a, 1)
                own(dve.tensor_tensor(gt[0][:, :, :], gt[0][:, :, :], gt[1][:, :, :], ALU.subtract))
                own(dve.memset(reset, 1.0))
                own(dve.memset(reset[:, 0:1], 0.0))
                own(dve.memset(reset[:, META::CHUNK], 0.0))
                for h in range(GH):
                    ins = dve.tensor_tensor_scan(gt[2][:, h, :], reset, gt[0][:, h, :], 0.0, ALU.mult, ALU.add)
                    if h < GH - 1:
                        ins.then_inc(dve_step, 1)
                        steps[0] += 1
                ins.then_inc(gate_d, 1)
                dve.wait_ge(gate_d, 2)
                dve.tensor_tensor(d_x, b_x[:, :, :, CHUNK - 1:CHUNK].broadcast_to(wide), b_x, ALU.subtract)\
                   .then_inc(dve_step, 1)
                steps[0] += 1
                dve.tensor_tensor(gt[0][:, :, 0:META], gt[2][:, :, META - 1:META].broadcast_to([P, GH, META]),
                                  gt[2][:, :, 0:META], ALU.subtract).then_inc(gate_d, 1)

            def gla_scaled():
                dve.wait_ge(proj_out, 2 * GH)
                dve.wait_ge(gate_a, 2)
                own(dve.scalar_tensor_tensor(out=gt[3][:, :, META:L], in0=proj[:, GQ:GQ + GH, META:L], scalar=QSCALE,
                                             in1=gt[3][:, :, META:L], op0=ALU.mult, op1=ALU.mult))
                dve.wait_ge(gate_a, 4)
                own(dve.tensor_tensor(gt[1][:, :, :], proj[:, GK:GK + GH, :], gt[0][:, :, :], ALU.mult))
                dve.tensor_tensor(d_x, b_x, b_x[:, :, :, CHUNK // 2:CHUNK // 2 + 1].broadcast_to(wide),
                                  ALU.subtract).then_inc(gate_d, 1)
                dve.wait_ge(fgate_t, 1)
                dve.tensor_copy(cq[:, :, :].rearrange("p t h -> p (t h)"), bank[6][:, 0:TT * FH]).then_inc(cq_ready, 1)

            def gla_scaled_middle():
                dve.wait_ge(gate_a, 5)
                q_x, k_x = proj[:, GQ:GQ + GH, META:L], proj[:, GK:GK + GH, META:L]
                dve.scalar_tensor_tensor(out=q_x, in0=q_x, scalar=QSCALE, in1=gt[2][:, :, META:L], op0=ALU.mult,
                                         op1=ALU.mult).then_inc(dve_step, 1)
                steps[0] += 1
                dve.wait_ge(gate_a, 6)
                dve.tensor_tensor(k_x, k_x, gt[0][:, :, META:L], ALU.mult).then_inc(gla_ops, 1)

            gate_steps = {0: gates_in, 2: fox_cumulated, 3: gla_in, 4: gla_cumulated, 5: gla_scaled,
                          6: gla_scaled_middle}

            def gla_masked(h):
                dve.wait_ge(kv_t, h + 1)
                dve.wait_ge(a2_zero, 2)
                if h >= 2:
                    dve.wait_ge(o_g, h - 1)
                for t in range(TT):
                    ins = dve.copy_predicated(a2[h % 2][:, t, :], chunkm[:, :].bitcast(U32),
                                              bank[2][:, t * P:(t + 1) * P])
                    if t < TT - 1:
                        ins.then_inc(dve_step, 1)
                        steps[0] += 1
                ins.then_inc(a_ready, 1)

            def gla_k(h):
                dve.wait_ge(kv_t, h + 1)
                if h:
                    dve.wait_ge(upd_g, h)
                own(dve.tensor_copy(kln[0:META, 0, :], bank[4][0:META, 0:P]))
                dve.tensor_copy(kln[:, 1:3, :].rearrange("p a b -> p (a b)"), bank[4][:, P:3 * P]).then_inc(k_ready, 1)

            def gla_states(h):
                dve.wait_ge(upd_g, h + 1)
                if h:
                    dve.wait_ge(o_g, h)
                own(dve.tensor_copy(st[:, 0, :], upd[0]))
                for n in range(1, NCH):
                    ins = dve.scalar_tensor_tensor(
                        out=st[:, n, :], in0=st[:, n - 1, :], scalar=dec[:, h, n - 1:n],
                        in1=upd[n], op0=ALU.mult, op1=ALU.add)
                    if n < NCH - 1:
                        own(ins)
                ins.then_inc(st_ready, 1)

            for i in range(NB - GLA_BLOCKS + 2):
                lo_unit(dve, FOX0 + i)
                proj_scaled(FOX0 + i - 2)
                if i in gate_steps:
                    gate_steps[i]()
                if (h := head_at(i, 4)) is not None:
                    gla_states(h)
                if (h := head_at(i, 2)) is not None:
                    gla_masked(h)
                    gla_k(h)

            def fox_mask(h):
                dve.wait_ge(scores_f, h + 1)
                for t in range(TT):
                    own(dve.copy_predicated(scores(h, t, slice(META + t * P, META + (t + 1) * P)),
                                            above[:, :].bitcast(U32), lowest[:, :]))
                    own(dve.tensor_reduce(rs[:, h, t:t + 1], scores(h, t, slice(0, META + (t + 1) * P)), AX, ALU.max))
                own(dve.tensor_tensor(rs[:, h, 2:4], rs[:, h, 0:2], cq[:, :, h], ALU.add))
                dve.tensor_tensor(rs[:, h, 4:6], cq[:, :, h], rs[:, h, 2:4], ALU.subtract).then_inc(bias_f, 1)

            def fox_pt_meta(h):
                dve.wait_ge(p_t, h + 1)
                if h:
                    dve.wait_ge(o_f, h)
                dve.tensor_copy(ptm[:, :, :].rearrange("p a b -> p (a b)"), bank[5][0:META, 0:TT * P]).then_inc(pt_d, 1)

            def fox_out(h):
                dve.wait_ge(o_f, h + 1)
                dve.wait_ge(p_ready, h + 1)
                own(dve.reciprocal(rs[:, h, 0:2], rs[:, h, 6:8]))
                for t in range(TT):
                    ins = dve.tensor_scalar(proj[:, FQ + h, t * P:(t + 1) * P], bank[7][:, t * HD:(t + 1) * HD],
                                            rs[:, h, t:t + 1], None, ALU.mult)
                    if t < TT - 1:
                        ins.then_inc(dve_step, 1)
                        steps[0] += 1
                ins.then_inc(o_fout, 1)

            own(dve.memset(lowest[:, :], LOWEST))
            for s in range(FH + 2):
                if s < FH:
                    fox_mask(s)
                if 1 <= s <= FH:
                    fox_pt_meta(s - 1)
                if s >= 2:
                    fox_out(s - 2)

            dve.wait_ge(o_gout, GH)
            dve.wait_ge(sq_f, FH)
            own(dve.tensor_scalar(ss[:, 0:TT * GH], ss[:, 0:TT * GH], 1.0 / DV, EPS, ALU.mult, ALU.add))
            mean_eps(ss[:, TT * GH:], ss[:, TT * GH:], HD)
            dve.wait_ge(root_out, 2)
            dve.reciprocal(rms[:, :], rms[:, :]).then_inc(rms_ready, 1)
            dve.wait_ge(rms_ready, 1)
            for h in range(GH):
                o = proj[:, GV + VH * h:GV + VH * (h + 1), :].rearrange("p a l -> p (a l)")
                for t in range(TT):
                    dve.tensor_scalar(o[:, t * DV:(t + 1) * DV], o[:, t * DV:(t + 1) * DV],
                                      rms[:, TT * h + t:TT * h + t + 1], None, ALU.mult).then_inc(on_d, 1)
            dve.wait_ge(silu_ready, 1)

            def gated(k):
                dve.wait_ge(mix_t, k + 1)
                if k >= 2:
                    dve.wait_ge(mixl_ready, k - 1)
                dve.scalar_tensor_tensor(out=mtmp[k % 2][:, :], in0=bank[4 + k % 4][:, 0:SEQ],
                                         scalar=ggain[:, k % VH:k % VH + 1], in1=proj[:, GR + k, META:L],
                                         op0=ALU.mult, op1=ALU.mult).then_inc(mix_f, 1)

            gated(0)
            for k in range(KD):
                if k + 1 < GH * VH:
                    gated(k + 1)
                dve.wait_ge(mixh_ready, k + 1)
                if k < GH * VH:
                    dve.wait_ge(mix_f, k + 1)
                    dve.tensor_tensor(mixl[:, k, :], mtmp[k % 2][:, :], mixh[:, k, :].bitcast(F32),
                                      ALU.subtract).then_inc(mixl_ready, 1)
                else:
                    dve.scalar_tensor_tensor(out=mixl[:, k, :], in0=bank[4 + k % 4][:, 0:SEQ], scalar=fgain[:, 0:1],
                                             in1=mixh[:, k, :].bitcast(F32), op0=ALU.mult,
                                             op1=ALU.subtract).then_inc(mixl_ready, 1)
                if k in EARLY_UNITS:
                    lo_unit(dve, EARLY_UNITS[k])

            def residual(n):
                dve.wait_ge(halves_used, halves(U_OUT + (D // 512) * (n + 1)))
                dve.wait_ge(x_again, 16)
                for t in range(TT):
                    r = resid[:, t, 512 * n:512 * (n + 1)]
                    ins = dve.tensor_tensor(r, bank[2 * (n % 2) + t][:, :], r, ALU.add)
                    if t < TT - 1:
                        ins.then_inc(dve_step, 1)
                        steps[0] += 1
                ins.then_inc(resid_ready, 1)

            for c in range(U_OUT + 4, U_EXP):
                lo_unit(dve, c)
                if (c - U_OUT) % 4 == 1 and c - U_OUT > 4:
                    residual((c - U_OUT) // 4 - 1)
            residual(D // 512 - 1)

            dve.wait_ge(quarters_sq, D // 512)
            own(dve.tensor_reduce(stat[:, 0:TT], sq2[:, :, :], AX, ALU.add))
            mean_eps(stat2[:, 0:TT], stat[:, 0:TT], D)
            dve.wait_ge(root_out, 3)
            own(dve.reciprocal(stat2[:, 0:TT], stat[:, 0:TT]))
            dve.wait_ge(routers_in, 16 * (G + 5))

            def normed(n):
                s = slice(512 * n, 512 * (n + 1))
                for t in range(TT):
                    dve.scalar_tensor_tensor(out=u2[:, t, s], in0=resid[:, t, s], scalar=stat2[:, t:t + 1],
                                             in1=g2b[:, s], op0=ALU.mult, op1=ALU.mult).then_inc(u2_ready, 1)

            def normed_lo(n):
                s = slice(512 * n, 512 * (n + 1))
                dve.wait_ge(u2h_ready, TT * (n + 1))
                dve.wait_ge(u2_ready, TT * (n + 1))
                for t in range(TT):
                    dve.tensor_tensor(u2l[:, t, s], u2[:, t, s], u2h[:, t, s].bitcast(F32),
                                      ALU.subtract).then_inc(u2l_ready, 1)

            dve.wait_ge(masks_ready, 7)
            for first in (0, 2 * SLOTS):
                own(dve.tensor_scalar(pick[:, :, first:first + SLOTS], count[:, None, 0:SLOTS].broadcast_to([P, TT, SLOTS]),
                                      0.0, None, ALU.mult))

            lo_unit(dve, U_EXP)

            dve.wait_ge(logits, 1)
            dve.wait_ge(masks_ready, 15)
            lg = rt["lg"]
            for t in range(TT):
                own(dve.scalar_tensor_tensor(out=lg[:, t, :], in0=bank[6 + t][:, 0:G + E], scalar=stat2[:, t:t + 1],
                                             in1=br[:, :], op0=ALU.mult, op1=ALU.add))
            own(dve.tensor_copy(rt["gp"][:, :, 0:G], lg[:, :, 0:G]))
            for t in range(TT):
                own(dve.max(rt["gm"][:, t, :], rt["gp"][:, t, :]))
                own(dve.max_index(gix[:, t, :], rt["gm"][:, t, :], rt["gp"][:, t, :]))
            dve.tensor_scalar(esum[:, 0:TT], rt["gm"][:, :, 0], -1.0, None, ALU.mult).then_inc(route_d, 1)
            own(dve.tensor_copy(rt["gi"][:, :, :], gix[:, :, :]))
            own(dve.tensor_tensor(rt["oh"][:, :, :], count[:, None, 0:G].broadcast_to([P, TT, G]),
                                  rt["gi"][:, :, 0:1].broadcast_to([P, TT, G]), ALU.is_equal))
            own(dve.tensor_tensor(rt["t32"][:, :, :].rearrange("p t (g e) -> p t g e", g=G),
                                  lg[:, :, G:].rearrange("p t (g e) -> p t g e", g=G),
                                  rt["oh"][:, :, :, None].broadcast_to([P, TT, G, E8]), ALU.mult))
            own(dve.tensor_reduce(rt["sel8"][:, :, :], rt["t32"][:, :, :].rearrange("p t (g e) -> p t e g", g=G),
                                  AX, ALU.add))
            own(dve.tensor_reduce(esum[:, 8:10], rt["sel8"][:, :, :], AX, ALU.max))
            dve.tensor_scalar(esum[:, 4:6], esum[:, 8:10], -1.0, None, ALU.mult).then_inc(route_d, 1)
            normed(0)
            dve.wait_ge(route_a, 2)
            own(dve.reciprocal(esum[:, 10:12], esum[:, 2:4]))
            own(dve.reciprocal(esum[:, 12:14], esum[:, 6:8]))
            own(dve.tensor_tensor(rt["pe"][:, :, :], rt["pe"][:, :, :],
                                  esum[:, 12:14][:, :, None].broadcast_to([P, TT, 8]), ALU.mult))
            for t in range(TT):
                own(dve.max(rt["top"][:, t, :], rt["pe"][:, t, :]))
                own(dve.max_index(tix[:, t, :], rt["top"][:, t, :], rt["pe"][:, t, :]))
            own(dve.tensor_copy(rt["ti"][:, :, :], tix[:, :, :]))
            own(dve.scalar_tensor_tensor(out=rt["eid"][:, :, :], in0=rt["gi"][:, :, 0:1].broadcast_to([P, TT, 2]),
                                         scalar=float(E8), in1=rt["ti"][:, :, 0:2], op0=ALU.mult, op1=ALU.add))
            for k in range(2):
                ins = dve.tensor_tensor(rt[f"m{k}"][:, :, :], count[:, None, 0:E].broadcast_to([P, TT, E]),
                                        rt["eid"][:, :, k:k + 1].broadcast_to([P, TT, E]), ALU.is_equal)
                if k == 0:
                    ins.then_inc(dve_step, 1)
                    steps[0] += 1
            own(ins)
            dve.tensor_tensor(rt["mm"][:, :, :], rt["m0"][:, :, :], rt["m1"][:, :, :], ALU.add).then_inc(route_d, 1)
            for n in range(1, D // 512):
                normed(n)
            dve.wait_ge(ranks, 1)
            dve.wait_ge(route_d, 3)
            for t in range(TT):
                own(dve.scalar_tensor_tensor(out=key[:, t, 0:E], in0=bank[6][:, 64 * t:64 * t + E], scalar=1.0,
                                             in1=rt["mm"][:, t, :], op0=ALU.add, op1=ALU.mult))
            own(dve.tensor_reduce(esum[:, 18:19], bank[6][:, 2 * 64:2 * 64 + E], AX, ALU.max))
            own(dve.tensor_scalar(rounds[:, :], limit[:, :], esum[:, 18:19], None, ALU.is_lt))
            own(dve.tensor_reduce(esum[:, 19:20], rounds[:, :], AX, ALU.add))
            dve.tensor_copy(nrounds[:, :], esum[:, 19:20]).then_inc(routed, 1)
            dve.wait_ge(routed, 1)

            def picked(e):
                for t in range(TT):
                    ins = dve.tensor_scalar(pick[:, t, SLOTS:2 * SLOTS], count[:, 1:SLOTS + 1],
                                            key[:, t, bass.ds(e, 1)], None, ALU.is_equal)
                    if t == TT - 1:
                        ins.then_inc(pick_ready, 1)

            def results(n, quarters):
                for q in quarters:
                    dve.wait_ge(ylo_ready, 4 * n + q + 1)
                    s = slice(512 * q, 512 * (q + 1))
                    dve.tensor_tensor(yrow[:, s], bank[2 + q][0:SLOTS, :], ylo[:, s], ALU.add).then_inc(y_ready, 1)

            def gate_sum(n):
                dve.wait_ge(glo_ready, n + 1)
                dve.tensor_tensor(gsum[:, :], bank[0][0:SLOTS, :], glo[:, :], ALU.add).then_inc(gsum_ready, 1)

            def hidden(n):
                dve.wait_ge(ulo_ready, n + 1)
                dve.tensor_tensor(usum[:, :], bank[1][0:SLOTS, :], ulo[:, :], ALU.add).then_inc(usum_ready, 1)
                dve.wait_ge(silu_e, n + 1)
                dve.wait_ge(usum_ready, n + 1)
                dve.tensor_tensor(gsum[:, :], glo[:, :], usum[:, :], ALU.mult).then_inc(h_ready, 1)

            def hidden_lo(n):
                dve.wait_ge(hsh_ready, n + 1)
                dve.tensor_tensor(hs[:, :, SLOTS:2 * SLOTS], bank[1][:, 0:FE // P * SLOTS]
                                  .rearrange("p (k s) -> p k s", s=SLOTS),
                                  hs[:, :, 0:SLOTS].bitcast(F32), ALU.subtract).then_inc(hsl_ready, 1)

            def slots_rows(n):
                dve.wait_ge(idn_mm, n + 1)
                dve.tensor_tensor(idn[:, :], bank[7][0:SLOTS, 0:1], empty[0:SLOTS, :], ALU.add).then_inc(idn_ready, 1)

            n_rounds = dve.value_load(nrounds[0:1, 0:1], min_val=1, max_val=SEQ // SLOTS)
            picked(0)
            for n in range(D // 512):
                normed_lo(n)
            lo_unit(dve, U_EXP + 1)
            for t in range(TT):
                for k in range(2):
                    own(dve.tensor_scalar(esum[:, 20 + 2 * t + k:21 + 2 * t + k], rowno[:, :],
                                          float(k * SEQ + t * P) - BIG, None, ALU.add))
                own(dve.tensor_scalar(rt["t32"][:, t, :], rt["m1"][:, t, :], esum[:, 21 + 2 * t:22 + 2 * t], None, ALU.mult))
                own(dve.scalar_tensor_tensor(out=rowid[:, t, 0:E], in0=rt["m0"][:, t, :],
                                             scalar=esum[:, 20 + 2 * t:21 + 2 * t], in1=rt["t32"][:, t, :],
                                             op0=ALU.mult, op1=ALU.add))
            dve.memset(empty[:, :], BIG).then_inc(rows_ready, 1)
            dve.wait_ge(rows_ready, 1)
            with dve.Fori(0, n_rounds) as r:
                m = 2 * E * r
                with dve.If(r > 0):
                    lo_unit(dve, U_EXP, m)
                    lo_unit(dve, U_EXP + 1, m)
                for j in range(2, 8):
                    lo_unit(dve, U_EXP + j, m)
                    if j == 4:
                        slots_rows(E * r)
                        picked(1)
                    if j == 5:
                        gate_sum(E * r)
                with dve.Fori(1, E) as e:
                    n = E * r + e
                    for j in range(PER):
                        lo_unit(dve, U_STEP + j, 2 * n - 2)
                        if j == 1:
                            hidden(n - 1)
                        if j == 3:
                            hidden_lo(n - 1)
                        if j == 5:
                            gate_sum(n)
                            dve.wait_ge(idx_ready, n)
                            slots_rows(n)
                            picked(e + 1)
                        if j == 9:
                            dve.wait_ge(idx_ready, n)
                            results(n - 1, (0, 1))
                        if j == 10:
                            results(n - 1, (2, 3))
                for j in range(4):
                    lo_unit(dve, U_STEP + j, 2 * E * r + 2 * E - 2)
                    if j == 1:
                        hidden(E * r + E - 1)
                        hidden_lo(E * r + E - 1)
                dve.wait_ge(idx_ready, E * r + E)
                results(E * r + E - 1, range(4))
                dve.wait_ge(xg_mm, 4 * (E + 1) * r + 4 * (E + 1))
                dve.wait_ge(pick_ready, (E + 1) * r + E + 1)
                dve.tensor_scalar(key[:, :, :], key[:, :, :], -float(SLOTS), None, ALU.add).then_inc(key_moved, 1)
                dve.wait_ge(key_moved, r + 1)
                picked(0)

            dve.wait_ge(routers_in, 16 * (G + 6))
            own(dve.tensor_tensor(esum[:, 14:16], rt["top"][:, :, 0], rt["top"][:, :, 1], ALU.add))
            own(dve.reciprocal(esum[:, 16:18], esum[:, 14:16]))
            own(dve.tensor_tensor(cw[:, :, :], rt["top"][:, :, 0:2],
                                  esum[:, 16:18][:, :, None].broadcast_to([P, TT, 2]), ALU.mult))
            own(dve.tensor_tensor(cw[:, :, :], cw[:, :, :],
                                  esum[:, 10:12][:, :, None].broadcast_to([P, TT, 2]), ALU.mult))
            for t in range(TT):
                for s in range(2):
                    dve.wait_ge(yk_in[2 * t + s], 16 * 2)
                    cols = slice(s * D // 2, (s + 1) * D // 2)
                    own(dve.scalar_tensor_tensor(out=resid[:, t, cols], in0=yk[:, t, 0, cols], scalar=cw[:, t, 0:1],
                                                 in1=resid[:, t, cols], op0=ALU.mult, op1=ALU.add))
                    dve.scalar_tensor_tensor(out=resid[:, t, cols], in0=yk[:, t, 1, cols], scalar=cw[:, t, 1:2],
                                             in1=resid[:, t, cols], op0=ALU.mult, op1=ALU.add).then_inc(summed, 1)
            for t in range(TT):
                dve.wait_ge(sums_ready, 1 + 2 * (t + 1))
                own(dve.tensor_tensor(stat2[:, 6 + t:7 + t], sq2[:, t, 0:1], sq2[:, t, 1:2], ALU.add))
                mean_eps(stat2[:, t:t + 1], stat2[:, 6 + t:7 + t], D)
                dve.wait_ge(root_out, 4 + t)
                own(dve.reciprocal(stat2[:, 4 + t:5 + t], stat[:, 2 + t:3 + t]))
                for s in range(2):
                    cols = slice(s * D // 2, (s + 1) * D // 2)
                    dve.scalar_tensor_tensor(out=u2[:, t, cols], in0=resid[:, t, cols], scalar=stat2[:, 4 + t:5 + t],
                                             in1=gfb[:, cols], op0=ALU.mult, op1=ALU.mult).then_inc(out_ready, 1)

        @block.tensor
        def _(pe):
            pe.wait_ge(masks_ready, 7)
            pe.wait_ge(x_in, 48)
            for k in range(KD):
                if k >= 4:
                    pe.wait_ge(ul_ready, k - 3)
                o = bank[k % 4]
                pe.transpose(o[:, 0:META], mn[:, k::KD], ident[0:META, 0:META])
                for t in range(TT):
                    ins = pe.transpose(o[:, META + t * P:META + (t + 1) * P], resid[:, t, k::KD], ident[:, :])
                ins.then_inc(xt_ready, 1)

            def block_unit(c, m=0, out=None):
                a = start_of(c) if isinstance(m, int) and c else 0
                out = out[:, a:]
                for s in range(2):
                    pe.wait_ge(lo_ready, halves(c, m) + s + 1)
                    h, l = hi[(2 * c + s) % SPLIT], lo[(2 * c + s) % SPLIT]
                    for kk in range(KD // 2):
                        k = KD // 2 * s + kk
                        pe.matmul(out, part(h, kk, P), uh[:, k, a:L], start=(k == 0), stop=False)
                        pe.matmul(out, part(h, kk, P), ul[:, k, a:L], start=False, stop=False)
                        ins = pe.matmul(out, part(l, kk, P), uh[:, k, a:L], start=False, stop=(k == KD - 1))
                    ins.then_inc(halves_used, 1)

            pe.wait_ge(ul_ready, KD)
            block_unit(0, out=bank[7][:, 0:L])
            for c in range(U_IN, STRAIGHT):
                if c >= 5:
                    pe.wait_ge(proj_out, c - U_IN - 1)
                block_unit(c, out=bank_of(c)[:, 0:L])
                if c == 2:
                    pe.wait_ge(diag_ready, TT + 1)
                    pe.matmul(bank[6][:, 0:META], ones[0:META, :], diag[0:META, TT, 0:META], start=True, stop=True)
                    for t in range(TT):
                        ins = pe.matmul(bank[6][:, META + t * P:META + (t + 1) * P], ones[:, :], diag[:, t, :],
                                        start=True, stop=True)
                    ins.then_inc(rstd_mm, 1)
            with pe.Fori(0, LOOPS) as i:
                for j in range(RAW):
                    c = STRAIGHT + j
                    pe.wait_ge(proj_out, nth(c - U_IN - 1, i))
                    block_unit(c, i, out=bank[c % 2][:, 0:L])

            def tokens(t):
                return slice(META + t * P, META + (t + 1) * P)

            def gla_first(h):
                pe.wait_ge(gla_ops, 1)
                pe.wait_ge(cq_ready, 1)
                if h:
                    pe.wait_ge(a_ready, h)
                    pe.wait_ge(k_ready, h)
                    pe.wait_ge(v_ready, h)
                    pe.wait_ge(st_ready, h)
                for t in range(TT):
                    pe.matmul(bank[2][:, t * P:(t + 1) * P], proj[:, GK + h, tokens(t)],
                              proj[:, GQ + h, tokens(t)], start=True, stop=True)
                pe.transpose(bank[4][0:META, 0:P], gt[1][:, h, 0:META], ident[:, :])
                for t in range(TT):
                    pe.transpose(bank[4][:, (t + 1) * P:(t + 2) * P], gt[1][:, h, tokens(t)], ident[:, :])
                for i in range(VH):
                    v = GV + VH * h + i
                    pe.transpose(bank[3][0:META, i * P:(i + 1) * P], proj[:, v, 0:META], ident[:, :])
                    pe.transpose(bank[3][:, DV + i * P:DV + (i + 1) * P], proj[:, v, tokens(0)], ident[:, :])
                    ins = pe.transpose(bank[5][:, i * P:(i + 1) * P], proj[:, v, tokens(1)], ident[:, :])
                ins.then_inc(kv_t, 1)

            def gla_update(h):
                pe.wait_ge(k_ready, h + 1)
                pe.wait_ge(v_ready, h + 1)
                pe.wait_ge(a_ready, h + 1)
                if h:
                    pe.wait_ge(st_ready, h)
                for n in range(NCH):
                    rows = slice(0, META) if n == 0 else slice((n - 1) % 2 * CHUNK, ((n - 1) % 2 + 1) * CHUNK)
                    tile = 0 if n == 0 else 1 + (n - 1) // 2
                    ins = pe.matmul(upd[n], kln[rows, tile, :],
                                    vn[rows, tile, :], start=True, stop=True)
                ins.then_inc(upd_g, 1)

            def gla_output(h):
                pe.wait_ge(a_ready, h + 1)
                pe.wait_ge(st_ready, h + 1)
                if h:
                    pe.wait_ge(o_gout, h)
                for t in range(TT):
                    o = bank[6][:, t * DV:(t + 1) * DV]
                    pe.matmul(o, a2[h % 2][:, t, :], vn[:, 1 + t, :], start=True, stop=False, skip_group_check=True)
                    for i in range(2):
                        n = 2 * t + i
                        cols = slice(META + n * CHUNK, META + (n + 1) * CHUNK)
                        ins = pe.matmul(o[i * CHUNK:(i + 1) * CHUNK, :], gt[3][:, h, cols], st[:, n, :],
                                        start=False, stop=(i == 1), skip_group_check=True)
                ins.then_inc(o_g, 1)

            def gates():
                pe.wait_ge(params_in, 16 * 5)
                pe.wait_ge(z_ready, 1)
                for h in range(GH):
                    ins = pe.matmul(bank[2 + h][:, 0:L], wgate2[:, h * P:(h + 1) * P], zt[:, :], start=True, stop=True)
                ins.then_inc(gates_mm, 1)

            def fox_gates_t():
                pe.wait_ge(fgate_d, 2)
                for t in range(TT):
                    ins = pe.transpose(bank[6][:, t * FH:(t + 1) * FH], ct[:, 2, META + t * P:META + (t + 1) * P],
                                       ident[0:FH, 0:FH])
                ins.then_inc(fgate_t, 1)

            gate_steps = {1: gates, 3: fox_gates_t}

            for i in range(NB - GLA_BLOCKS):
                c = FOX0 + i
                pe.wait_ge(proj_out, c - U_IN - 1)
                block_unit(c, out=bank[c % 2][:, 0:L])
                if i in gate_steps:
                    gate_steps[i]()
                if (h := head_at(i, 2)) is not None:
                    gla_update(h)
                if (h := head_at(i, 4)) is not None:
                    gla_output(h)
                if (h := head_at(i, 0)) is not None:
                    gla_first(h)

            def fox_scores(h):
                if h >= 2:
                    pe.wait_ge(p_ready, h - 1)
                elif h == 0:
                    pe.wait_ge(proj_out, NB)
                    pe.wait_ge(heads_consts, 2)
                for t in range(TT):
                    w = META + (t + 1) * P
                    pe.matmul(scores(h, t, slice(0, w)), proj[:, FQ + h, tokens(t)], proj[:, FK + h, 0:w],
                              start=True, stop=False)
                    ins = pe.matmul(scores(h, t, slice(0, w)), sel[:, h, :], ct[:, 3, 0:w], start=False, stop=True)
                ins.then_inc(scores_f, 1)
                if h:
                    pe.wait_ge(vf_ready, h)
                pe.transpose(bank[6][0:META, 0:HD], proj[:, FV + h, 0:META], ident[:, :])
                for t in range(TT):
                    ins = pe.transpose(bank[6][:, (t + 1) * HD:(t + 2) * HD], proj[:, FV + h, tokens(t)], ident[:, :])
                ins.then_inc(vf_t, 1)

            def fox_transpose(h):
                pe.wait_ge(p_ready, h + 1)
                if h:
                    pe.wait_ge(pt_a, h)
                    pe.wait_ge(pt_d, h)
                for t in range(TT):
                    pe.transpose(bank[5][0:META, t * P:(t + 1) * P], pr[:, t, 0:META], ident[:, :])
                pe.transpose(bank[4][:, 0:P], pr[:, 0, tokens(0)], ident[:, :])
                pe.transpose(bank[4][:, P:2 * P], pr[:, 1, tokens(0)], ident[:, :])
                pe.transpose(bank[4][:, 2 * P:3 * P], pr[:, 1, tokens(1)], ident[:, :]).then_inc(p_t, 1)

            def fox_values(h):
                pe.wait_ge(pt_a, h + 1)
                pe.wait_ge(pt_d, h + 1)
                pe.wait_ge(vf_ready, h + 1)
                if h:
                    pe.wait_ge(o_fout, h)
                v = vf[h % 2]
                for t in range(TT):
                    o = bank[7][:, t * HD:(t + 1) * HD]
                    pe.matmul(o, ptm[:, t, :], v[0:META, 0, :], start=True, stop=False)
                    for i in range(t + 1):
                        ins = pe.matmul(o, pt[:, t + i, :], v[:, 1 + i, :], start=False, stop=(i == t))
                ins.then_inc(o_f, 1)

            for s in range(FH + 2):
                if s < FH:
                    if s == 0:
                        pe.wait_ge(st_ready, GH)
                        pe.wait_ge(o_gout, GH)
                        pe.wait_ge(v_ready, GH)
                    fox_scores(s)
                if 1 <= s <= FH:
                    fox_transpose(s - 1)
                if s >= 2:
                    fox_values(s - 2)

            def resid_blocks(n):
                pe.wait_ge(resid_ready, n + 1)
                for i in (2 * n, 2 * n + 1):
                    if i >= 2:
                        pe.wait_ge(u2t_a, i - 1)
                    for j in range(2):
                        for t in range(TT):
                            k = 2 * i + j
                            ins = pe.transpose(bank[4 + i % 2][:, j * SEQ + t * P:j * SEQ + (t + 1) * P],
                                               resid[:, t, k * P:(k + 1) * P], ident[:, :])
                    ins.then_inc(u2_t, 1)

            def some_logits(n):
                pe.wait_ge(wr_ready, 1)
                pe.wait_ge(u2t_a, 2 * n + 2)
                for k in range(4 * n, 4 * n + 4):
                    for t in range(TT):
                        ins = pe.matmul(bank[6 + t][:, 0:G + E], u2t[:, k, t * P:(t + 1) * P], wr[:, k, :],
                                        start=(k == 0), stop=(k == KD - 1))
                return ins

            def output_step(n, k):
                g = 2 * (U_OUT + n * (D // 512) + k // 4) + k % 4 // 2
                h, l = hi[g % SPLIT], lo[g % SPLIT]
                pe.wait_ge(lo_ready, g + 1)
                pe.wait_ge(mixl_ready, k + 1)
                for t in range(TT):
                    o = bank[2 * (n % 2) + t][:, :]
                    cols = slice(t * P, (t + 1) * P)
                    pe.matmul(o, mixh[:, k, cols], part(h, k % 2, 512), start=(k == 0), stop=False)
                    pe.matmul(o, mixl[:, k, cols], part(h, k % 2, 512), start=False, stop=False)
                    ins = pe.matmul(o, mixh[:, k, cols], part(l, k % 2, 512), start=False, stop=(k == KD - 1))
                if k % 2 == 1:
                    ins.then_inc(halves_used, 1)

            for k in range(KD):
                if k >= 4:
                    pe.wait_ge(mixl_ready, k - 3)
                if k < GH * VH:
                    h, i = k // VH, k % VH
                    o = proj[:, GV + VH * h:GV + VH * (h + 1), :].rearrange("p a l -> p (a l)")
                    src = [o[:, t * DV + i * P:t * DV + (i + 1) * P] for t in range(TT)]
                    pe.wait_ge(on_d, TT * (h + 1))
                else:
                    src = [proj[:, FQ + k - GH * VH, t * P:(t + 1) * P] for t in range(TT)]
                    pe.wait_ge(on_p, TT * (k - GH * VH + 1))
                for t in range(TT):
                    ins = pe.transpose(bank[4 + k % 4][:, t * P:(t + 1) * P], src[t], ident[:, :])
                ins.then_inc(mix_t, 1)
                if k >= EARLY_OUT:
                    output_step(0, k - EARLY_OUT)

            for n in range(D // 512):
                if n >= 2:
                    pe.wait_ge(resid_ready, n - 1)
                for k in range(KD - EARLY_OUT if n == 0 else 0, KD):
                    output_step(n, k)
                    if n and k == 11:
                        resid_blocks(n - 1)
                    if n >= 2 and k == 7:
                        some_logits(n - 2)
            some_logits(D // 512 - 2)
            resid_blocks(D // 512 - 1)
            some_logits(D // 512 - 1).then_inc(logits, 1)

            pe.wait_ge(route_d, 3)
            mm = rt["mm"]
            pe.matmul(bank[6][:, 0:E], above[:, :], mm[:, 0, :], start=True, stop=True)
            pe.matmul(bank[6][:, 64:64 + E], above[:, :], mm[:, 1, :], start=True, stop=False)
            pe.matmul(bank[6][:, 64:64 + E], ones[:, 0:P], mm[:, 0, :], start=False, stop=True)
            for t in range(TT):
                ins = pe.matmul(bank[6][:, 128:128 + E], ones[:, 0:P], mm[:, t, :], start=(t == 0), stop=(t == TT - 1))
            ins.then_inc(ranks, 1)

            def pick_rows(q, before, b=6):
                if q and b == 6:
                    pe.wait_ge(xg_ready, before + q)
                for first, u in ((SLOTS, u2h), (0, u2l)):
                    for t in range(TT):
                        ins = pe.matmul(bank[b][:, :], pick[:, t, first:first + 2 * SLOTS],
                                        u[:, t, 512 * q:512 * (q + 1)], start=(first > 0 and t == 0),
                                        stop=(first == 0 and t == TT - 1))
                ins.then_inc(xg_mm, 1)

            def gather(q, before):
                pe.wait_ge(xg_ready, before + q + 1)
                if q:
                    pe.wait_ge(xs_ready, before + q)
                for kk in range(4):
                    ins = pe.transpose(bank[7][:, kk * 2 * SLOTS:(kk + 1) * 2 * SLOTS], xg[:, kk * P:(kk + 1) * P],
                                       ident[:, :])
                ins.then_inc(xs_t, 1)

            def expert_unit(c, m, outs, lhs, first, last):
                for i, (o, k) in enumerate(zip(outs, lhs)):
                    g = 2 * c + i // 2
                    if i % 2 == 0:
                        pe.wait_ge(lo_ready, halves(c, m) + i // 2 + 1)
                    pe.matmul(o[:, :], k, part(hi[g % SPLIT], i % 2, 512), start=first(i), stop=False)
                    ins = pe.matmul(o[:, :], k, part(lo[g % SPLIT], i % 2, 512), start=False, stop=last(i))
                    if i % 2 == 1:
                        ins.then_inc(halves_used, 1)

            pe.wait_ge(routed, 1)
            n_rounds = pe.value_load(nrounds[0:1, 0:1], min_val=1, max_val=SEQ // SLOTS)
            def gate_or_up(w, q, c, m):
                expert_unit(c + q, m, [bank[w]] * 4, [xs[:, 4 * q + i, :] for i in range(4)],
                            lambda i: q == 0 and i == 0, lambda i: q == 3 and i == 3)

            def down(c, m):
                for q in range(4):
                    expert_unit(c + q, m, bank[2:6], [hs[:, q, :]] * 4, lambda i: q == 0, lambda i: q == 3)

            def slots_rows(e):
                for t in range(TT):
                    ins = pe.matmul(bank[7][0:SLOTS, 0:1], pick[:, t, SLOTS:2 * SLOTS].bitcast(F32),
                                    rowid[:, t, bass.ds(e, 1)], start=(t == 0), stop=(t == TT - 1))
                ins.then_inc(idn_mm, 1)

            def up_and_gather(n, before, c, m):
                pe.wait_ge(idn_ready, n + 1)
                pe.wait_ge(pick_ready, n + r + 2)
                for q in range(4):
                    pick_rows(q, before)
                    gate_or_up(1, q, c, m)
                    gather(q, before)

            def hidden_t(n):
                pe.wait_ge(h_ready, n + 1)
                for k in range(FE // P):
                    ins = pe.matmul(bank[1][:, k * SLOTS:(k + 1) * SLOTS], gsum[:, k * P:(k + 1) * P],
                                    ident[0:SLOTS, 0:SLOTS], start=True, stop=True)
                ins.then_inc(h_t, 1)

            def hidden_split(n):
                pe.wait_ge(hsh_ready, n + 1)
                pe.wait_ge(hsl_ready, n + 1)

            with pe.Fori(0, n_rounds) as r:
                pe.wait_ge(pick_ready, (E + 1) * r + 1)
                m = 2 * E * r
                for q in range(4):
                    pe.wait_ge(u2l_ready, TT * (q + 1))
                    pick_rows(q, 4 * (E + 1) * r, 2 + q)
                gather(0, 4 * (E + 1) * r)
                for q in range(4):
                    if q + 1 < 4:
                        gather(q + 1, 4 * (E + 1) * r)
                    pe.wait_ge(xs_ready, 4 * (E + 1) * r + q + 1)
                    gate_or_up(0, q, U_EXP, m)
                pe.wait_ge(rows_ready, 1)
                slots_rows(0)
                up_and_gather(E * r, 4 * (E + 1) * r + 4, U_EXP + 4, m)
                with pe.Fori(1, E) as e:
                    n = E * r + e
                    m = 2 * n - 2
                    before = 4 * (n + r)
                    for q in range(4):
                        pe.wait_ge(xs_ready, before + q + 1)
                        gate_or_up(0, q, U_STEP, m)
                        if q == 2:
                            hidden_t(n - 1)
                    slots_rows(e)
                    hidden_split(n - 1)
                    down(U_STEP + 4, m)
                    up_and_gather(n, before + 4, U_STEP + 8, m)
                    pe.wait_ge(y_ready, 4 * n)
                hidden_t(E * r + E - 1)
                hidden_split(E * r + E - 1)
                down(U_STEP, 2 * E * r + 2 * E - 2)
                pe.wait_ge(xs_ready, 4 * (E + 1) * r + 4 * (E + 1))
                pe.wait_ge(y_ready, 4 * E * r + 4 * E)


_INS = ['x', 'meta_tokens', 'norm1_g', 'w_in', 'b_fox_f', 'gla_w_gate2', 'gla_b_gate', 'gla_norm_g',
        'fox_norm_g', 'w_out', 'norm2_g', 'w_router_group', 'b_router_group', 'w_router_expert',
        'b_router_expert', 'w_exp_gate', 'w_exp_up', 'w_exp_down', 'norm_f_g']


def kernel(**inputs):
    import numpy as _np
    import concourse.bacc as _bacc
    from concourse import mybir as _mybir
    from concourse.bass_utils import run_bass_kernel_spmd as _run

    nc = _bacc.Bacc("TRN2", target_bir_lowering=False, num_devices=1)
    arrays, args = {}, []
    for name in _INS:
        a = _np.ascontiguousarray(inputs[name])
        arrays[f"in_{name}_dram"] = a
        args.append(nc.dram_tensor(f"in_{name}_dram", a.shape, _mybir.dt.from_np(a.dtype), kind="ExternalInput").ap())
    shape = inputs["x"].shape
    args.append(nc.dram_tensor("out_dram", shape, _mybir.dt.float32, kind="ExternalOutput").ap())
    hybrid_layer(nc, *args)
    r = _run(nc, [arrays], core_ids=[0])
    return r.results[0]["out_dram"]
```
